# Optimizing a Trainium2 kernel written in Bass

```python
import math
import jax, jax.numpy as jnp
from jax import lax
import numpy as np

D_MODEL = 1024
BATCH = 1
SEQ = 512
DEPTH = 2
DEC_BATCH = 8
DEC_SEQ = 8
PAST_LEN = 256
PAGE_SIZE = 128

HEAD_DIM = 64
N_MOBA_HEADS = 4
N_SWA_HEADS = 4
SWA_GROUPS = ((128, 1), (512, 4), (2048, 16))
N_SWA_GROUPS = len(SWA_GROUPS)
N_ATTN_HEADS = N_MOBA_HEADS + N_SWA_GROUPS * N_SWA_HEADS
ATTN_IN = 3 * N_ATTN_HEADS * HEAD_DIM
ATTN_OUT = (N_MOBA_HEADS + N_SWA_HEADS) * HEAD_DIM
MOBA_BLOCK = 256
MOBA_TOPK = 3
Q_BLOCK = 128
ROPE_THETA = 10000.0
GLA_HEADS = 4
GLA_DK = D_MODEL // 2 // GLA_HEADS
GLA_DV = D_MODEL // GLA_HEADS
GLA_RANK = 16
GLA_TAU = 16.0
GLA_CHUNK = 64
GLA_IN = 2 * GLA_HEADS * GLA_DK + 2 * GLA_HEADS * GLA_DV
D_FF = 2816
CONV_W = 3
N_EVEN = (DEPTH + 1) // 2
N_ODD = DEPTH // 2
DN_ALPHA = (2.0 * DEPTH) ** 0.25
DN_BETA = (8.0 * DEPTH) ** -0.25
LN_EPS = 1e-5
RMS_EPS = 1e-6

kernel_name = "moba_dilated_gla_convffn_deepnorm_step"

def layer_norm(x, g, b):
    xf = x.astype(jnp.float32)
    mu = xf.mean(-1, keepdims=True)
    var = jnp.mean(jnp.square(xf - mu), -1, keepdims=True)
    return ((xf - mu) * lax.rsqrt(var + LN_EPS) * g + b).astype(x.dtype)

def rope(x, pos):
    half = HEAD_DIM // 2
    inv = ROPE_THETA ** (-jnp.arange(half, dtype=jnp.float32) / half)
    ang = pos.astype(jnp.float32)[:, None] * inv[None, :]
    cos, sin = jnp.cos(ang)[:, None, :], jnp.sin(ang)[:, None, :]
    xf = x.astype(jnp.float32)
    x1, x2 = xf[..., :half], xf[..., half:]
    return jnp.concatenate([x1 * cos - x2 * sin, x2 * cos + x1 * sin], -1).astype(x.dtype)

def attn_qkv(x, w_in, pos):
    B, T, _ = x.shape
    h = (x @ w_in).reshape(B, T, 3, N_ATTN_HEADS, HEAD_DIM)
    return rope(h[:, :, 0], pos), rope(h[:, :, 1], pos), h[:, :, 2]

def moba_blocks(k_all, v_all):
    B, L = k_all.shape[:2]
    nb = -(-L // MOBA_BLOCK)
    pad = nb * MOBA_BLOCK - L

    def blk(a):
        a = jnp.pad(a, ((0, 0), (0, pad), (0, 0), (0, 0)))
        return a.reshape(B, nb, MOBA_BLOCK, N_MOBA_HEADS, HEAD_DIM).transpose(0, 3, 1, 2, 4)

    kb, vb = blk(k_all), blk(v_all)
    kmean = kb.astype(jnp.float32).mean(axis=3)
    return kb, vb, kmean

def moba_attend(q, q_pos, kb, vb, kmean):
    B, Tq = q.shape[:2]
    nb = kb.shape[2]
    topk = min(MOBA_TOPK, nb)
    scale = HEAD_DIM ** -0.5
    qblk = q_pos // MOBA_BLOCK
    gate = jnp.einsum('bqhd,bhnd->bqhn', q.astype(jnp.float32), kmean)
    is_past = jnp.arange(nb)[None, :] < qblk[:, None]
    gate = jnp.where(is_past[None, :, None, :], gate, -jnp.inf)
    _, sel = lax.top_k(gate, topk)
    sel_ok = sel < qblk[None, :, None, None]
    bi = jnp.arange(B)[:, None, None, None]
    hi = jnp.arange(N_MOBA_HEADS)[None, None, :, None]
    k_sel = kb[bi, hi, sel]
    v_sel = vb[bi, hi, sel]
    k_own = kb[:, :, qblk]
    v_own = vb[:, :, qblk]
    s_sel = jnp.einsum('bqhd,bqhnjd->bqhnj', q, k_sel).astype(jnp.float32) * scale
    s_sel = jnp.where(sel_ok[..., None], s_sel, -jnp.inf).reshape(B, Tq, N_MOBA_HEADS, topk * MOBA_BLOCK)
    own_pos = qblk[:, None] * MOBA_BLOCK + jnp.arange(MOBA_BLOCK)[None, :]
    s_own = jnp.einsum('bqhd,bhqjd->bqhj', q, k_own).astype(jnp.float32) * scale
    s_own = jnp.where((own_pos <= q_pos[:, None])[None, :, None, :], s_own, -jnp.inf)
    p = jax.nn.softmax(jnp.concatenate([s_sel, s_own], -1), axis=-1)
    p_sel = p[..., :topk * MOBA_BLOCK].reshape(B, Tq, N_MOBA_HEADS, topk, MOBA_BLOCK).astype(vb.dtype)
    p_own = p[..., topk * MOBA_BLOCK:].astype(vb.dtype)
    return (jnp.einsum('bqhnj,bqhnjd->bqhd', p_sel, v_sel)
            + jnp.einsum('bqhj,bhqjd->bqhd', p_own, v_own))

def dilated_attend(q, k_src, v_src, q_idx, dil, n_keys):
    idx = q_idx[:, None] - dil * jnp.arange(n_keys)[None, :]
    ok = idx >= 0
    idx = jnp.maximum(idx, 0)
    kg = k_src[:, idx]
    vg = v_src[:, idx]
    s = jnp.einsum('bqhd,bqnhd->bqhn', q, kg).astype(jnp.float32) * (HEAD_DIM ** -0.5)
    s = jnp.where(ok[None, :, None, :], s, -jnp.inf)
    m = s.max(-1, keepdims=True)
    p = jnp.exp(s - m)
    den = p.sum(-1, keepdims=True)
    o = jnp.einsum('bqhn,bqnhd->bqhd', (p / den).astype(v_src.dtype), vg)
    return o, (m + jnp.log(den))[..., 0]

def attention_mix(q, q_pos, k_moba, v_moba, swa_k, swa_v, swa_idx, q_block, w_out):
    B, Tq = q.shape[:2]
    nq = Tq // q_block
    kb, vb, kmean = moba_blocks(k_moba, v_moba)

    def blocks(a):
        return a.reshape((B, nq, q_block) + a.shape[2:]).swapaxes(0, 1)

    def one_block(inp):
        qb, pb, idxs = inp
        o_a = moba_attend(qb[:, :, :N_MOBA_HEADS], pb, kb, vb, kmean)
        outs, lses = [], []
        for g, (win, dil) in enumerate(SWA_GROUPS):
            h0 = N_MOBA_HEADS + g * N_SWA_HEADS
            o_g, l_g = dilated_attend(qb[:, :, h0:h0 + N_SWA_HEADS], swa_k[g], swa_v[g],
                                      idxs[g], dil, win // dil + 1)
            outs.append(o_g)
            lses.append(l_g)
        wgt = jax.nn.softmax(jnp.stack(lses), axis=0)
        o_b = jnp.einsum('gbqh,gbqhd->bqhd', wgt, jnp.stack(outs).astype(jnp.float32))
        return jnp.concatenate([o_a, o_b.astype(o_a.dtype)], axis=2)

    idx_blocks = tuple(i.reshape(nq, q_block) for i in swa_idx)
    o = lax.map(one_block, (blocks(q), q_pos.reshape(nq, q_block), idx_blocks))
    o = o.swapaxes(0, 1).reshape(B, Tq, ATTN_OUT)
    return o @ w_out

def attn_layer_prompt(x, w_in, w_out):
    B, S, _ = x.shape
    pos = jnp.arange(S, dtype=jnp.int32)
    q, k, v = attn_qkv(x, w_in, pos)
    ka, va = k[:, :, :N_MOBA_HEADS], v[:, :, :N_MOBA_HEADS]
    swa_k, swa_v, swa_idx, new_bufs = [], [], [], []
    for g, (win, _) in enumerate(SWA_GROUPS):
        h0 = N_MOBA_HEADS + g * N_SWA_HEADS
        kg, vg = k[:, :, h0:h0 + N_SWA_HEADS], v[:, :, h0:h0 + N_SWA_HEADS]
        swa_k.append(kg)
        swa_v.append(vg)
        swa_idx.append(pos)
        keep = min(win, S)
        new_bufs.append(jnp.stack([kg[:, S - keep:], vg[:, S - keep:]], axis=2))
    y = attention_mix(q, pos, ka, va, swa_k, swa_v, swa_idx, Q_BLOCK, w_out)
    return y, jnp.stack([ka, va], axis=2), new_bufs

def attn_layer_sample(x, w_in, w_out, moba_pool, page_table, swa_bufs):
    Bd, T, _ = x.shape
    pos = PAST_LEN + jnp.arange(T, dtype=jnp.int32)
    q, k, v = attn_qkv(x, w_in, pos)
    new_moba = jnp.stack([k[:, :, :N_MOBA_HEADS], v[:, :, :N_MOBA_HEADS]], axis=2)
    past = moba_pool[page_table].reshape((Bd, -1) + moba_pool.shape[2:])
    full = jnp.concatenate([past.astype(new_moba.dtype), new_moba], axis=1)
    swa_k, swa_v, swa_idx, new_bufs = [], [], [], []
    for g in range(N_SWA_GROUPS):
        h0 = N_MOBA_HEADS + g * N_SWA_HEADS
        new_g = jnp.stack([k[:, :, h0:h0 + N_SWA_HEADS], v[:, :, h0:h0 + N_SWA_HEADS]], axis=2)
        buf = swa_bufs[g]
        wb = buf.shape[1]
        ext = jnp.concatenate([buf.astype(new_g.dtype), new_g], axis=1)
        swa_k.append(ext[:, :, 0])
        swa_v.append(ext[:, :, 1])
        swa_idx.append(wb + jnp.arange(T, dtype=jnp.int32))
        new_bufs.append(ext[:, T:])
    y = attention_mix(q, pos, full[:, :, 0], full[:, :, 1], swa_k, swa_v, swa_idx, 1, w_out)
    return y, new_moba, new_bufs

def gla_scan(q, k, v, loga, s0):
    B, T, H, _ = q.shape
    c = math.gcd(T, GLA_CHUNK)
    n = T // c

    def chunks(a):
        return a.astype(jnp.float32).reshape(B, n, c, H, a.shape[-1]).transpose(1, 0, 3, 2, 4)

    tri = jnp.tril(jnp.ones((c, c), dtype=bool))

    def step(S, inp):
        qc, kc, vc, gc = inp
        b = jnp.cumsum(gc, axis=2)
        o_inter = jnp.einsum('bhtd,bhdv->bhtv', qc * jnp.exp(b), S)
        diff = b[:, :, :, None, :] - b[:, :, None, :, :]
        decay = jnp.exp(jnp.where(tri[None, None, :, :, None], diff, -jnp.inf))
        att = jnp.einsum('bhtd,bhsd,bhtsd->bhts', qc, kc, decay)
        o = o_inter + jnp.einsum('bhts,bhsv->bhtv', att, vc)
        b_last = b[:, :, -1:, :]
        S = (jnp.exp(b_last[:, :, 0, :])[..., None] * S
             + jnp.einsum('bhsd,bhsv->bhdv', kc * jnp.exp(b_last - b), vc))
        return S, o

    S, o = lax.scan(step, s0.astype(jnp.float32), (chunks(q), chunks(k), chunks(v), chunks(loga)))
    return o.transpose(1, 0, 3, 2, 4).reshape(B, T, H, v.shape[-1]), S

def gla_mix(x, s0, w_in, w_a1, w_a2, b_a, norm_g, w_out):
    B, T, _ = x.shape
    nk, nv = GLA_HEADS * GLA_DK, GLA_HEADS * GLA_DV
    h = x @ w_in
    q = h[..., :nk].reshape(B, T, GLA_HEADS, GLA_DK) * (GLA_DK ** -0.5)
    k = h[..., nk:2 * nk].reshape(B, T, GLA_HEADS, GLA_DK)
    v = h[..., 2 * nk:2 * nk + nv].reshape(B, T, GLA_HEADS, GLA_DV)
    r = h[..., 2 * nk + nv:]
    loga = jax.nn.log_sigmoid(((x @ w_a1) @ w_a2 + b_a).astype(jnp.float32)) / GLA_TAU
    o, S = gla_scan(q, k, v, loga.reshape(B, T, GLA_HEADS, GLA_DK), s0)
    on = o * lax.rsqrt(jnp.mean(jnp.square(o), -1, keepdims=True) + RMS_EPS) * norm_g
    y = (on.reshape(B, T, nv).astype(x.dtype) * jax.nn.silu(r)) @ w_out
    return y, S.astype(x.dtype)

def conv_ffn(x, buf, w_up, conv_w, conv_b, w_down):
    T = x.shape[1]
    u = x @ w_up
    ext = jnp.concatenate([buf.astype(u.dtype), u], axis=1)
    y = conv_b + sum(conv_w[j] * ext[:, j:j + T] for j in range(CONV_W))
    val, gate = y[..., :D_FF], y[..., D_FF:]
    return (jax.nn.silu(gate) * val) @ w_down, ext[:, -(CONV_W - 1):]

def setup_inputs(seed: int = 0) -> dict:
    key = jax.random.key(seed)
    ks = iter(jax.random.split(key, 40))

    def nrm(shape, scale=1.0):
        return jax.random.normal(next(ks), shape, jnp.float32) * scale

    n_pages = PAST_LEN // PAGE_SIZE
    n_used = DEC_BATCH * n_pages
    n_phys = (5 * n_used + 3) // 4
    page_table = jax.random.permutation(next(ks), n_phys)[:n_used].reshape(DEC_BATCH, n_pages).astype(jnp.int32)
    kv_tail = (2, N_SWA_HEADS, HEAD_DIM)
    return {
        "x_prompt": nrm((BATCH, SEQ, D_MODEL)),
        "x_sample": nrm((DEC_BATCH, DEC_SEQ, D_MODEL)),
        "cache_moba_kv": nrm((N_EVEN, n_phys, PAGE_SIZE, 2, N_MOBA_HEADS, HEAD_DIM)),
        "state_swa0_kv": nrm((N_EVEN, DEC_BATCH, min(SWA_GROUPS[0][0], PAST_LEN)) + kv_tail),
        "state_swa1_kv": nrm((N_EVEN, DEC_BATCH, min(SWA_GROUPS[1][0], PAST_LEN)) + kv_tail),
        "state_swa2_kv": nrm((N_EVEN, DEC_BATCH, min(SWA_GROUPS[2][0], PAST_LEN)) + kv_tail),
        "state_gla": nrm((N_ODD, DEC_BATCH, GLA_HEADS, GLA_DK, GLA_DV), 2.0),
        "state_ffn_conv": nrm((DEPTH, DEC_BATCH, CONV_W - 1, 2 * D_FF)),
        "page_table": page_table,
        "attn_w_in": nrm((N_EVEN, D_MODEL, ATTN_IN), D_MODEL ** -0.5),
        "attn_w_out": nrm((N_EVEN, ATTN_OUT, D_MODEL), ATTN_OUT ** -0.5 * DN_BETA),
        "gla_w_in": nrm((N_ODD, D_MODEL, GLA_IN), D_MODEL ** -0.5),
        "gla_w_a1": nrm((N_ODD, D_MODEL, GLA_RANK), D_MODEL ** -0.5),
        "gla_w_a2": nrm((N_ODD, GLA_RANK, GLA_HEADS * GLA_DK), GLA_RANK ** -0.5),
        "gla_b_a": nrm((N_ODD, GLA_HEADS * GLA_DK), 0.1),
        "gla_norm_g": 1.0 + nrm((N_ODD, GLA_DV), 0.01),
        "gla_w_out": nrm((N_ODD, GLA_HEADS * GLA_DV, D_MODEL), (GLA_HEADS * GLA_DV) ** -0.5 * DN_BETA),
        "ln_mix_g": 1.0 + nrm((DEPTH, D_MODEL), 0.01),
        "ln_mix_b": nrm((DEPTH, D_MODEL), 0.01),
        "ffn_w_up": nrm((DEPTH, D_MODEL, 2 * D_FF), D_MODEL ** -0.5),
        "ffn_conv_w": nrm((DEPTH, CONV_W, 2 * D_FF), CONV_W ** -0.5),
        "ffn_conv_b": nrm((DEPTH, 2 * D_FF), 0.01),
        "ffn_w_down": nrm((DEPTH, D_FF, D_MODEL), D_FF ** -0.5 * DN_BETA),
        "ln_ffn_g": 1.0 + nrm((DEPTH, D_MODEL), 0.01),
        "ln_ffn_b": nrm((DEPTH, D_MODEL), 0.01),
    }

def reference(x_prompt, x_sample, cache_moba_kv, state_swa0_kv, state_swa1_kv, state_swa2_kv,
              state_gla, state_ffn_conv, page_table, attn_w_in, attn_w_out, gla_w_in, gla_w_a1,
              gla_w_a2, gla_b_a, gla_norm_g, gla_w_out, ln_mix_g, ln_mix_b, ffn_w_up, ffn_conv_w,
              ffn_conv_b, ffn_w_down, ln_ffn_g, ln_ffn_b):
    xp, xs = x_prompt, x_sample
    B = xp.shape[0]
    swa_states = (state_swa0_kv, state_swa1_kv, state_swa2_kv)
    moba_p, moba_s, gla_p, gla_s, conv_p, conv_s = [], [], [], [], [], []
    swa_p = [[] for _ in range(N_SWA_GROUPS)]
    swa_s = [[] for _ in range(N_SWA_GROUPS)]
    for l in range(DEPTH):
        i = l // 2
        if l % 2 == 0:
            mp, rows_p, bufs_p = attn_layer_prompt(xp, attn_w_in[i], attn_w_out[i])
            ms, rows_s, bufs_s = attn_layer_sample(xs, attn_w_in[i], attn_w_out[i], cache_moba_kv[i],
                                                   page_table, [s[i] for s in swa_states])
            moba_p.append(rows_p)
            moba_s.append(rows_s)
            for g in range(N_SWA_GROUPS):
                swa_p[g].append(bufs_p[g])
                swa_s[g].append(bufs_s[g])
        else:
            s0 = jnp.zeros((B, GLA_HEADS, GLA_DK, GLA_DV), jnp.float32)
            mp, sp = gla_mix(xp, s0, gla_w_in[i], gla_w_a1[i], gla_w_a2[i], gla_b_a[i], gla_norm_g[i], gla_w_out[i])
            ms, ss = gla_mix(xs, state_gla[i], gla_w_in[i], gla_w_a1[i], gla_w_a2[i], gla_b_a[i], gla_norm_g[i], gla_w_out[i])
            gla_p.append(sp)
            gla_s.append(ss)
        xp = layer_norm(DN_ALPHA * xp + mp, ln_mix_g[l], ln_mix_b[l])
        xs = layer_norm(DN_ALPHA * xs + ms, ln_mix_g[l], ln_mix_b[l])
        buf0 = jnp.zeros((B, CONV_W - 1, 2 * D_FF), xp.dtype)
        fp, cbp = conv_ffn(xp, buf0, ffn_w_up[l], ffn_conv_w[l], ffn_conv_b[l], ffn_w_down[l])
        fs, cbs = conv_ffn(xs, state_ffn_conv[l], ffn_w_up[l], ffn_conv_w[l], ffn_conv_b[l], ffn_w_down[l])
        conv_p.append(cbp)
        conv_s.append(cbs)
        xp = layer_norm(DN_ALPHA * xp + fp, ln_ffn_g[l], ln_ffn_b[l])
        xs = layer_norm(DN_ALPHA * xs + fs, ln_ffn_g[l], ln_ffn_b[l])
    moba_kv_prompt = jnp.stack(moba_p)
    moba_kv_sample = jnp.stack(moba_s)
    swa0_kv_prompt, swa0_kv_sample = jnp.stack(swa_p[0]), jnp.stack(swa_s[0])
    swa1_kv_prompt, swa1_kv_sample = jnp.stack(swa_p[1]), jnp.stack(swa_s[1])
    swa2_kv_prompt, swa2_kv_sample = jnp.stack(swa_p[2]), jnp.stack(swa_s[2])
    gla_state_prompt, gla_state_sample = jnp.stack(gla_p), jnp.stack(gla_s)
    ffn_conv_prompt, ffn_conv_sample = jnp.stack(conv_p), jnp.stack(conv_s)
    return (xp, xs, moba_kv_prompt, moba_kv_sample, swa0_kv_prompt, swa0_kv_sample,
            swa1_kv_prompt, swa1_kv_sample, swa2_kv_prompt, swa2_kv_sample,
            gla_state_prompt, gla_state_sample, ffn_conv_prompt, ffn_conv_sample)


_drawn_inputs = setup_inputs


def setup_inputs(seed=0):
    import zlib

    import numpy as np

    out = dict(_drawn_inputs(seed))
    spreads = {}
    factors = {'gla_norm_g': 8.0,
     'ln_mix_g': 3.693,
     'ln_mix_b': 3.822,
     'ffn_conv_b': 8.0,
     'ln_ffn_g': 3.868,
     'ln_ffn_b': 3.81}
    for name, (base, spread) in spreads.items():
        noise = np.random.default_rng([zlib.crc32(name.encode()), seed]).standard_normal(out[name].shape)
        drawn = base * np.exp(spread * noise) if base else spread * noise
        out[name] = __import__('jax').numpy.asarray(drawn.astype(out[name].dtype))
    for name, factor in factors.items():
        out[name] = (out[name] * factor).astype(out[name].dtype)
    return out
```

```python
from contextlib import ExitStack

import concourse.bass as bass
from concourse import mybir

F32 = mybir.dt.float32
I32 = mybir.dt.int32
U8 = mybir.dt.uint8
ALU = mybir.AluOpType
ACT = mybir.ActivationFunctionType
AXX = mybir.AxisListType.X

P = 128
D = 1024
KD = D // P
NP = 512
SEQS, T_NEW = 8, 8
NS = SEQS * T_NEW
NT = NP + NS
TILES = [(0, P), (P, P), (2 * P, P), (3 * P, P), (NP, NS)]
NTILE = len(TILES)
PQ = NP // P
HALF = 512
HD = 64
PAGE = 128
DFF = 2816
NJ = DFF // P
DOWN_GROUPS = [(0, 8), (8, 8), (16, 6)]
SIDE = 2 * SEQS + 4
TAIL = 2 + 2 * SEQS
ALPHA = (2.0 * 2) ** 0.25
LN_EPS = 1e-5
RMS_EPS = 1e-6
ATT_SCALE = HD ** -0.5
GH, GK, GV = 4, 128, 256
NLEV = 7
TAU = 16.0
LOWEST = -3.0e38

GROUP_PAST = [256, 128, 256, 256]
GROUP_AT = [0, 320, 512, 832]
S_COLS = 1152
CACHE_BLOCK = [0, 2, 3, 5]
NBLK = 7
KEY_BLOCKS = []
for g_ in range(4):
    for b_ in range(GROUP_PAST[g_] // P):
        KEY_BLOCKS.append((GROUP_AT[g_] + b_ * P, P, g_, CACHE_BLOCK[g_] + b_))
    KEY_BLOCKS.append((GROUP_AT[g_] + GROUP_PAST[g_], NS, g_, None))

CHUNKS = ([("attn_in", c, NTILE) for c in range(6)] + [("attn_out", 0, 2 * NTILE)]
          + [("down0", c, NTILE) for c in range(6)]
          + [("gla_q", 0, GH), ("gla_k", 0, GH)] + [("gla_v", c, NTILE) for c in range(2)]
          + [("gla_r", c, NTILE) for c in range(2)] + [("gla_out", c, NTILE) for c in range(2)]
          + [("down1", c, NTILE) for c in range(6)])
RING = 3
CHUNK_NO = {(k, c): n for n, (k, c, _) in enumerate(CHUNKS)}
STEPS_BEFORE = [sum(s for _, _, s in CHUNKS[:n]) for n in range(len(CHUNKS) + 1)]


def steps_at(kind, c, t):
    return STEPS_BEFORE[CHUNK_NO[(kind, c)]] + t + 1


LEV_WITH_SAMPLE = [l < 3 or l == NLEV for l in range(NLEV + 1)]
LEV_BEFORE = [sum(1 + w for w in LEV_WITH_SAMPLE[:l]) for l in range(NLEV + 2)]
LEV_ALL = LEV_BEFORE[-1]


def pieces_of(t, g):
    return g != 1 or t >= PQ - 1


ROPED = 3
K_STORES, stores_ = [], [0] * ROPED
for r_ in range(4 * NTILE):
    c_, t_ = divmod(r_, NTILE)
    stores_[r_ % ROPED] += 16 * sum(pieces_of(t_, 2 * (c_ - 2) + half_) for half_ in range(2)) if c_ >= 2 else 0
    K_STORES.append(stores_[r_ % ROPED])
V_STORES = 16 * sum(pieces_of(t_, g_) for t_ in range(NTILE) for g_ in range(4))


class Count:

    def __init__(self, sem):
        self.sem, self.n = sem, 0

    def one(self):
        self.n += 1
        return 1


def build_program(nc, io):
    with ExitStack() as ctx:
        def sb(name, shape, dt=F32):
            return ctx.enter_context(nc.sbuf_tensor(name, shape, dt))

        def sem(name):
            return ctx.enter_context(nc.semaphore(name))

        x_reg = sb("x_reg", [P, NTILE * D])
        xT_reg = sb("xT_reg", [P, KD * NT])
        wring = sb("wring", [P, RING, 4096])
        gb_reg = sb("gb_reg", [P, 2 * D])
        ident = sb("ident", [P, P])
        ln_stats = sb("ln_stats", [P, NTILE, 2, 6])
        ln_mv = sb("ln_mv", [P, NTILE, 2])
        ln_sd = sb("ln_sd", [P, NTILE, 2])
        page_ids = sb("page_ids", [1, 16], I32)
        eps_ln = sb("eps_ln", [P, 2])
        ARENA = 28112
        arena = sb("arena", [P, ARENA])
        ps = ctx.enter_context(nc.psum_tensor("ps", [P, 8, HALF], F32))
        TURN = (5, 6)

        x_tok = x_reg[:, :].rearrange("p (t c) -> p t c", t=NTILE)
        xT = xT_reg[:, :].rearrange("p (k n) -> p k n", k=KD)
        gb = gb_reg[:, :].rearrange("p (a c) -> p a c", a=2)

        def cut(region, at, n):
            return region[:, at:at + n]

        v_tok = cut(arena, 0, 5120).rearrange("p (t c) -> p t c", t=NTILE)
        qkT = cut(arena, 5120, 16 * NT).rearrange("p (c n) -> p c n", c=16)
        v_cache = cut(arena, 14336, 4 * NBLK * 256).rearrange("p (s b c) -> p s b c", s=4, b=NBLK)
        masks = cut(arena, 21504, 1792)
        MASK_AT = [0, 512, 768, 1280]
        s_buf = cut(arena, 23296, 3584).rearrange("p (b c) -> p b c", b=2)

        def score_at(qi, g):
            width = (qi + 1) * P
            return [0, 512, 512 + min(width, 256), 512 + min(width, 256) + width][g]

        small = cut(arena, 26880, 512)
        mx = small[:, 0:64].rearrange("p (n g) -> p n g", g=4)
        mb = small[:, 64:96].rearrange("p (n g) -> p n g", g=2)
        nm = small[:, 96:128].rearrange("p (n g) -> p n g", g=2)
        den = small[:, 128:160].rearrange("p (n g) -> p n g", g=2)
        rden = small[:, 160:192].rearrange("p (n g) -> p n g", g=2)
        smx = small[:, 192:200].rearrange("p (n g) -> p n g", g=4)
        smb = small[:, 200:204].rearrange("p (n g) -> p n g", g=2)
        snm = small[:, 204:208].rearrange("p (n g) -> p n g", g=2)
        sden = small[:, 208:212].rearrange("p (n g) -> p n g", g=2)
        srd = small[:, 212:216].rearrange("p (n g) -> p n g", g=2)
        rope_a = cut(arena, 23296, 512)
        rope_b = cut(arena, 23808, 512)
        roped_buf = cut(arena, 24320, 1536).rearrange("p (b c) -> p b c", b=3)
        cos_t = cut(arena, 25856, 320).rearrange("p (t c) -> p t c", t=NTILE)
        sin_t = cut(arena, 26176, 320).rearrange("p (t c) -> p t c", t=NTILE)
        k_stage = cut(x_reg, 0, NBLK * 256).rearrange("p (b c) -> p b c", b=NBLK)
        pT = cut(x_reg, 1792, 14 * P).rearrange("p (b c) -> p b c", b=14)
        s_mask = cut(x_reg, 3584, S_COLS)
        oT = cut(xT_reg, 0, 4 * NT).rearrange("p (c n) -> p c n", c=4)
        kcT = cut(xT_reg, 2304, 14 * P).rearrange("p (a c) -> p a c", a=14)
        o_tok = cut(xT_reg, 4096, 512)
        qz = gb_reg[:, :].rearrange("p (c s h q) -> p c s h q", c=8, s=SEQS, h=4)

        hT = cut(arena, 0, NJ * NT).rearrange("p (j n) -> p j n", j=NJ)
        wup = cut(arena, 12672, 4096).rearrange("p (u v k c) -> p u v k c", u=2, v=2, k=KD)
        side = cut(arena, 16768, 2 * DFF)
        feat = cut(arena, 22400, 2 * NJ * SIDE).rearrange("p (v j r) -> p v j r", v=2, j=NJ)
        ext = cut(arena, 23280, 4 * 514).rearrange("p (u v n) -> p u v n", u=2, v=2)
        ext_s = cut(arena, 25336, 320).rearrange("p (u v s n) -> p u v s n", u=2, v=2, s=SEQS)
        conv_y = cut(arena, 25656, 4 * NT).rearrange("p (u v n) -> p u v n", u=2, v=2)
        fj = cut(arena, 27960, 2 * 2 * SIDE).rearrange("p (u v r) -> p u v r", u=2, v=2)
        tl = cut(arena, 28040, 4 * TAIL).rearrange("p (u v r) -> p u v r", u=2, v=2)

        g_v = cut(arena, 0, 5120).rearrange("p (t c) -> p t c", t=NTILE)
        g_r = cut(arena, 5120, 5120).rearrange("p (t c) -> p t c", t=NTILE)
        g_q = cut(arena, 10240, GH * NT).rearrange("p (h n) -> p h n", h=GH)
        g_k = cut(arena, 12544, GH * NT).rearrange("p (h n) -> p h n", h=GH)
        g_b = cut(arena, 14848, GH * NT).rearrange("p (h n) -> p h n", h=GH)
        g_tmp = cut(arena, 17152, GH * NT)
        lev_e = cut(arena, 17152, 2 * NT).rearrange("p (b n) -> p b n", b=2)
        lev_q = cut(arena, 18304, 2 * NT).rearrange("p (b n) -> p b n", b=2)
        lev_k = cut(arena, 19456, 2 * NT).rearrange("p (b n) -> p b n", b=2)
        att = cut(arena, 20608, 2 * NT).rearrange("p (b n) -> p b n", b=2)
        g_qb = cut(arena, 21760, NT)
        g_kb = cut(arena, 22336, NT)
        g_kt = cut(arena, 22912, NTILE * P).rearrange("p (t c) -> p t c", t=NTILE)
        g_qz = cut(arena, 23552, SEQS * NS).rearrange("p (s n) -> p s n", s=SEQS)
        g_kz = cut(arena, 24064, SEQS * P).rearrange("p (s n) -> p s n", s=SEQS)
        g_state = cut(arena, 25088, GV)
        g_sst = cut(arena, 25344, SEQS * GV).rearrange("p (s n) -> p s n", s=SEQS)
        g_mask = cut(arena, 27392, (NLEV + 1) * P // 4).bitcast(U8).rearrange("p (l c) -> p l c", l=NLEV + 1)
        mask_words = cut(arena, 20608, (NLEV + 1) * P).bitcast(I32).rearrange("p (l c) -> p l c", l=NLEV + 1)
        g_small = cut(arena, 27648, 64)
        g_ss = g_small[:, 0:20].rearrange("p (t h) -> p t h", t=NTILE)
        g_rs = g_small[:, 20:40].rearrange("p (t h) -> p t h", t=NTILE)
        g_ba = g_small[:, 40:44]
        g_a1 = cut(arena, 27712, P).rearrange("p (k r) -> p k r", k=KD)
        g_norm = cut(arena, 27840, GV)
        seq_of_row = cut(arena, 28096, SEQS)[0:NS, :]
        g_qz_own = cut(arena, 23552, SEQS * (NS + T_NEW)).rearrange("p (s n) -> p s n", s=SEQS)[:, :, 0:T_NEW]
        g_reset = cut(arena, 24064, NT)
        g_a2 = cut(arena, 22912, 512)
        g_t1 = cut(arena, 23424, NT)
        squares = sb("squares", [P, GV])

        x_loaded = sem("x_loaded")
        consts_loaded = sem("consts_loaded")
        pages_loaded = sem("pages_loaded")
        w_loaded = [sem(f"w_loaded{i}") for i in range(RING)]
        steps = sem("steps")
        turned = sem("turned")
        turned_out = sem("turned_out")
        vec = sem("vec")
        qk_read = sem("qk_read")
        roped = sem("roped")
        v_stored = sem("v_stored")
        qz_zero = sem("qz_zero")
        v_read = sem("v_read")
        k_stored = [sem(f"k_stored{i}") for i in range(ROPED)]
        kv_stored = sem("kv_stored")
        s_ready = sem("s_ready")
        s_read = sem("s_read")
        nm_ready = sem("nm_ready")
        probs = sem("probs")
        pv_done = sem("pv_done")
        o_ready = sem("o_ready")
        qz_ready = sem("qz_ready")
        k_cached = sem("k_cached")
        v_cached = sem("v_cached")
        smask_loaded = sem("smask_loaded")
        sc_done = sem("sc_done")
        s_norm = sem("s_norm")
        spv_done = sem("spv_done")
        soT_ready = sem("soT_ready")
        x_again = sem("x_again")
        gb_loaded = sem("gb_loaded")
        z_read = sem("z_read")
        ln_var = sem("ln_var")
        ln_root = sem("ln_root")
        ln_done = sem("ln_done")
        side_loaded = sem("side_loaded")
        pads_zero = sem("pads_zero")
        wup_loaded = [sem(f"wup_loaded{u}") for u in range(2)]
        up_filled = sem("up_filled")
        ext_ready = sem("ext_ready")
        conv_step = sem("conv_step")
        silu_done = sem("silu_done")
        tail_ready = sem("tail_ready")
        tail_turned = sem("tail_turned")
        tail_out = sem("tail_out")
        tail_stored = sem("tail_stored")
        gla_loaded = sem("gla_loaded")
        gla_state_in = sem("gla_state_in")
        gla_state_out = sem("gla_state_out")
        fm_read = sem("fm_read")
        low_filled = sem("low_filled")
        gates = sem("gates")
        tok_read = sem("tok_read")
        r_scaled = sem("r_scaled")
        lev_diff = sem("lev_diff")
        lev_exp = sem("lev_exp")
        lev_ready = sem("lev_ready")
        lev_prod = sem("lev_prod")
        lev_read = sem("lev_read")
        kz_ready = sem("kz_ready")
        go_done = sem("go_done")
        gs_done = sem("gs_done")
        sq_done = sem("sq_done")
        go_read = sem("go_read")
        gs_read = sem("gs_read")
        y_ready = sem("y_ready")
        y_stored = sem("y_stored")

        TURNS_X = 2 * NTILE
        TURNS_QK = 4 * NTILE
        P_BLOCKS = [(qi + 1) + min(qi + 1, 2) + 2 * (qi + 1) for qi in range(PQ)]
        P_BATCH = [-(-b // 4) for b in P_BLOCKS]
        UP0 = TURNS_X + TURNS_QK
        K_BATCH = 4
        SP_BATCH = -(-len(KEY_BLOCKS) // 4)
        BATCH_BEFORE_SAMPLE = UP0 + 4 * sum(P_BATCH) + PQ
        BATCH_GLA = BATCH_BEFORE_SAMPLE + 2 * (4 * K_BATCH + SP_BATCH) + 2 * TURNS_X + 2

        block = ctx.enter_context(nc.Block())

        def chunk_source(kind, c):
            def whole(w, cols):
                return w[:, cols].rearrange("(k p) c -> p k c", p=P)
            def ring(n, k):
                return lambda slot: wring[:, slot, 0:n * k].rearrange("p (k c) -> p k c", k=k)
            if kind == "attn_in":
                return whole(io["attn_w_in"][0], slice(c * HALF, (c + 1) * HALF)), ring(HALF, KD)
            if kind == "attn_out":
                return whole(io["attn_w_out"][0], slice(0, D)), ring(D, 4)
            if kind in ("down0", "down1"):
                half, (k0, kn) = c // 3, DOWN_GROUPS[c % 3]
                w = io["ffn_w_down"][int(kind[-1])]
                return (w[k0 * P:(k0 + kn) * P, half * HALF:(half + 1) * HALF]
                        .rearrange("(k p) c -> p k c", p=P)), ring(HALF, kn)
            if kind == "gla_out":
                return whole(io["gla_w_out"][0], slice(c * HALF, (c + 1) * HALF)), ring(HALF, KD)
            first = {"gla_q": 0, "gla_k": 1, "gla_v": 2, "gla_r": 4}[kind] + c
            return whole(io["gla_w_in"][0], slice(first * HALF, (first + 1) * HALF)), ring(HALF, KD)

        def ring_at(n):
            kind, c, _ = CHUNKS[n]
            return chunk_source(kind, c)[1](n % RING)

        @block.sync
        def _(sp):
            def load_chunk(n):
                if n >= RING:
                    sp.wait_ge(steps, STEPS_BEFORE[n - RING + 1])
                src, _ = chunk_source(*CHUNKS[n][:2])
                sp.dma_start(ring_at(n), src).then_inc(w_loaded[n % RING], 16)

            sp.dma_start(x_tok[:, 0:PQ, :], io["x_prompt"][0].rearrange("(t p) c -> p t c", p=P)).then_inc(x_loaded, 16)
            sp.dma_start(x_tok[0:NS, PQ, :], io["x_sample"].rearrange("s t c -> (s t) c")).then_inc(x_loaded, 16)
            for n in range(RING):
                load_chunk(n)
            sp.dma_start(page_ids[:, :], io["page_table"].rearrange("s (g o) -> o (s g)", o=1)).then_inc(pages_loaded, 16)
            for g in range(3):
                rows = io[f"state_swa{g}_kv"].shape[2]
                sp.dma_start(io[f"swa{g}_s"][0, :, 0:rows - T_NEW].rearrange("s r a h d -> s (r a h d)"),
                             io[f"state_swa{g}_kv"][0, :, T_NEW:rows].rearrange("s r a h d -> s (r a h d)")).then_inc(kv_stored, 16)
            for n in range(RING, 7):
                load_chunk(n)
            sp.wait_ge(turned, TURNS_X)
            sp.dma_start(s_mask, io["sample_masks"][:, 0, :]).then_inc(smask_loaded, 16)
            sp.wait_ge(pages_loaded, 16)

            def cache_rows(s, what):
                def to(b, n):
                    return k_stage[:, b:b + n, :] if what == 0 else v_cache[:, s % 4, b:b + n, :]
                done = k_cached if what == 0 else v_cached
                for pg in range(2):
                    page = sp.value_load(page_ids[0:1, 2 * s + pg:2 * s + pg + 1], min_val=0,
                                         max_val=io["cache_moba_kv"].shape[1] - 1)
                    src = io["cache_moba_kv"][0, bass.ds(page, 1), :, what].rearrange("o r h d -> r o (h d)")
                    sp.dma_start(to(pg, 1), src).then_inc(done, 16)
                for g in range(3):
                    src = io[f"state_swa{g}_kv"][0, s, :, what].rearrange("(b r) h d -> r b (h d)", r=P)
                    sp.dma_start(to(CACHE_BLOCK[g + 1], GROUP_PAST[g + 1] // P), src).then_inc(done, 16)

            for s in range(4):
                cache_rows(s, 1)
            for s in range(SEQS):
                if s >= 1:
                    sp.wait_ge(turned, BATCH_BEFORE_SAMPLE + s * K_BATCH + (SP_BATCH if s > 4 else 0))
                if s == 4:
                    sp.wait_ge(s_read, 16 * 4 + 4)
                    sp.dma_start(s_mask, io["sample_masks"][:, 1, :]).then_inc(smask_loaded, 16)
                cache_rows(s, 0)
                if s == 4:
                    sp.wait_ge(spv_done, 1)
                    for s2 in range(4, SEQS):
                        cache_rows(s2, 1)
            sp.wait_ge(spv_done, 2)
            sp.dma_start(x_tok[:, 0:PQ, :], io["x_prompt"][0].rearrange("(t p) c -> p t c", p=P)).then_inc(x_again, 16)
            sp.dma_start(x_tok[0:NS, PQ, :], io["x_sample"].rearrange("s t c -> (s t) c")).then_inc(x_again, 16)

            def load_ln(n, which, l):
                for a, v in enumerate((io[f"ln_{which}_g"], io[f"ln_{which}_b"])):
                    sp.dma_start(gb[:, a, :], v[l:l + 1, :].partition_broadcast(P)
                                 .rearrange("q o c -> q (o c)")).then_inc(gb_loaded, 16)

            def ffn_up(l, between):
                for a, (r0, rn, src) in enumerate((
                        (0, 2 * SEQS, io["state_ffn_conv"][l].rearrange("s r c -> (s r) c")),
                        (2 * SEQS, 3, io["ffn_conv_w"][l]),
                        (2 * SEQS + 3, 1, io["ffn_conv_b"][l:l + 1, :]))):
                    sp.dma_start(side[r0:r0 + rn, :], src).then_inc(side_loaded, 16)

                def load_up(j, u):
                    for v in range(2):
                        src = (io["ffn_w_up"][l].rearrange("(k p) c -> p k c", p=P)
                               [:, :, bass.ds(j * P + v * DFF, P)])
                        sp.dma_start(wup[:, u, v, :, :], src).then_inc(wup_loaded[u], 16)
                load_up(0, 0)
                load_up(1, 1)
                for n in between:
                    load_chunk(n)
                with sp.Fori(0, NJ // 2 - 1) as i:
                    for u in range(2):
                        sp.wait_ge(up_filled, i * 2 + (l * NJ + u + 1))
                        load_up(i * 2 + (2 + u), u)

            sp.wait_ge(soT_ready, 2)
            load_ln(0, "mix", 0)
            load_chunk(7)
            load_chunk(8)
            ffn_up(0, [9])
            sp.wait_ge(ln_done, NTILE)
            load_ln(1, "ffn", 0)
            for n in range(10, 13):
                load_chunk(n)
            sp.wait_ge(tail_stored, 32)
            sp.wait_ge(conv_step, NJ * 13)
            sp.dma_start(mask_words, io["level_masks"]).then_inc(gla_loaded, 16)
            sp.dma_start(g_a1, io["gla_w_a1"][0].rearrange("(k p) r -> p k r", p=P)).then_inc(gla_loaded, 16)
            with nc.allow_non_contiguous_dma(reason="512 biases, feature-major"):
                sp.dma_start(g_ba, io["gla_b_a"][0].rearrange("(h d o) -> d h o", h=GH, o=1).rearrange("d h o -> d (h o)")).then_inc(gla_loaded, 16)
            sp.dma_start(g_a2[0:16, :], io["gla_w_a2"][0]).then_inc(gla_loaded, 16)
            sp.dma_start(g_reset, io["scan_reset"]).then_inc(gla_loaded, 16)
            sp.dma_start(g_norm, io["gla_norm_g"][0:1, :].partition_broadcast(P).rearrange("q o c -> q (o c)")).then_inc(gla_loaded, 16)
            sp.dma_start(seq_of_row, io["seq_of_row"]).then_inc(gla_loaded, 16)
            for n in range(13, 19):
                load_chunk(n)
            sp.wait_ge(ln_done, 2 * NTILE)
            load_ln(2, "mix", 1)
            for h in range(GH):
                if h >= 1:
                    sp.wait_ge(gla_state_out, 32 * h)
                sp.dma_start(g_sst, io["state_gla"][0, :, h].rearrange("s d v -> d s v")).then_inc(gla_state_in, 16)
                if h < 2:
                    load_chunk(19 + h)
            sp.wait_ge(go_done, GH * NTILE)
            sp.wait_ge(gla_state_out, 32 * GH)
            sp.wait_ge(go_read, GH * NTILE)
            load_chunk(21)
            ffn_up(1, [22, 23])
            sp.wait_ge(ln_done, 3 * NTILE)
            load_ln(3, "ffn", 1)
            for n in range(24, 27):
                load_chunk(n)

        @block.tensor
        def _(pe):
            batch = Count(turned)

            def turn(pieces):
                bank = TURN[batch.n % 2]
                if batch.n >= 2:
                    pe.wait_ge(turned_out, batch.n - 1)
                for col, src in pieces:
                    rows, cols = src.shape
                    last = pe.transpose(ps[0:cols, bank, col:col + rows], src, ident[0:rows, 0:rows])
                last.then_inc(turned, batch.one())

            def turn_x(t):
                r0, n = TILES[t]
                for half in range(2):
                    turn([(j * P, x_tok[0:n, t, (half * 4 + j) * P:(half * 4 + j + 1) * P]) for j in range(4)])

            def chunk_here(n):
                pe.wait_ge(w_loaded[n % RING], 16 * (n // RING + 1))

            def project(srcT, t, w, bank, ks, first, last_group, k_src0=0):
                r0, n = TILES[t]
                for i in range(ks):
                    mm = pe.matmul(ps[0:n, bank, :], srcT[:, k_src0 + i, r0:r0 + n], w[:, i, :],
                                   start=first and i == 0, stop=last_group and i == ks - 1)
                mm.then_inc(steps, 1)

            pe.wait_ge(consts_loaded, 16)
            pe.wait_ge(x_loaded, 32)
            for t in range(NTILE):
                turn_x(t)

            def turn_rope(r):
                c, t = divmod(r, NTILE)
                n = TILES[t][1]
                pe.wait_ge(roped, r + 1)
                turn([(j * P, roped_buf[0:n, r % 3, j * P:(j + 1) * P]) for j in range(4)])

            for c in range(6):
                chunk_here(c)
                for t in range(NTILE):
                    if c == 0:
                        pe.wait_ge(turned_out, 2 * t + 2)
                    elif c <= 4:
                        pe.wait_ge(qk_read, (c - 1) * NTILE + t + 1)
                    else:
                        pe.wait_ge(v_read, t + 1)
                    project(xT, t, ring_at(c), t, KD, True, True)
                    r = c * NTILE + t - 2
                    if 0 <= r < 4 * NTILE:
                        turn_rope(r)

            def head_rows(g, h):
                return slice(HD * (h % 2), HD * (h % 2) + HD), 2 * g + h // 2

            def scores(n):
                qi, h = divmod(n, 4)
                for g in range(4):
                    rows, c = head_rows(g, h)
                    k0 = max(0, qi - 1) * P if g == 1 else 0
                    if n >= 1:
                        pe.wait_ge(s_read, 4 * (n - 1) + g + 1)
                    elif g == 0:
                        pe.wait_ge(turned_out, UP0)
                        pe.wait_ge(qk_read, 4 * NTILE)
                        pe.wait_ge(v_read, 2 * NTILE)
                    pe.matmul(ps[:, g, 0:(qi + 1) * P - k0], qkT[rows, c, qi * P:(qi + 1) * P],
                              qkT[rows, 8 + c, k0:(qi + 1) * P], start=True, stop=True).then_inc(s_ready, 1)

            def prob_blocks(qi):
                out = []
                for g in range(4):
                    k0 = max(0, qi - 1) if g == 1 else 0
                    out += [(score_at(qi, g) + (kt - k0) * P, kt, g) for kt in range(k0, qi + 1)]
                return out

            def values(n):
                qi, h = divmod(n, 4)
                blocks = prob_blocks(qi)
                pe.wait_ge(probs, 2 * n + 2)
                for b0 in range(0, len(blocks), 4):
                    turn([(j * P, s_buf[:, n % 2, col:col + P]) for j, (col, _, _) in enumerate(blocks[b0:b0 + 4])])
                if n >= 2:
                    pe.wait_ge(o_ready, 2 * (n - 1))
                pe.wait_ge(turned_out, batch.n)
                bank = (4, 7)[n % 2]
                for merged in range(2):
                    mine = [i for i, b in enumerate(blocks) if (b[2] > 0) == bool(merged)]
                    for i in mine:
                        _, kt, g = blocks[i]
                        mm = pe.matmul(ps[:, bank, merged * HD:merged * HD + HD], pT[:, i, :],
                                       v_tok[:, kt, (4 * g + h) * HD:(4 * g + h + 1) * HD],
                                       start=i == mine[0], stop=i == mine[-1])
                mm.then_inc(pv_done, 1)

            def turn_o(qi):
                pe.wait_ge(o_ready, 8 * (qi + 1))
                turn([(j * P, o_tok[:, j * P:(j + 1) * P]) for j in range(4)])

            scores(0)
            for n in range(16):
                if n + 1 < 16:
                    scores(n + 1)
                values(n)
                if n % 4 == 3:
                    turn_o(n // 4)

            pe.wait_ge(qz_ready, 1)
            for tile in range(2):
                for s4 in range(4):
                    s = 4 * tile + s4
                    pe.wait_ge(k_cached, 80 * (s + 1))
                    for b0 in range(0, 14, 4):
                        turn([(j * P, k_stage[:, (b0 + j) % NBLK, (b0 + j) // NBLK * P:(b0 + j) // NBLK * P + P])
                              for j in range(min(4, 14 - b0))])
                    pe.wait_ge(turned_out, batch.n)
                    if s4 == 0:
                        pe.wait_ge(s_read, 64 + 4 * tile)
                    for g in range(4):
                        rows = slice(32 * s4, 32 * s4 + 32)
                        past = GROUP_PAST[g]
                        for pair in range(2):
                            b = pair * NBLK + CACHE_BLOCK[g]
                            pe.matmul(ps[rows, g, 0:past], qz[:, 2 * g + pair, s].rearrange("p h q -> p (h q)"),
                                      kcT[:, b:b + past // P, :].rearrange("p b c -> p (b c)"),
                                      start=pair == 0, stop=pair == 1, tile_position=(0, 32 * s4))
                        for pair in range(2):
                            mm = pe.matmul(ps[rows, g, past:past + NS], qz[:, 2 * g + pair, s].rearrange("p h q -> p (h q)"),
                                           qkT[:, 8 + 2 * g + pair, NP:NT],
                                           start=pair == 0, stop=pair == 1, tile_position=(0, 32 * s4))
                    mm.then_inc(sc_done, 1)
                pe.wait_ge(s_norm, 2 * tile + 2)
                pe.wait_ge(v_cached, 320 * (tile + 1))
                for b0 in range(0, len(KEY_BLOCKS), 4):
                    turn([(j * P, s_buf[:, 0, col:col + kn]) for j, (col, kn, _, _) in enumerate(KEY_BLOCKS[b0:b0 + 4])])
                pe.wait_ge(turned_out, batch.n)
                if tile == 0:
                    pe.wait_ge(o_ready, 32)
                else:
                    pe.wait_ge(soT_ready, 1)
                for merged in range(2):
                    mine = [i for i, b in enumerate(KEY_BLOCKS) if (b[2] > 0) == bool(merged)]
                    mine = [i for i in mine if KEY_BLOCKS[i][3] is None] + [i for i in mine if KEY_BLOCKS[i][3] is not None]
                    for pair in range(2):
                        at = (2 * merged + pair) * P
                        for i in mine:
                            _, kn, g, cb = KEY_BLOCKS[i]
                            if cb is None:
                                mm = pe.matmul(ps[:, 4, at:at + P], v_tok[0:NS, PQ, g * 256 + pair * P:g * 256 + pair * P + P],
                                               pT[0:NS, i, :], start=i == mine[0], stop=False, skip_group_check=True)
                                continue
                            for s4 in range(4):
                                mm = pe.matmul(ps[:, 4, at + 32 * s4:at + 32 * s4 + 32], v_cache[:, s4, cb, pair * P:pair * P + P],
                                               pT[:, i, 32 * s4:32 * s4 + 32], start=False, stop=i == mine[-1],
                                               skip_group_check=True)
                mm.then_inc(spv_done, 1)

            pe.wait_ge(soT_ready, 2)
            chunk_here(6)
            w = ring_at(6)
            for half in range(2):
                for t in range(NTILE):
                    if half == 1:
                        pe.wait_ge(z_read, t + 1)
                    project(oT, t, w[:, :, half * HALF:(half + 1) * HALF], t, 4, True, True)

            def after_ln(stage):
                for t in range(NTILE):
                    pe.wait_ge(ln_done, stage * NTILE + t + 1)
                    turn_x(t)
                pe.wait_ge(turned_out, batch.n)

            def ffn(l):
                pe.wait_ge(side_loaded, 48 * (l + 1))
                for v in range(2):
                    turn([(j * SIDE, side[0:SIDE, (v * NJ + j) * P:(v * NJ + j + 1) * P]) for j in range(NJ)])
                pe.wait_ge(turned_out, batch.n)

                def up(j, u, first):
                    pe.wait_ge(wup_loaded[u], (j - u) * 16 + (l * NJ * 16 + 32))
                    if not first:
                        pe.wait_ge(ext_ready, j + (l * NJ - 1))
                    sbank = (4, 7)[u]
                    for v in range(2):
                        for k in range(KD):
                            pe.matmul(ps[:, 2 * v + u, :], wup[:, u, v, k, :], xT[:, k, 0:NP], start=k == 0, stop=k == KD - 1)
                        for k in range(KD):
                            mm = pe.matmul(ps[:, sbank, v * NS:v * NS + NS], wup[:, u, v, k, :], xT[:, k, NP:NT],
                                           start=k == 0, stop=k == KD - 1)
                    mm.then_inc(up_filled, 1)

                def turn_tail(j, u, first):
                    pe.wait_ge(tail_ready, j + (l * NJ + 1))
                    if not first:
                        pe.wait_ge(tail_out, j + (l * NJ - 1))
                    for v in range(2):
                        mm = pe.transpose(ps[0:TAIL, TURN[u], v * P:v * P + P], tl[:, u, v, :], ident[:, :])
                    mm.then_inc(tail_turned, 1)

                up(0, 0, True)
                up(1, 1, True)
                turn_tail(0, 0, True)
                with pe.Fori(1, NJ // 2) as i:
                    up(i * 2, 0, False)
                    turn_tail(i * 2 - 1, 1, False)
                    up(i * 2 + 1, 1, False)
                    turn_tail(i * 2, 0, False)
                turn_tail(NJ - 1, 1, False)

                pe.wait_ge(conv_step, (l + 1) * NJ * 13)
                first_chunk = CHUNK_NO[(f"down{l}", 0)]
                zr = (2 + 4 * l) * NTILE
                for c in range(6):
                    half, (k0, kn) = c // 3, DOWN_GROUPS[c % 3]
                    chunk_here(first_chunk + c)
                    for t in range(NTILE):
                        if c == 0 and t == 0:
                            pe.wait_ge(ext_ready, (l + 1) * NJ)
                        if c == 3:
                            pe.wait_ge(z_read, zr + t + 1)
                        project(hT, t, ring_at(first_chunk + c), t, kn, c % 3 == 0, c % 3 == 2, k0)

            after_ln(0)
            ffn(0)
            pe.wait_ge(tail_out, NJ)
            after_ln(1)

            fm = Count(fm_read)

            def fm_banks(i):
                return i % 2, 2 + i % 2

            def feature_major(i, kn, lhs, rhs, done, bias_free=True):
                a, b = fm_banks(i)
                for k in range(kn):
                    pe.matmul(ps[:, a, :], lhs(k), rhs(k, 0, NP), start=k == 0, stop=k == kn - 1)
                for k in range(kn):
                    mm = pe.matmul(ps[:, b, 0:NS], lhs(k), rhs(k, NP, NT), start=k == 0, stop=k == kn - 1)
                mm.then_inc(done, 1)

            for i in range(2 * GH):
                n = 13 + i // GH
                if i % GH == 0:
                    chunk_here(n)
                if i >= 2:
                    pe.wait_ge(fm_read, i - 1)
                w, h = ring_at(n), i % GH
                feature_major(i, KD, lambda k: w[:, k, h * P:(h + 1) * P], lambda k, a, b: xT[:, k, a:b], steps)
            pe.wait_ge(gla_loaded, 112)
            for k in range(KD):
                pe.matmul(ps[0:16, 4, :], g_a1[:, k, :], xT[:, k, 0:NP], start=k == 0, stop=k == KD - 1)
            for k in range(KD):
                mm = pe.matmul(ps[0:16, 7, 0:NS], g_a1[:, k, :], xT[:, k, NP:NT], start=k == 0, stop=k == KD - 1)
            mm.then_inc(low_filled, 1)
            pe.wait_ge(fm_read, 2 * GH + 1)
            for h in range(GH):
                if h >= 2:
                    pe.wait_ge(fm_read, 2 * GH + h)
                feature_major(h, 1, lambda k: g_a2[0:16, h * P:(h + 1) * P], lambda k, a, b: g_t1[0:16, a:b], low_filled)
            pe.wait_ge(fm_read, 3 * GH + 1)
            for c in range(4):
                chunk_here(15 + c)
                for t in range(NTILE):
                    if c >= 1:
                        pe.wait_ge(tok_read, (c - 1) * NTILE + t + 1)
                    project(xT, t, ring_at(15 + c), t, KD, True, True)
            pe.wait_ge(tok_read, 4 * NTILE)

            def level_products(h, l):
                a = l % 2
                done = h * LEV_ALL + LEV_BEFORE[l]
                kk, qq = (lev_k[:, a], lev_q[:, a]) if l < NLEV else (g_k[:, h], g_q[:, h])
                if done:
                    pe.wait_ge(lev_read, done)
                if l < NLEV:
                    pe.wait_ge(lev_ready, h * NLEV + l + 1)
                for c in range(PQ):
                    mm = pe.matmul(ps[:, a, c * P:(c + 1) * P], kk[:, c * P:(c + 1) * P], qq[:, c * P:(c + 1) * P],
                                   start=True, stop=True)
                mm.then_inc(lev_prod, 1)
                if LEV_WITH_SAMPLE[l]:
                    pe.matmul(ps[0:NS, 2, 0:NS], kk[:, NP:NT], qq[:, NP:NT], start=True, stop=True).then_inc(lev_prod, 1)

            for h in range(GH):
                for l in range(NLEV + 1):
                    level_products(h, l)
                pe.wait_ge(kz_ready, 3 * h + 1)
                turn([(c * P, g_kb[:, c * P:(c + 1) * P]) for c in range(PQ)])
                turn([(0, g_kb[:, NP:NT])])
                pe.wait_ge(turned_out, batch.n)
                pe.wait_ge(lev_read, (h + 1) * LEV_ALL)
                for c in range(PQ):
                    n = h * NTILE + c
                    if n >= 2:
                        pe.wait_ge(go_read, n - 1)
                    bank = (4, 7)[n % 2]
                    vv = g_v[:, c, h * GV:(h + 1) * GV]
                    mm = pe.matmul(ps[:, bank, 0:GV], att[:, h % 2, c * P:(c + 1) * P], vv, start=True, stop=c == 0)
                    if c >= 1:
                        pe.wait_ge(gs_read, h * (PQ + SEQS) + c)
                        mm = pe.matmul(ps[:, bank, 0:GV], g_qb[:, c * P:(c + 1) * P], g_state, start=False, stop=True)
                    mm.then_inc(go_done, 1)
                    if h >= 1 or c >= 1:
                        pe.wait_ge(gs_read, h * (PQ + SEQS) + c)
                    pe.matmul(ps[:, 3, 0:GV], g_kt[:, c, :], vv, start=True, stop=True).then_inc(gs_done, 1)
                n = h * NTILE + PQ
                pe.wait_ge(go_read, n - 1)
                bank = (4, 7)[n % 2]
                vv = g_v[0:NS, PQ, h * GV:(h + 1) * GV]
                pe.wait_ge(kz_ready, 3 * h + 3)
                pe.wait_ge(gla_state_in, 16 * (h + 1))
                pe.matmul(ps[0:NS, bank, 0:GV], att[0:NS, h % 2, NP:NT], vv, start=True, stop=False)
                for s in range(SEQS):
                    mm = pe.matmul(ps[0:NS, bank, 0:GV], g_qz[:, s, :], g_sst[:, s, :], start=False, stop=s == SEQS - 1)
                mm.then_inc(go_done, 1)
                for s in range(SEQS):
                    pe.wait_ge(gs_read, h * (PQ + SEQS) + PQ + s)
                    pe.matmul(ps[:, 3, 0:GV], g_kz[0:NS, s, :], vv, start=True, stop=True).then_inc(gs_done, 1)

            for t in range(NTILE):
                r0, n = TILES[t]
                pe.wait_ge(y_ready, t + 1)
                for half in range(2):
                    turn([(j * P, g_r[0:n, t, (half * 4 + j) * P:(half * 4 + j + 1) * P]) for j in range(4)])
            pe.wait_ge(turned_out, batch.n)
            pe.wait_ge(lev_read, GH * LEV_ALL)
            pe.wait_ge(gs_read, GH * (PQ + SEQS))
            pe.wait_ge(go_read, GH * NTILE)
            for c in range(2):
                chunk_here(19 + c)
                for t in range(NTILE):
                    if c == 1:
                        pe.wait_ge(z_read, 4 * NTILE + t + 1)
                    project(xT, t, ring_at(19 + c), t, KD, True, True)
            after_ln(2)
            ffn(1)

        @block.scalar
        def _(act):
            batch = Count(turned_out)

            def take(dst, src_view, wait_more=None):
                act.wait_ge(turned, batch.n + 1)
                act.activation(dst, src_view(ps[:, TURN[batch.n % 2], :]), ACT.Copy).then_inc(turned_out, batch.one())

            def take_x(t):
                r0, n = TILES[t]
                for half in range(2):
                    take(xT[:, half * 4:half * 4 + 4, r0:r0 + n],
                         lambda b: b.rearrange("p (j c) -> p j c", j=4)[:, :, 0:n])

            for t in range(NTILE):
                take_x(t)

            for c in range(6):
                for t in range(NTILE):
                    if c >= 4:
                        n = TILES[t][1]
                        act.wait_ge(steps, steps_at("attn_in", c, t))
                        act.activation(v_tok[0:n, t, (c - 4) * HALF:(c - 3) * HALF], ps[0:n, t, :], ACT.Copy).then_inc(v_read, 1)
                    r = c * NTILE + t - 2
                    if 0 <= r < 4 * NTILE:
                        rc, rt = divmod(r, NTILE)
                        r0, rn = TILES[rt]
                        take(qkT[:, 4 * rc:4 * rc + 4, r0:r0 + rn],
                             lambda b: b.rearrange("p (j c) -> p j c", j=4)[:, :, 0:rn])

            def exps(n):
                qi = n // 4
                width = (qi + 1) * P
                sbuf = s_buf[:, n % 2]
                act.wait_ge(nm_ready, n + 1)
                act.activation(sbuf[:, 0:width], sbuf[:, 0:width], ACT.Exp, bias=nm[:, n, 0:1], scale=ATT_SCALE,
                               accum_out=den[:, n, 0:1]).then_inc(probs, 1)
                end = score_at(qi, 3) + width
                act.activation(sbuf[:, 512:end], sbuf[:, 512:end], ACT.Exp, bias=nm[:, n, 1:2], scale=ATT_SCALE,
                               accum_out=den[:, n, 1:2]).then_inc(probs, 1)

            def take_probs(n):
                nblk = P_BLOCKS[n // 4]
                if n >= 1:
                    act.wait_ge(pv_done, n)
                for b0 in range(0, nblk, 4):
                    k = min(4, nblk - b0)
                    take(pT[:, b0:b0 + k, :], lambda b: b.rearrange("p (j c) -> p j c", j=4)[:, 0:k, :])

            exps(0)
            for n in range(16):
                if n + 1 < 16:
                    exps(n + 1)
                take_probs(n)
                if n % 4 == 3:
                    qi = n // 4
                    take(oT[:, :, qi * P:(qi + 1) * P], lambda b: b.rearrange("p (j c) -> p j c", j=4))

            for tile in range(2):
                for s4 in range(4):
                    s = 4 * tile + s4
                    if s >= 1:
                        act.wait_ge(sc_done, s)
                    for b0 in range(0, 14, 4):
                        k = min(4, 14 - b0)
                        take(kcT[:, b0:b0 + k, :], lambda b: b.rearrange("p (j c) -> p j c", j=4)[:, 0:k, :])
                act.wait_ge(nm_ready, 17 + tile)
                for merged, (a, b) in enumerate(((0, 320), (320, S_COLS))):
                    act.activation(s_buf[:, 0, a:b], s_buf[:, 0, a:b], ACT.Exp, bias=snm[:, tile, merged:merged + 1],
                                   scale=ATT_SCALE, accum_out=sden[:, tile, merged:merged + 1]).then_inc(probs, 1)
                act.wait_ge(pv_done, 16)
                if tile:
                    act.wait_ge(spv_done, tile)
                for b0 in range(0, len(KEY_BLOCKS), 4):
                    blocks = KEY_BLOCKS[b0:b0 + 4]
                    full = [b[1] for b in blocks]
                    act.wait_ge(turned, batch.n + 1)
                    bank = TURN[batch.n % 2]
                    for j, kn in enumerate(full):
                        ins = act.activation(pT[0:kn, b0 + j, :], ps[0:kn, bank, j * P:(j + 1) * P], ACT.Copy)
                    ins.then_inc(turned_out, batch.one())

            def ln_roots(stage):
                for t in range(NTILE):
                    n = TILES[t][1]
                    act.wait_ge(ln_var, stage * NTILE + t + 1)
                    act.activation(ln_sd[0:n, t, 0:1], ln_mv[0:n, t, 1:2], ACT.Sqrt, bias=eps_ln[0:n, 0:1]).then_inc(ln_root, 1)
                    if stage < 3 and t >= 1:
                        take_x(t - 1)
                if stage < 3:
                    take_x(NTILE - 1)

            def ffn(l):
                for v in range(2):
                    take(feat[:, v, :, :].rearrange("p j r -> p (j r)"), lambda b: b[:, 0:NJ * SIDE])
                act.wait_ge(turned_out, batch.n)

                act.wait_ge(pads_zero, l + 1)

                def copy_up(j, u, first):
                    if not first:
                        act.wait_ge(conv_step, j * 13 + (l * NJ * 13 - 13))
                        act.wait_ge(tail_ready, j + (l * NJ - 1))
                    act.activation(fj[:, u, :, :], feat[:, :, bass.ds(j, 1), :].rearrange("p v o r -> p v (o r)"), ACT.Copy)
                    for v in range(2):
                        act.activation(ext_s[:, u, v, :, 0:2], feat[:, v, bass.ds(j, 1), 0:2 * SEQS].rearrange("p o (s r) -> p s (o r)", r=2), ACT.Copy)
                    act.wait_ge(up_filled, j + (l * NJ + 1))
                    for v in (1, 0):
                        act.activation(ext[:, u, v, 2:514], ps[:, 2 * v + u, :], ACT.Copy)
                        ins = act.activation(ext_s[:, u, v, :, 2:10], ps[:, (4, 7)[u], v * NS:v * NS + NS].rearrange("p (s t) -> p s t", s=SEQS), ACT.Copy)
                    ins.then_inc(ext_ready, 1)

                def silu(j, u):
                    act.wait_ge(conv_step, j * 13 + (l * NJ * 13 + 6))
                    act.activation(conv_y[:, u, 1, :], conv_y[:, u, 1, :], ACT.Silu).then_inc(silu_done, 1)

                def take_tail(j, u):
                    act.wait_ge(tail_turned, j + (l * NJ + 1))
                    dst = side[0:TAIL, :].rearrange("r (v c) -> r v c", v=2)[:, :, bass.ds(j * P, P)]
                    act.activation(dst, ps[0:TAIL, TURN[u], 0:2 * P].rearrange("r (v c) -> r v c", v=2), ACT.Copy).then_inc(tail_out, 1)

                copy_up(0, 0, True)
                silu(0, 0)
                copy_up(1, 1, True)
                silu(1, 1)
                take_tail(0, 0)
                with act.Fori(1, NJ // 2) as i:
                    copy_up(i * 2, 0, False)
                    silu(i * 2, 0)
                    take_tail(i * 2 - 1, 1)
                    copy_up(i * 2 + 1, 1, False)
                    silu(i * 2 + 1, 1)
                    take_tail(i * 2, 0)
                take_tail(NJ - 1, 1)

            ln_roots(0)
            ffn(0)
            ln_roots(1)

            def copy_fm(i, dst, scale=1.0, func=ACT.Copy, bias=None):
                for bank, a, b in ((i % 2, 0, NP), (2 + i % 2, NP, NT)):
                    if bias is None:
                        ins = act.activation(dst[:, a:b], ps[:, bank, 0:b - a], func, scale=scale)
                    else:
                        ins = act.activation(dst[:, a:b], ps[:, bank, 0:b - a], ACT.Identity, bias=bias)
                ins.then_inc(fm_read, 1)

            for i in range(2 * GH):
                act.wait_ge(steps, steps_at("gla_q" if i < GH else "gla_k", 0, i % GH))
                copy_fm(i, (g_q if i < GH else g_k)[:, i % GH], GK ** -0.5 if i < GH else 1.0)
            act.wait_ge(low_filled, 1)
            act.activation(g_t1[0:16, 0:NP], ps[0:16, 4, :], ACT.Copy)
            act.activation(g_t1[0:16, NP:NT], ps[0:16, 7, 0:NS], ACT.Copy).then_inc(fm_read, 1)
            for h in range(GH):
                act.wait_ge(low_filled, 2 + h)
                copy_fm(h, g_b[:, h], bias=g_ba[:, h:h + 1])
            zz = g_b.rearrange("p h n -> p (h n)")
            act.wait_ge(fm_read, 3 * GH + 1)
            act.activation(g_tmp, zz, ACT.Abs).then_inc(gates, 1)
            act.wait_ge(gates, 1)
            act.activation(g_tmp, g_tmp, ACT.Exp, scale=-1.0).then_inc(gates, 1)
            act.wait_ge(gates, 2)
            act.activation(g_tmp, g_tmp, ACT.Ln, bias=1.0).then_inc(gates, 1)
            for c in range(4):
                for t in range(NTILE):
                    n = TILES[t][1]
                    act.wait_ge(steps, STEPS_BEFORE[15] + c * NTILE + t + 1)
                    dst = (g_v if c < 2 else g_r)[0:n, t, (c % 2) * HALF:(c % 2 + 1) * HALF]
                    act.activation(dst, ps[0:n, t, :], ACT.Copy if c < 2 else ACT.Silu).then_inc(tok_read, 1)
            sq = Count(sq_done)
            for h in range(GH):
                for l in range(NLEV):
                    ncol = NT if l < 3 else NP
                    act.wait_ge(lev_diff, h * (NLEV + 1) + l + 1)
                    e = lev_e[:, l % 2, 0:ncol]
                    act.activation(e, e, ACT.Exp, scale=1.0 / TAU).then_inc(lev_exp, 1)
                act.wait_ge(lev_ready, h * NLEV + NLEV - 1)
                act.activation(lev_e[:, 1, :], g_b[:, h], ACT.Exp, scale=1.0 / TAU).then_inc(lev_exp, 1)
                act.wait_ge(lev_diff, (h + 1) * (NLEV + 1))
                act.activation(lev_e[:, 0, :], lev_e[:, 0, :], ACT.Exp, scale=1.0 / TAU).then_inc(lev_exp, 1)
                if h >= 1:
                    act.wait_ge(gs_done, h * (PQ + SEQS))
                take(g_kt[:, 0:PQ, :], lambda b: b.rearrange("p (j c) -> p j c", j=4))
                take(g_kt[0:NS, PQ, :], lambda b: b[0:NS, 0:P])
                for t in range(NTILE):
                    n = TILES[t][1]
                    act.wait_ge(go_done, sq.n + 1)
                    if sq.n >= 1:
                        act.wait_ge(sq_done, sq.n)
                    act.activation(squares[0:n, :], ps[0:n, (4, 7)[sq.n % 2], 0:GV], ACT.Square,
                                   accum_out=g_ss[0:n, t, h:h + 1]).then_inc(sq_done, sq.one())
            act.wait_ge(sq_done, GH * NTILE)
            act.activation(g_rs.rearrange("p t h -> p (t h)"), g_ss.rearrange("p t h -> p (t h)"), ACT.Sqrt,
                           bias=eps_ln[:, 1:2], scale=1.0 / GV).then_inc(gates, 1)
            for t in range(NTILE):
                take_x(t)
            ln_roots(2)
            ffn(1)
            ln_roots(3)

        @block.vector
        def _(dve):
            vs = Count(vec)

            def settle():
                dve.wait_ge(vec, vs.n)

            dve.memset(eps_ln[:, 0:1], LN_EPS)
            dve.memset(eps_ln[:, 1:2], RMS_EPS).then_inc(vec, vs.one())
            dve.wait_ge(consts_loaded, 64)
            for r in range(4 * NTILE):
                c, t = divmod(r, NTILE)
                n = TILES[t][1]
                dve.wait_ge(steps, steps_at("attn_in", c, t))
                if r >= 1:
                    dve.wait_ge(roped, r)
                src = ps[0:n, t, :].rearrange("p (h a d) -> p h a d", h=8, a=2)
                a4 = rope_a[0:n, :].rearrange("p (h d) -> p h d", h=8)
                b4 = rope_b[0:n, :].rearrange("p (h a d) -> p h a d", h=8, a=2)
                dve.tensor_tensor(a4, ps[0:n, t, :].rearrange("p (h d) -> p h d", h=8),
                                  cos_t[0:n, t:t + 1, :].to_broadcast([n, 8, HD]), ALU.mult)
                for a in range(2):
                    ins = dve.tensor_tensor(b4[:, :, a, :], src[:, :, 1 - a, :],
                                            sin_t[0:n, t:t + 1, 32 * a:32 * a + 32].to_broadcast([n, 8, 32]), ALU.mult)
                ins.then_inc(qk_read, 1)
                dve.wait_ge(qk_read, r + 1)
                if r >= 3:
                    dve.wait_ge(turned, TURNS_X + r - 2)
                if r - 3 >= 2 * NTILE:
                    dve.wait_ge(k_stored[r % ROPED], K_STORES[r - 3])
                dve.tensor_tensor(roped_buf[0:n, r % 3, :], rope_a[0:n, :], rope_b[0:n, :], ALU.add).then_inc(roped, 1)

            def soft_scores(n):
                qi, h = divmod(n, 4)
                if n >= 2:
                    dve.wait_ge(pv_done, n - 1)
                else:
                    dve.wait_ge(turned, UP0)
                    for i in range(ROPED):
                        dve.wait_ge(k_stored[i], stores_[i])
                for g in range(4):
                    full = 256 if g == 1 else 512
                    width = min((qi + 1) * P, full)
                    dve.wait_ge(s_ready, 4 * n + g + 1)
                    acc = mb[:, n, 0:1] if g == 0 else mx[:, n, g:g + 1]
                    dve.tensor_tensor_reduce(s_buf[:, n % 2, score_at(qi, g):score_at(qi, g) + width], ps[:, g, 0:width],
                                             masks[:, MASK_AT[g] + full - width:MASK_AT[g] + full],
                                             1.0, LOWEST, ALU.add, ALU.max, acc).then_inc(s_read, 1)
                dve.wait_ge(s_read, 4 * n + 4)
                dve.tensor_reduce(mb[:, n, 1:2], mx[:, n, 1:4], AXX, ALU.max).then_inc(vec, vs.one())
                settle()
                dve.tensor_scalar(nm[:, n, :], mb[:, n, :], -ATT_SCALE, None, ALU.mult).then_inc(nm_ready, 1)

            def outputs(n):
                qi, h = divmod(n, 4)
                dve.wait_ge(probs, 2 * n + 2)
                dve.reciprocal(rden[:, n, :], den[:, n, :]).then_inc(vec, vs.one())
                settle()
                dve.wait_ge(pv_done, n + 1)
                if h == 0 and qi >= 1:
                    dve.wait_ge(turned, UP0 + 4 * sum(P_BATCH[:qi]) + qi)
                for merged in range(2):
                    at = merged * 256 + h * HD
                    dve.tensor_scalar(o_tok[:, at:at + HD], ps[:, (4, 7)[n % 2], merged * HD:merged * HD + HD],
                                      rden[:, n, merged:merged + 1], None, ALU.mult).then_inc(o_ready, 1)

            soft_scores(0)
            for n in range(16):
                if n + 1 < 16:
                    soft_scores(n + 1)
                outputs(n)

            for tile in range(2):
                dve.wait_ge(sc_done, 4 * tile + 4)
                dve.wait_ge(smask_loaded, 16 * (tile + 1))
                if tile == 0:
                    dve.wait_ge(pv_done, 16)
                else:
                    dve.wait_ge(turned, BATCH_BEFORE_SAMPLE + 4 * K_BATCH + SP_BATCH)
                for g in range(4):
                    a, width = GROUP_AT[g], GROUP_PAST[g] + NS
                    acc = smb[:, tile, 0:1] if g == 0 else smx[:, tile, g:g + 1]
                    dve.tensor_tensor_reduce(s_buf[:, 0, a:a + width], ps[:, g, 0:width], s_mask[:, a:a + width],
                                             1.0, LOWEST, ALU.add, ALU.max, acc).then_inc(s_read, 1)
                dve.wait_ge(s_read, 64 + 4 * (tile + 1))
                dve.tensor_reduce(smb[:, tile, 1:2], smx[:, tile, 1:4], AXX, ALU.max).then_inc(vec, vs.one())
                settle()
                dve.tensor_scalar(snm[:, tile, :], smb[:, tile, :], -ATT_SCALE, None, ALU.mult).then_inc(nm_ready, 1)
                dve.wait_ge(probs, 32 + 2 * (tile + 1))
                dve.reciprocal(srd[:, tile, :], sden[:, tile, :]).then_inc(vec, vs.one())
                settle()
                for merged, (a, b) in enumerate(((0, 320), (320, S_COLS))):
                    dve.tensor_scalar(s_buf[:, 0, a:b], s_buf[:, 0, a:b], srd[:, tile, merged:merged + 1], None,
                                      ALU.mult).then_inc(s_norm, 1)
                dve.wait_ge(spv_done, tile + 1)
                for merged in range(2):
                    for pair in range(2):
                        for b in range(2):
                            src = (ps[HD * b:HD * b + HD, 4, (2 * merged + pair) * P:(2 * merged + pair + 1) * P]
                                   .rearrange("p (s h q) -> p s h q", s=4, h=4)[:, :, 2 * pair + b, :])
                            t0 = NP + 32 * tile
                            dst = oT[HD * b:HD * b + HD, 2 * merged + pair, t0:t0 + 32].rearrange("p (s q) -> p s q", s=4)
                            ins = dve.tensor_copy(dst, src)
                ins.then_inc(soT_ready, 1)

            def residual(stage, half, t, step):
                n = TILES[t][1]
                dve.wait_ge(steps, step)
                z = x_tok[0:n, t, half * HALF:(half + 1) * HALF]
                dve.scalar_tensor_tensor(z, z, ALPHA, ps[0:n, t, :], ALU.mult, ALU.add).then_inc(z_read, 1)
                dve.wait_ge(z_read, (2 * stage + half) * NTILE + t + 1)
                dve.bn_stats(ln_stats[0:n, t, half, :], z).then_inc(vec, vs.one())

            def normalise(stage, t):
                n = TILES[t][1]
                settle()
                dve.bn_aggr(ln_mv[0:n, t, :], ln_stats[0:n, t, :, :]).then_inc(ln_var, 1)
                dve.wait_ge(ln_root, stage * NTILE + t + 1)
                dve.reciprocal(ln_sd[0:n, t, 1:2], ln_sd[0:n, t, 0:1]).then_inc(vec, vs.one())
                settle()
                x = x_tok[0:n, t, :]
                dve.tensor_scalar(x, x, ln_mv[0:n, t, 0:1], ln_sd[0:n, t, 1:2], ALU.subtract, ALU.mult).then_inc(vec, vs.one())
                settle()
                dve.tensor_tensor(x, x, gb[0:n, 0, :], ALU.mult).then_inc(vec, vs.one())
                settle()
                dve.tensor_tensor(x, x, gb[0:n, 1, :], ALU.add).then_inc(ln_done, 1)

            def residual_ln(stage, step_of):
                dve.wait_ge(gb_loaded, 32 * (stage + 1))
                for half in range(2):
                    for t in range(NTILE):
                        residual(stage, half, t, step_of(half, t))
                        if half == 1:
                            normalise(stage, t)

            def conv(j, u, l, first):
                dve.wait_ge(ext_ready, j + (l * NJ + 1))
                base = j * 13 + l * NJ * 13
                for v in (1, 0):
                    at = 0 if v else 6
                    for tap in range(3):
                        if tap:
                            dve.wait_ge(conv_step, base + (at + 2 * tap))
                        w = fj[:, u, v, 2 * SEQS + tap:2 * SEQS + tap + 1]
                        yp, ys = conv_y[:, u, v, 0:NP], conv_y[:, u, v, NP:NT].rearrange("p (s t) -> p s t", s=SEQS)
                        ep, es = ext[:, u, v, tap:tap + NP], ext_s[:, u, v, :, tap:tap + T_NEW]
                        for y, e in ((yp, ep), (ys, es)):
                            if tap == 0:
                                ins = dve.tensor_scalar(y, e, w, fj[:, u, v, SIDE - 1:SIDE], ALU.mult, ALU.add)
                            else:
                                ins = dve.scalar_tensor_tensor(y, e, w, y, ALU.mult, ALU.add)
                            ins.then_inc(conv_step, 1)
                if not first:
                    dve.wait_ge(tail_turned, j + (l * NJ - 1))
                for v in range(2):
                    dve.tensor_copy(tl[:, u, v, 0:2], ext[:, u, v, 512:514])
                    ins = dve.tensor_copy(tl[:, u, v, 2:TAIL].rearrange("p (s r) -> p s r", r=2), ext_s[:, u, v, :, 8:10])
                ins.then_inc(tail_ready, 1)
                dve.wait_ge(conv_step, base + 12)
                dve.wait_ge(silu_done, j + (l * NJ + 1))
                dve.tensor_tensor(hT[:, bass.ds(j, 1), :].rearrange("p o n -> p (o n)"), conv_y[:, u, 0, :],
                                  conv_y[:, u, 1, :], ALU.mult).then_inc(conv_step, 1)

            def ffn(l):
                conv(0, 0, l, True)
                conv(1, 1, l, True)
                with dve.Fori(1, NJ // 2) as i:
                    conv(i * 2, 0, l, False)
                    conv(i * 2 + 1, 1, l, False)

            dve.wait_ge(x_again, 32)
            residual_ln(0, lambda half, t: steps_at("attn_out", 0, half * NTILE + t))
            dve.wait_ge(v_stored, V_STORES)
            ffn(0)
            residual_ln(1, lambda half, t: steps_at("down0", 3 * half + 2, t))

            dve.wait_ge(gates, 3)
            zz = g_b.rearrange("p h n -> p (h n)")
            dve.scalar_tensor_tensor(zz, zz, 0.0, g_tmp, ALU.min, ALU.subtract).then_inc(vec, vs.one())
            settle()
            dve.wait_ge(gla_loaded, 112)
            for h in range(GH):
                dve.tensor_tensor_scan(g_b[:, h], g_reset, g_b[:, h], 0.0, ALU.mult, ALU.add).then_inc(vec, vs.one())
            settle()
            dve.tensor_copy(g_mask, mask_words).then_inc(vec, vs.one())
            settle()
            for z in (lev_q, lev_k, att, g_qz, g_ss):
                dve.memset(z, 0.0).then_inc(vec, vs.one())
            settle()

            def blocks(x, ncol, half):
                return x[:, 0:ncol].rearrange("p (n a c) -> p n a c", a=2, c=half)

            def differences(h, l):
                half = 1 << l
                ncol = NT if l < 3 else NP
                if l >= 2:
                    dve.wait_ge(lev_ready, h * NLEV + l - 1)
                elif h:
                    dve.wait_ge(kz_ready, 3 * h)
                    dve.wait_ge(gs_read, h * (PQ + SEQS))
                b, d = blocks(g_b[:, h], ncol, half), blocks(lev_e[:, l % 2], ncol, half)
                ref = b[:, :, 0, half - 1:half].to_broadcast([P, ncol // (2 * half), half])
                dve.tensor_tensor(d[:, :, 1, :], b[:, :, 1, :], ref, ALU.subtract)
                dve.tensor_tensor(d[:, :, 0, :], ref, b[:, :, 0, :], ALU.subtract).then_inc(lev_diff, 1)

            def decayed(h, l):
                half = 1 << l
                ncol = NT if l < 3 else NP
                dve.wait_ge(lev_exp, h * (NLEV + 2) + l + 1)
                if l >= 2:
                    dve.wait_ge(lev_prod, h * LEV_ALL + LEV_BEFORE[l - 1])
                elif h:
                    dve.wait_ge(lev_prod, h * LEV_ALL)
                e = blocks(lev_e[:, l % 2], ncol, half)
                q, k = blocks(g_q[:, h], ncol, half), blocks(g_k[:, h], ncol, half)
                dve.tensor_tensor(blocks(lev_q[:, l % 2], ncol, half)[:, :, 1, :], q[:, :, 1, :], e[:, :, 1, :], ALU.mult)
                dve.tensor_tensor(blocks(lev_k[:, l % 2], ncol, half)[:, :, 0, :], k[:, :, 0, :], e[:, :, 0, :],
                                  ALU.mult).then_inc(lev_ready, 1)

            def placed(h, l):
                n = h * LEV_ALL + LEV_BEFORE[l]
                if l == 0 and h >= 2:
                    dve.wait_ge(go_done, (h - 1) * NTILE)
                dve.wait_ge(lev_prod, n + 1)
                if n:
                    dve.wait_ge(lev_read, n)
                a = att[:, h % 2]
                m = g_mask[:, l:l + 1, :].to_broadcast([P, PQ, P])
                dve.copy_predicated(a[:, 0:NP].rearrange("p (c n) -> p c n", c=PQ), m,
                                    ps[:, l % 2, :].rearrange("p (c n) -> p c n", c=PQ)).then_inc(lev_read, 1)
                if LEV_WITH_SAMPLE[l]:
                    dve.wait_ge(lev_prod, n + 2)
                    dve.copy_predicated(a[0:NS, NP:NT], g_mask[0:NS, l, 0:NS], ps[0:NS, 2, 0:NS]).then_inc(lev_read, 1)

            for h in range(GH):
                differences(h, 0)
                differences(h, 1)
                for l in range(NLEV):
                    decayed(h, l)
                    if l >= 1:
                        placed(h, l - 1)
                    if l + 2 < NLEV:
                        dve.wait_ge(lev_ready, h * NLEV + l + 1)
                        differences(h, l + 2)
                placed(h, NLEV - 1)
                placed(h, NLEV)
                dve.wait_ge(lev_ready, (h + 1) * NLEV)
                dve.wait_ge(lev_exp, h * (NLEV + 2) + NLEV + 1)
                if h:
                    dve.wait_ge(go_done, h * NTILE)
                    dve.wait_ge(turned, BATCH_GLA + 2 * h)
                e0 = lev_e[:, 1]
                dve.tensor_tensor(g_qb, g_q[:, h], e0, ALU.mult).then_inc(vec, vs.one())
                e1 = lev_e[:, 0]
                for a, b, n, c in ((0, NP, PQ, P), (NP, NT, SEQS, T_NEW)):
                    bb = g_b[:, h, a:b].rearrange("p (n c) -> p n c", n=n)
                    ins = dve.tensor_tensor(e1[:, a:b].rearrange("p (n c) -> p n c", n=n),
                                            bb[:, :, c - 1:c].to_broadcast([P, n, c]), bb, ALU.subtract)
                ins.then_inc(lev_diff, 1)
                dve.wait_ge(lev_exp, (h + 1) * (NLEV + 2))
                dve.tensor_tensor(g_kb, g_k[:, h], e1, ALU.mult).then_inc(kz_ready, 1)
                settle()
                if h:
                    dve.wait_ge(gs_done, h * (PQ + SEQS))
                dve.tensor_copy(g_qz_own, g_qb[:, NP:NT].rearrange("p (s t) -> p s t", s=SEQS)).then_inc(kz_ready, 1)
                dve.wait_ge(turned_out, BATCH_GLA + 2 * h + 2)
                dve.tensor_tensor(g_kz[0:NS, :, :], g_kt[0:NS, PQ:PQ + 1, :].to_broadcast([NS, SEQS, P]),
                                  seq_of_row.rearrange("p (s o) -> p s o", o=1).to_broadcast([NS, SEQS, P]), ALU.mult).then_inc(kz_ready, 1)
                if h == 0:
                    dve.wait_ge(r_scaled, NTILE)

                def gate_out(t):
                    n = h * NTILE + t
                    rows = TILES[t][1]
                    dve.wait_ge(sq_done, n + 1)
                    r = g_r[0:rows, t, h * GV:(h + 1) * GV]
                    dve.tensor_tensor(r, ps[0:rows, (4, 7)[n % 2], 0:GV], r, ALU.mult).then_inc(go_read, 1)

                for c in range(PQ):
                    n = h * (PQ + SEQS) + c
                    dve.wait_ge(gs_done, n + 1)
                    if c == 0:
                        if h:
                            dve.wait_ge(gla_state_out, 32 * h)
                        dve.tensor_copy(g_state, ps[:, 3, 0:GV]).then_inc(gs_read, 1)
                    else:
                        dve.wait_ge(go_done, h * NTILE + c + 1)
                        dve.wait_ge(gs_read, n)
                        dve.scalar_tensor_tensor(g_state, g_state, e0[:, c * P + P - 1:c * P + P], ps[:, 3, 0:GV],
                                                 ALU.mult, ALU.add).then_inc(gs_read, 1)
                    gate_out(c)
                dve.wait_ge(go_done, (h + 1) * NTILE)
                gate_out(PQ)
                for s in range(SEQS):
                    n = h * (PQ + SEQS) + PQ + s
                    dve.wait_ge(gs_done, n + 1)
                    col = NP + s * T_NEW + T_NEW - 1
                    dve.scalar_tensor_tensor(g_sst[:, s, :], g_sst[:, s, :], e0[:, col:col + 1], ps[:, 3, 0:GV],
                                             ALU.mult, ALU.add).then_inc(gs_read, 1)
            dve.wait_ge(gates, 4)
            dve.reciprocal(g_rs, g_rs).then_inc(vec, vs.one())
            settle()
            dve.wait_ge(go_read, GH * NTILE)
            for t in range(NTILE):
                n = TILES[t][1]
                r = g_r[0:n, t, :].rearrange("p (h c) -> p h c", h=GH)
                dve.tensor_tensor(r, r, g_rs[0:n, t, :].rearrange("p (h o) -> p h o", o=1).to_broadcast([n, GH, GV]),
                                  ALU.mult).then_inc(y_ready, 1)
            residual_ln(2, lambda half, t: steps_at("gla_out", half, t))
            ffn(1)
            residual_ln(3, lambda half, t: steps_at("down1", 3 * half + 2, t))

        @block.gpsimd
        def _(pool):
            pool.dma_start(ident[:, :], io["ident"]).then_inc(consts_loaded, 16)
            pool.wait_ge(consts_loaded, 16)
            pool.dma_start(cos_t, io["rope_cos"]).then_inc(consts_loaded, 16)
            pool.dma_start(sin_t, io["rope_sin"]).then_inc(consts_loaded, 16)
            pool.dma_start(masks, io["prompt_masks"]).then_inc(consts_loaded, 16)
            pool.memset(gb_reg[:, :], 0.0).then_inc(qz_zero, 1)

            new_rows = {0: ("moba", None), 1: ("swa0", 120), 2: ("swa1", 248), 3: ("swa2", 248)}

            def store_piece(src, t, g, a, done):
                if not pieces_of(t, g):
                    return
                name, at = new_rows[g]
                if t < PQ:
                    r0 = 0 if g == 1 else t * P
                    dst = io[f"{name}_p"][0, 0, r0:r0 + P, a].rearrange("r h d -> r (h d)")
                elif g == 0:
                    dst = io["moba_s"][0, :, :, a].rearrange("s r h d -> s r (h d)")
                else:
                    dst = io[f"{name}_s"][0, :, at:at + T_NEW, a].rearrange("s r h d -> s r (h d)")
                pool.dma_start(dst, src).then_inc(done, 16)

            for r in range(2 * NTILE, 4 * NTILE):
                c, t = divmod(r, NTILE)
                n = TILES[t][1]
                pool.wait_ge(roped, r + 1)
                for half in range(2):
                    store_piece(roped_buf[0:n, r % 3, half * 256:half * 256 + 256], t, 2 * (c - 2) + half, 0, k_stored[r % ROPED])
            pool.wait_ge(qz_zero, 1)
            pool.wait_ge(turned_out, UP0)
            for c in range(8):
                for b in range(2):
                    src = qkT[HD * b:HD * b + HD, c, NP:NT].rearrange("p (s q) -> p s q", s=SEQS)
                    ins = pool.tensor_copy(qz[HD * b:HD * b + HD, c, :, 2 * (c % 2) + b, :], src)
            ins.then_inc(qz_ready, 1)
            pool.wait_ge(v_read, 2 * NTILE)
            for t in range(NTILE):
                n = TILES[t][1]
                for g in range(4):
                    store_piece(v_tok[0:n, t, g * 256:(g + 1) * 256], t, g, 1, v_stored)

            def ffn(l):
                pool.memset(ext[:, :, :, 0:2], 0.0).then_inc(pads_zero, 1)

                pool.wait_ge(tail_out, (l + 1) * NJ)
                pool.dma_start(io["ffn_p"][l, 0], side[0:2, :]).then_inc(tail_stored, 16)
                pool.dma_start(io["ffn_s"][l].rearrange("s r c -> (s r) c"), side[2:TAIL, :]).then_inc(tail_stored, 16)

            pool.wait_ge(soT_ready, 2)
            ffn(0)
            pool.wait_ge(gla_loaded, 112)
            for t in range(NTILE):
                n = TILES[t][1]
                pool.wait_ge(tok_read, 3 * NTILE + t + 1)
                r = g_r[0:n, t, :].rearrange("p (h c) -> p h c", h=GH)
                pool.tensor_tensor(r, r, g_norm[0:n, :].rearrange("p (o c) -> p o c", o=1).to_broadcast([n, GH, GV]),
                                   ALU.mult).then_inc(r_scaled, 1)
            for h in range(GH):
                pool.wait_ge(gs_read, h * (PQ + SEQS) + PQ)
                pool.dma_start(io["gla_p"][0, 0, h], g_state).then_inc(gla_state_out, 16)
                pool.wait_ge(gs_read, (h + 1) * (PQ + SEQS))
                pool.dma_start(io["gla_s"][0, :, h].rearrange("s d v -> d s v"), g_sst).then_inc(gla_state_out, 16)
            pool.wait_ge(go_read, GH * NTILE)
            pool.wait_ge(gla_state_out, 32 * GH)
            ffn(1)
            for t in range(NTILE):
                n = TILES[t][1]
                pool.wait_ge(ln_done, 3 * NTILE + t + 1)
                dst = (io["y_prompt"][0, t * P:(t + 1) * P, :] if t < PQ
                       else io["y_sample"].rearrange("s t c -> (s t) c"))
                pool.dma_start(dst, x_tok[0:n, t, :]).then_inc(y_stored, 16)
            pool.wait_ge(y_stored, 16 * NTILE)
            pool.wait_ge(tail_stored, 64)
            pool.wait_ge(gla_state_out, 32 * GH)
            for i in range(ROPED):
                pool.wait_ge(k_stored[i], stores_[i])
            pool.wait_ge(v_stored, V_STORES)
            pool.wait_ge(kv_stored, 48)


_INS = ["x_prompt", "x_sample", "cache_moba_kv", "state_swa0_kv", "state_swa1_kv", "state_swa2_kv", "state_gla",
        "state_ffn_conv", "page_table", "attn_w_in", "attn_w_out", "gla_w_in", "gla_w_a1", "gla_w_a2", "gla_b_a",
        "gla_norm_g", "gla_w_out", "ln_mix_g", "ln_mix_b", "ffn_w_up", "ffn_conv_w", "ffn_conv_b", "ffn_w_down",
        "ln_ffn_g", "ln_ffn_b"]
_OUTS = [("y_prompt", (1, 512, 1024)), ("y_sample", (8, 8, 1024)),
         ("moba_p", (1, 1, 512, 2, 4, 64)), ("moba_s", (1, 8, 8, 2, 4, 64)),
         ("swa0_p", (1, 1, 128, 2, 4, 64)), ("swa0_s", (1, 8, 128, 2, 4, 64)),
         ("swa1_p", (1, 1, 512, 2, 4, 64)), ("swa1_s", (1, 8, 256, 2, 4, 64)),
         ("swa2_p", (1, 1, 512, 2, 4, 64)), ("swa2_s", (1, 8, 256, 2, 4, 64)),
         ("gla_p", (1, 1, 4, 128, 256)), ("gla_s", (1, 8, 4, 128, 256)),
         ("ffn_p", (2, 1, 2, 5632)), ("ffn_s", (2, 8, 2, 5632))]


def shape_constants():
    import numpy as np

    past_len, theta, off = 256, 10000.0, -1.0e30
    half = HD // 2
    inv = np.float32(theta) ** (-np.arange(half, dtype=np.float32) / np.float32(half))
    cos, sin = np.zeros((P, NTILE, HD), np.float32), np.zeros((P, NTILE, HD), np.float32)
    for t, (first, n) in enumerate(TILES):
        pos = (first + np.arange(n)) if t < PQ else past_len + np.arange(n) % T_NEW
        ang = pos.astype(np.float32)[:, None] * inv[None, :]
        cos[:n, t] = np.concatenate([np.cos(ang), np.cos(ang)], 1)
        sin[:n, t] = np.concatenate([-np.sin(ang), np.sin(ang)], 1)

    i, past = np.arange(P)[:, None], np.arange(-3 * P, P)[None, :]
    causal = past <= i
    window = (past <= i) & (i - past <= 128)
    groups = [causal, window[:, 2 * P:], causal & ((i - past) % 4 == 0), causal & ((i - past) % 16 == 0)]
    prompt = np.where(np.concatenate(groups, 1), 0.0, off).astype(np.float32)

    sample = np.zeros((P, 2, S_COLS), np.float32)
    row = np.arange(P)
    s4, q = row // 32, row % T_NEW
    tok = np.arange(NS)
    for g in range(4):
        n = GROUP_PAST[g]
        dil = (1, 1, 4, 16)[g]
        back = n + q[:, None] - np.arange(n)[None, :]
        seen = (back % dil == 0) & ((back <= 128 * dil) | (g == 0))
        for tile in range(2):
            same = (tok // T_NEW)[None, :] == (4 * tile + s4)[:, None]
            ago = q[:, None] - (tok % T_NEW)[None, :]
            new = same & (ago >= 0) & (ago % dil == 0)
            sample[:, tile, GROUP_AT[g]:GROUP_AT[g] + n + NS] = np.where(np.concatenate([seen, new], 1), 0.0, off)

    level = np.zeros((P, NLEV + 1, P), np.int32)
    s, t = np.arange(P)[:, None], np.arange(P)[None, :]
    for l in range(NLEV):
        h = 1 << l
        level[:, l] = (s // (2 * h) == t // (2 * h)) & (s // h % 2 == 0) & (t // h % 2 == 1)
    level[:, NLEV] = s == t
    reset = np.ones((P, NT), np.float32)
    reset[:, 0:NP:P] = 0.0
    reset[:, NP:NT:T_NEW] = 0.0
    seq_of_row = (np.arange(NS)[:, None] // T_NEW == np.arange(SEQS)[None, :]).astype(np.float32)
    return {"ident": np.eye(P, dtype=np.float32), "rope_cos": cos, "rope_sin": sin, "prompt_masks": prompt,
            "sample_masks": sample, "level_masks": level, "scan_reset": reset, "seq_of_row": seq_of_row}


def kernel(**inputs):
    import numpy as np
    import concourse.bacc as bacc
    from concourse.bass_utils import run_bass_kernel_spmd

    nc = bacc.Bacc("TRN2", target_bir_lowering=False, num_devices=1)
    arrays, io = {}, {}
    given = {name: np.ascontiguousarray(inputs[name]) for name in _INS}
    for name, a in list(given.items()) + list(shape_constants().items()):
        arrays[f"in_{name}"] = a
        io[name] = nc.dram_tensor(f"in_{name}", a.shape, mybir.dt.from_np(a.dtype), kind="ExternalInput").ap()
    for name, shape in _OUTS:
        io[name] = nc.dram_tensor(f"out_{name}", shape, F32, kind="ExternalOutput").ap()
    build_program(nc, io)
    r = run_bass_kernel_spmd(nc, [arrays], core_ids=[0])
    return tuple(r.results[0][f"out_{name}"] for name, _ in _OUTS)
```

```python
from contextlib import ExitStack

import concourse.bass as bass
from concourse import mybir

F32 = mybir.dt.float32
F32R = mybir.dt.float32r
I32 = mybir.dt.int32
U8 = mybir.dt.uint8
ALU = mybir.AluOpType
ACT = mybir.ActivationFunctionType
AXX = mybir.AxisListType.X

P = 128
D = 1024
KD = D // P
NP = 512
SEQS, T_NEW = 8, 8
NS = SEQS * T_NEW
NT = NP + NS
TILES = [(0, P), (P, P), (2 * P, P), (3 * P, P), (NP, NS)]
NTILE = len(TILES)
PQ = NP // P
HALF = 512
SPLIT = NT // 2
PRE = NP - SPLIT
HD = 64
PAGE = 128
DFF = 2816
NJ = DFF // P
DOWN_GROUPS = [(k0, min(4, NJ - k0)) for k0 in range(0, NJ, 4)]
SIDE = 2 * SEQS + 4
UP_RUNS = [(1, 0), (1, 1), (0, 0), (0, 1)]
TAIL = 2 + 2 * SEQS
ALPHA = (2.0 * 2) ** 0.25
LN_EPS = 1e-5
RMS_EPS = 1e-6
ATT_SCALE = HD ** -0.5
GH, GK, GV = 4, 128, 256
NLEV = 7
TAU = 16.0
LOWEST = -3.0e38

GROUP_PAST = [256, 128, 256, 256]
GROUP_AT = [0, 320, 512, 832]
S_COLS = 1152
CACHE_BLOCK = [0, 2, 3, 5]
NBLK = 7
KEY_BLOCKS = []
for g_ in range(4):
    for b_ in range(GROUP_PAST[g_] // P):
        KEY_BLOCKS.append((GROUP_AT[g_] + b_ * P, P, g_, CACHE_BLOCK[g_] + b_))
    KEY_BLOCKS.append((GROUP_AT[g_] + GROUP_PAST[g_], NS, g_, None))

UNIT = 2048
UNITS = ([("attn_in", c, NTILE) for c in range(12)] + [("attn_out", c, NTILE) for c in range(2)]
         + [("up0", j, 4) for j in range(NJ)] + [("down0", c, NTILE) for c in range(2 * len(DOWN_GROUPS))]
         + [("gla_qk", c, 4) for c in range(4)] + [("gla_a1", 0, 2)] + [("gla_vr", c, NTILE) for c in range(8)]
         + [("gla_out", c, NTILE) for c in range(4)]
         + [("up1", j, 4) for j in range(NJ)] + [("down1", c, NTILE) for c in range(2 * len(DOWN_GROUPS))])
UNIT_NO = {(k, c): n for n, (k, c, _) in enumerate(UNITS)}
STEPS_BEFORE = [sum(s for _, _, s in UNITS[:n]) for n in range(len(UNITS) + 1)]
LOADS = 2


def steps_at(kind, c, t):
    return STEPS_BEFORE[UNIT_NO[(kind, c)]] + t + 1


def unit_width(n):
    kind, c, _ = UNITS[n]
    if kind in ("down0", "down1"):
        return DOWN_GROUPS[c % len(DOWN_GROUPS)][1] * HALF
    return KD * P if kind == "gla_a1" else UNIT


LEV_WITH_SAMPLE = [l < 3 or l == NLEV for l in range(NLEV + 1)]
LEV_BEFORE = [sum(1 + w for w in LEV_WITH_SAMPLE[:l]) for l in range(NLEV + 2)]
LEV_ALL = LEV_BEFORE[-1]


def pieces_of(t, g):
    return g != 1 or t >= PQ - 1


ROPED = 3
K_STORES, stores_ = [], [0] * ROPED
for r_ in range(4 * NTILE):
    c_, t_ = divmod(r_, NTILE)
    stores_[r_ % ROPED] += 16 * sum(pieces_of(t_, 2 * (c_ - 2) + half_) for half_ in range(2)) if c_ >= 2 else 0
    K_STORES.append(stores_[r_ % ROPED])
V_STORES = 16 * sum(pieces_of(t_, g_) for t_ in range(NTILE) for g_ in range(4))


class Count:

    def __init__(self, sem):
        self.sem, self.n = sem, 0

    def one(self):
        self.n += 1
        return 1


def build_program(nc, io):
    with ExitStack() as ctx:
        def sb(name, shape, dt=F32):
            return ctx.enter_context(nc.sbuf_tensor(name, shape, dt))

        def sem(name):
            return ctx.enter_context(nc.semaphore(name))

        SBUF_FIRST = 16512

        def at_place(name, shape, first, dt=F32):
            return nc.alloc_sbuf_tensor_at(name, shape, dt, offset=SBUF_FIRST + 4 * first)

        SLOT = NT + NS
        x_reg = at_place("x_reg", [P, NTILE * D], 0)
        xh_reg = at_place("xh_reg", [P, KD * SLOT], 5120, F32R)
        xl_reg = at_place("xl_reg", [P, KD * SLOT], 10240, F32R)
        raw = at_place("raw", [P, 2, UNIT], 15360)
        w_hi = at_place("w_hi", [P, 2, UNIT], 19456, F32R)
        w_lo = at_place("w_lo", [P, 2, UNIT], 23552, F32R)
        ident = at_place("ident", [P, P], 27648)
        ln_stats = at_place("ln_stats", [P, NTILE, 2, 6], 27776)
        ln_mv = at_place("ln_mv", [P, NTILE, 2], 27840)
        ln_sd = at_place("ln_sd", [P, NTILE, 2], 27856)
        eps_ln = at_place("eps_ln", [P, 2], 27872)
        page_ids = at_place("page_ids", [1, 16], 27880, I32)
        arena = at_place("arena", [P, 24016], 27904)
        attn_side = at_place("attn_side", [P, 4 * SLOT], 5120 + 4 * SLOT)
        gla_side = at_place("gla_side", [P, 2 * KD * SLOT], 5120)
        v_cache_reg = at_place("v_cache_reg", [P, 4 * NBLK * 256], 19456)
        ps = ctx.enter_context(nc.psum_tensor("ps", [P, 8, HALF], F32))
        TURN = (5, 6)

        x_tok = x_reg[:, :].rearrange("p (t c) -> p t c", t=NTILE)
        xTh = xh_reg[:, :].rearrange("p (k n) -> p k n", k=KD)
        xTl = xl_reg[:, :].rearrange("p (k n) -> p k n", k=KD)

        def cut(region, at, n):
            return region[:, at:at + n]

        gb = cut(arena, 21560, 2 * D).rearrange("p (a c) -> p a c", a=2)

        v_tok = cut(arena, 0, 5120).rearrange("p (t c) -> p t c", t=NTILE)
        qkT = cut(arena, 5120, 16 * NT).rearrange("p (c n) -> p c n", c=16)
        v_cache = v_cache_reg[:, :].rearrange("p (s b c) -> p s b c", s=4, b=NBLK)
        masks = cut(arena, 14336, 1792)
        MASK_AT = [0, 512, 768, 1280]
        s_buf = cut(arena, 16128, 3584).rearrange("p (b c) -> p b c", b=2)

        def score_at(qi, g):
            width = (qi + 1) * P
            return [0, 512, 512 + min(width, 256), 512 + min(width, 256) + width][g]

        small = cut(arena, 19712, 216)
        mx = small[:, 0:64].rearrange("p (n g) -> p n g", g=4)
        mb = small[:, 64:96].rearrange("p (n g) -> p n g", g=2)
        nm = small[:, 96:128].rearrange("p (n g) -> p n g", g=2)
        den = small[:, 128:160].rearrange("p (n g) -> p n g", g=2)
        rden = small[:, 160:192].rearrange("p (n g) -> p n g", g=2)
        smx = small[:, 192:200].rearrange("p (n g) -> p n g", g=4)
        smb = small[:, 200:204].rearrange("p (n g) -> p n g", g=2)
        snm = small[:, 204:208].rearrange("p (n g) -> p n g", g=2)
        sden = small[:, 208:212].rearrange("p (n g) -> p n g", g=2)
        srd = small[:, 212:216].rearrange("p (n g) -> p n g", g=2)
        rope_a = cut(arena, 16128, 512)
        rope_b = cut(arena, 16640, 512)
        roped_buf = cut(arena, 17152, 1536).rearrange("p (b c) -> p b c", b=3)
        cos_t = cut(arena, 18688, 320).rearrange("p (t c) -> p t c", t=NTILE)
        sin_t = cut(arena, 19008, 320).rearrange("p (t c) -> p t c", t=NTILE)
        k_stage = cut(x_reg, 0, NBLK * 256).rearrange("p (b c) -> p b c", b=NBLK)
        pT = cut(x_reg, 1792, 14 * P).rearrange("p (b c) -> p b c", b=14)
        s_mask = cut(x_reg, 3584, S_COLS)
        kcT = cut(attn_side, 0, 14 * P).rearrange("p (a c) -> p a c", a=14)
        o_tok = cut(attn_side, 14 * P, 512)
        qz_reg = cut(arena, 19968, 2048)
        qz = qz_reg.rearrange("p (c s h q) -> p c s h q", c=8, s=SEQS, h=4)

        hT = cut(arena, 0, NJ * NT).rearrange("p (j n) -> p j n", j=NJ)
        side = cut(arena, 12672, 2 * DFF)
        feat = cut(arena, 18304, 2 * NJ * SIDE).rearrange("p (v j r) -> p v j r", v=2, j=NJ)
        ext = cut(arena, 19184, 4 * 514).rearrange("p (u v n) -> p u v n", u=2, v=2)
        ext_s = cut(arena, 21240, 320).rearrange("p (u v s n) -> p u v s n", u=2, v=2, s=SEQS)
        conv_y = cut(arena, 21560, 4 * NT).rearrange("p (u v n) -> p u v n", u=2, v=2)
        fj = cut(arena, 23864, 2 * 2 * SIDE).rearrange("p (u v r) -> p u v r", u=2, v=2)
        tl = cut(arena, 23944, 4 * TAIL).rearrange("p (u v r) -> p u v r", u=2, v=2)

        g_v = cut(arena, 0, 5120).rearrange("p (t c) -> p t c", t=NTILE)
        g_r = cut(arena, 5120, 5120).rearrange("p (t c) -> p t c", t=NTILE)
        g_q = cut(arena, 10240, GH * NT).rearrange("p (h n) -> p h n", h=GH)
        g_k = cut(arena, 12544, GH * NT).rearrange("p (h n) -> p h n", h=GH)
        g_b = cut(arena, 14848, GH * NT).rearrange("p (h n) -> p h n", h=GH)
        g_tmp = cut(arena, 21560, GH * NT)
        lev_e = cut(arena, 17152, 2 * NT).rearrange("p (b n) -> p b n", b=2)
        att = cut(arena, 18304, 2 * NT).rearrange("p (b n) -> p b n", b=2)
        lev_q = cut(arena, 21560, 2 * NT).rearrange("p (b n) -> p b n", b=2)
        lev_k = cut(arena, 22712, 2 * NT).rearrange("p (b n) -> p b n", b=2)
        g_mask = cut(arena, 19456, (NLEV + 1) * P // 4).bitcast(U8).rearrange("p (l c) -> p l c", l=NLEV + 1)
        mask_words = cut(arena, 17152, (NLEV + 1) * P).bitcast(I32).rearrange("p (l c) -> p l c", l=NLEV + 1)
        g_small = cut(arena, 19712, 64)
        g_ss = g_small[:, 0:20].rearrange("p (t h) -> p t h", t=NTILE)
        g_rs = g_small[:, 20:40].rearrange("p (t h) -> p t h", t=NTILE)
        g_ba = g_small[:, 40:44]
        g_norm = cut(arena, 19776, GV)
        seq_of_row = cut(arena, 20032, SEQS)[0:NS, :]
        g_reset = cut(arena, 20064, NT)
        g_a2 = cut(arena, 20640, 512)
        g_t1 = cut(arena, 18304, NT)
        g_qb = cut(gla_side, 0, NT)
        g_kb = cut(gla_side, 576, NT)
        g_kt = cut(gla_side, 1152, NTILE * P).rearrange("p (t c) -> p t c", t=NTILE)
        g_qz = cut(gla_side, 1792, SEQS * NS).rearrange("p (s n) -> p s n", s=SEQS)
        g_qz_own = cut(gla_side, 1792, SEQS * (NS + T_NEW)).rearrange("p (s n) -> p s n", s=SEQS)[:, :, 0:T_NEW]
        g_kz = cut(gla_side, 2368, SEQS * P).rearrange("p (s n) -> p s n", s=SEQS)
        g_state = cut(gla_side, 3392, GV)
        g_sst = cut(gla_side, 3648, SEQS * GV).rearrange("p (s n) -> p s n", s=SEQS)
        squares = cut(gla_side, 5696, GV)

        x_loaded = sem("x_loaded")
        consts_loaded = sem("consts_loaded")
        pages_loaded = sem("pages_loaded")
        raw_loaded = [sem(f"raw_loaded{i}") for i in range(2)]
        hi_done = sem("hi_done")
        lo_done = sem("lo_done")
        h_hi = sem("h_hi")
        h_lo = sem("h_lo")
        x_lo = sem("x_lo")
        pad_zero = sem("pad_zero")
        steps = sem("steps")
        turned = sem("turned")
        turned_out = sem("turned_out")
        vec = sem("vec")
        qk_read = sem("qk_read")
        roped = sem("roped")
        v_stored = sem("v_stored")
        qz_zero = sem("qz_zero")
        v_read = sem("v_read")
        k_stored = [sem(f"k_stored{i}") for i in range(ROPED)]
        kv_stored = sem("kv_stored")
        s_ready = sem("s_ready")
        s_read = sem("s_read")
        nm_ready = sem("nm_ready")
        probs = sem("probs")
        pv_done = sem("pv_done")
        o_ready = sem("o_ready")
        qz_ready = sem("qz_ready")
        k_cached = sem("k_cached")
        v_cached = sem("v_cached")
        smask_loaded = sem("smask_loaded")
        sc_done = sem("sc_done")
        s_norm = sem("s_norm")
        spv_done = sem("spv_done")
        soT_ready = sem("soT_ready")
        x_again = sem("x_again")
        gb_loaded = sem("gb_loaded")
        z_read = sem("z_read")
        ln_var = sem("ln_var")
        ln_root = sem("ln_root")
        ln_done = sem("ln_done")
        side_loaded = sem("side_loaded")
        pads_zero = sem("pads_zero")
        ext_ready = sem("ext_ready")
        conv_step = sem("conv_step")
        silu_done = sem("silu_done")
        tail_ready = sem("tail_ready")
        tail_turned = sem("tail_turned")
        tail_out = sem("tail_out")
        tail_stored = sem("tail_stored")
        gla_loaded = sem("gla_loaded")
        gla_state_in = sem("gla_state_in")
        gla_state_out = sem("gla_state_out")
        fm_read = sem("fm_read")
        low_filled = sem("low_filled")
        gates = sem("gates")
        tok_read = sem("tok_read")
        r_scaled = sem("r_scaled")
        lev_diff = sem("lev_diff")
        lev_exp = sem("lev_exp")
        lev_ready = sem("lev_ready")
        lev_prod = sem("lev_prod")
        lev_read = sem("lev_read")
        kz_ready = sem("kz_ready")
        go_done = sem("go_done")
        gs_done = sem("gs_done")
        sq_done = sem("sq_done")
        go_read = sem("go_read")
        gs_read = sem("gs_read")
        y_ready = sem("y_ready")
        y_stored = sem("y_stored")

        TURNS_X = 2 * NTILE
        TURNS_QK = 4 * NTILE
        P_BLOCKS = [(qi + 1) + min(qi + 1, 2) + 2 * (qi + 1) for qi in range(PQ)]
        P_BATCH = [-(-b // 4) for b in P_BLOCKS]
        UP0 = TURNS_X + TURNS_QK
        K_BATCH = 4
        SP_BATCH = -(-len(KEY_BLOCKS) // 4)
        BATCH_BEFORE_SAMPLE = UP0 + 4 * sum(P_BATCH) + PQ
        BATCH_LN0 = BATCH_BEFORE_SAMPLE + 2 * (4 * K_BATCH + SP_BATCH)
        BATCH_LN1 = BATCH_LN0 + TURNS_X + 2
        BATCH_GLA = BATCH_LN1 + TURNS_X
        BATCH_Y = BATCH_GLA + 2 * GH
        BATCH_LN2 = BATCH_Y + TURNS_X
        BATCH_O = [UP0 + 4 * sum(P_BATCH[:qi + 1]) + qi for qi in range(PQ)]
        LO_BATCHES = ([b for b in range(TURNS_X)] + BATCH_O
                      + [b0 + b for b0 in (BATCH_LN0, BATCH_LN1, BATCH_Y, BATCH_LN2) for b in range(TURNS_X)])

        block = ctx.enter_context(nc.Block())

        def unit_source(n):
            kind, c, _ = UNITS[n]
            if kind in ("attn_in", "gla_vr", "gla_out"):
                w = {"attn_in": io["attn_w_in"], "gla_vr": io["gla_w_in"], "gla_out": io["gla_w_out"]}[kind][0]
                k0, kn, c0, cn = c % 2 * 4, 4, (c // 2 + (2 if kind == "gla_vr" else 0)) * HALF, HALF
            elif kind == "attn_out":
                w, k0, kn, c0, cn = io["attn_w_out"][0], 0, 4, c * HALF, HALF
            elif kind in ("down0", "down1"):
                w = io["ffn_w_down"][int(kind[-1])]
                (k0, kn), c0, cn = DOWN_GROUPS[c % len(DOWN_GROUPS)], c // len(DOWN_GROUPS) * HALF, HALF
            elif kind == "gla_qk":
                w, k0, kn, c0, cn = io["gla_w_in"][0], 0, KD, c * 2 * P, 2 * P
            else:
                w, k0, kn, c0, cn = io["gla_w_a1"][0], 0, KD, 0, 16
            src = w[k0 * P:(k0 + kn) * P, c0:c0 + cn].rearrange("(k p) c -> p k c", p=P)
            dst = raw[:, n % 2, 0:unit_width(n)].rearrange("p (k c) -> p k c", k=kn)[:, :, 0:cn]
            return [(dst[:, a:a + kn // 2, :], src[:, a:a + kn // 2, :]) for a in (0, kn // 2)]

        def of_unit(w, n, kn):
            return w[:, n % 2, 0:unit_width(n)].rearrange("p (k c) -> p k c", k=kn)

        @block.sync
        def _(sp):
            def load_unit(n):
                if n >= 2:
                    sp.wait_ge(lo_done, n - 1)
                for dst, src in unit_source(n):
                    sp.dma_start(dst, src).then_inc(raw_loaded[n % 2], 16)

            sp.dma_start(x_tok[:, 0:PQ, :], io["x_prompt"][0].rearrange("(t p) c -> p t c", p=P)).then_inc(x_loaded, 16)
            sp.dma_start(x_tok[0:NS, PQ, :], io["x_sample"].rearrange("s t c -> (s t) c")).then_inc(x_loaded, 16)
            load_unit(0)
            load_unit(1)
            sp.dma_start(page_ids[:, :], io["page_table"].rearrange("s (g o) -> o (s g)", o=1)).then_inc(pages_loaded, 16)
            for g in range(3):
                rows = io[f"state_swa{g}_kv"].shape[2]
                sp.dma_start(io[f"swa{g}_s"][0, :, 0:rows - T_NEW].rearrange("s r a h d -> s (r a h d)"),
                             io[f"state_swa{g}_kv"][0, :, T_NEW:rows].rearrange("s r a h d -> s (r a h d)")).then_inc(kv_stored, 16)
            for n in range(2, 14):
                load_unit(n)
            sp.wait_ge(turned, TURNS_X)
            sp.dma_start(s_mask, io["sample_masks"][:, 0, :]).then_inc(smask_loaded, 16)
            sp.wait_ge(pages_loaded, 16)

            def cache_rows(s, what):
                def to(b, n):
                    return k_stage[:, b:b + n, :] if what == 0 else v_cache[:, s % 4, b:b + n, :]
                done = k_cached if what == 0 else v_cached
                for pg in range(2):
                    page = sp.value_load(page_ids[0:1, 2 * s + pg:2 * s + pg + 1], min_val=0,
                                         max_val=io["cache_moba_kv"].shape[1] - 1)
                    src = io["cache_moba_kv"][0, bass.ds(page, 1), :, what].rearrange("o r h d -> r o (h d)")
                    sp.dma_start(to(pg, 1), src).then_inc(done, 16)
                for g in range(3):
                    src = io[f"state_swa{g}_kv"][0, s, :, what].rearrange("(b r) h d -> r b (h d)", r=P)
                    sp.dma_start(to(CACHE_BLOCK[g + 1], GROUP_PAST[g + 1] // P), src).then_inc(done, 16)

            sp.wait_ge(steps, STEPS_BEFORE[12])
            for s in range(4):
                cache_rows(s, 1)
            for s in range(SEQS):
                if s >= 1:
                    sp.wait_ge(turned, BATCH_BEFORE_SAMPLE + s * K_BATCH + (SP_BATCH if s > 4 else 0))
                if s == 4:
                    sp.wait_ge(s_read, 16 * 4 + 4)
                    sp.dma_start(s_mask, io["sample_masks"][:, 1, :]).then_inc(smask_loaded, 16)
                cache_rows(s, 0)
                if s == 4:
                    sp.wait_ge(spv_done, 1)
                    for s2 in range(4, SEQS):
                        cache_rows(s2, 1)
            sp.wait_ge(spv_done, 2)
            sp.dma_start(x_tok[:, 0:PQ, :], io["x_prompt"][0].rearrange("(t p) c -> p t c", p=P)).then_inc(x_again, 16)
            sp.dma_start(x_tok[0:NS, PQ, :], io["x_sample"].rearrange("s t c -> (s t) c")).then_inc(x_again, 16)

            def load_ln(n, which, l):
                for a, v in enumerate((io[f"ln_{which}_g"], io[f"ln_{which}_b"])):
                    sp.dma_start(gb[:, a, :], v[l:l + 1, :].partition_broadcast(P)
                                 .rearrange("q o c -> q (o c)")).then_inc(gb_loaded, 16)

            def ffn_up(l):
                for a, (r0, rn, src) in enumerate((
                        (0, 2 * SEQS, io["state_ffn_conv"][l].rearrange("s r c -> (s r) c")),
                        (2 * SEQS, 3, io["ffn_conv_w"][l]),
                        (2 * SEQS + 3, 1, io["ffn_conv_b"][l:l + 1, :]))):
                    sp.dma_start(side[r0:r0 + rn, :], src).then_inc(side_loaded, 16)
                base = UNIT_NO[(f"up{l}", 0)]
                with sp.Fori(0, NJ // 2) as i:
                    for u in range(2):
                        sp.wait_ge(lo_done, i * 2 + (base + u - 1))
                        slot = (base + u) % 2
                        place = raw[:, slot, :].rearrange("p (v k c) -> p v k c", v=2, k=KD)
                        for v in range(2):
                            src = (io["ffn_w_up"][l].rearrange("(k p) c -> p k c", p=P)
                                   [:, :, bass.ds((i * 2 + u) * P + v * DFF, P)])
                            sp.dma_start(place[:, v, :, :], src).then_inc(raw_loaded[slot], 16)

            def ffn_down(l, extra):
                base = UNIT_NO[(f"down{l}", 0)]
                load_unit(base)
                load_unit(base + 1)
                sp.wait_ge(conv_step, (l + 1) * NJ * 13)
                load_ln(2 * l + 1, "ffn", l)
                for n in range(base + 2, base + 12 + extra):
                    load_unit(n)

            sp.wait_ge(soT_ready, 2)
            load_ln(0, "mix", 0)
            ffn_up(0)
            ffn_down(0, 2)
            sp.wait_ge(tail_stored, 32)
            sp.dma_start(mask_words, io["level_masks"]).then_inc(gla_loaded, 16)
            with nc.allow_non_contiguous_dma(reason="512 biases, feature-major"):
                sp.dma_start(g_ba, io["gla_b_a"][0].rearrange("(h d o) -> d h o", h=GH, o=1).rearrange("d h o -> d (h o)")).then_inc(gla_loaded, 16)
            sp.dma_start(g_a2[0:16, :], io["gla_w_a2"][0]).then_inc(gla_loaded, 16)
            sp.dma_start(g_reset, io["scan_reset"]).then_inc(gla_loaded, 16)
            sp.dma_start(g_norm, io["gla_norm_g"][0:1, :].partition_broadcast(P).rearrange("q o c -> q (o c)")).then_inc(gla_loaded, 16)
            sp.dma_start(seq_of_row, io["seq_of_row"]).then_inc(gla_loaded, 16)
            out = UNIT_NO[("gla_out", 0)]
            for n in range(UNIT_NO[("gla_qk", 2)], out + 2):
                load_unit(n)
            for h in range(GH):
                if h == 0:
                    sp.wait_ge(steps, STEPS_BEFORE[out])
                else:
                    sp.wait_ge(gla_state_out, 32 * h)
                sp.dma_start(g_sst, io["state_gla"][0, :, h].rearrange("s d v -> d s v")).then_inc(gla_state_in, 16)
                if h == 0:
                    load_unit(out + 2)
                    load_unit(out + 3)
            sp.wait_ge(lev_prod, GH * LEV_ALL)
            load_ln(2, "mix", 1)
            sp.wait_ge(go_done, GH * NTILE)
            sp.wait_ge(gla_state_out, 32 * GH)
            sp.wait_ge(go_read, GH * NTILE)
            ffn_up(1)
            ffn_down(1, 0)

        @block.tensor
        def _(pe):
            batch = Count(turned)

            def turn(pieces):
                bank = TURN[batch.n % 2]
                if batch.n >= 2:
                    pe.wait_ge(turned_out, batch.n - 1)
                if batch.n - 2 in LO_BATCHES:
                    pe.wait_ge(x_lo, LO_BATCHES.index(batch.n - 2) + 1)
                for col, src in pieces:
                    rows, cols = src.shape
                    last = pe.transpose(ps[0:cols, bank, col:col + rows], src, ident[0:rows, 0:rows])
                last.then_inc(turned, batch.one())

            def turn_x(t):
                r0, n = TILES[t]
                for half in range(2):
                    turn([(j * P, x_tok[0:n, t, (half * 4 + j) * P:(half * 4 + j + 1) * P]) for j in range(4)])

            def unit_here(n):
                pe.wait_ge(lo_done, n + 1)

            def lo_here(stage_batch, n):
                pe.wait_ge(x_lo, LO_BATCHES.index(stage_batch) + n)

            def three_products(out, lhs, rhs, ks, first, last):
                for i in range(ks):
                    for a, b in ((0, 0), (0, 1), (1, 0)):
                        mm = pe.matmul(out, lhs(i, a), rhs(i, b), start=first and i == 0 and a + b == 0,
                                       stop=last and i == ks - 1 and a == 1)
                return mm

            def project(n, t, k0, kn, first, last):
                parts = xTh, xTl
                w = of_unit(w_hi, n, kn), of_unit(w_lo, n, kn)
                three_products(ps[:, t, :], lambda i, a: parts[a][:, k0 + i, t * P:(t + 1) * P],
                               lambda i, b: w[b][:, i, :], kn, first, last).then_inc(steps, 1)

            pe.wait_ge(consts_loaded, 16)
            pe.wait_ge(x_loaded, 32)
            for t in range(NTILE):
                turn_x(t)

            def turn_rope(r):
                c, t = divmod(r, NTILE)
                n = TILES[t][1]
                pe.wait_ge(roped, r + 1)
                turn([(j * P, roped_buf[0:n, r % 3, j * P:(j + 1) * P]) for j in range(4)])

            pe.wait_ge(pad_zero, 2)
            for n in range(12):
                c, late = divmod(n, 2)
                unit_here(n)
                for t in range(NTILE):
                    if n == 0:
                        pe.wait_ge(turned_out, 2 * t + 2)
                        lo_here(0, 2 * t + 2)
                    elif not late and c <= 4:
                        pe.wait_ge(qk_read, (c - 1) * NTILE + t + 1)
                    elif not late:
                        pe.wait_ge(v_read, t + 1)
                    project(n, t, 4 * late, 4, not late, bool(late))
                    r = c * NTILE + t - 2
                    if late == (t >= 2) and 0 <= r < 4 * NTILE:
                        turn_rope(r)

            def head_rows(g, h):
                return slice(HD * (h % 2), HD * (h % 2) + HD), 2 * g + h // 2

            def scores(n):
                qi, h = divmod(n, 4)
                for g in range(4):
                    rows, c = head_rows(g, h)
                    k0 = max(0, qi - 1) * P if g == 1 else 0
                    if n >= 1:
                        pe.wait_ge(s_read, 4 * (n - 1) + g + 1)
                    elif g == 0:
                        pe.wait_ge(turned_out, UP0)
                        pe.wait_ge(qk_read, 4 * NTILE)
                        pe.wait_ge(v_read, 2 * NTILE)
                    pe.matmul(ps[:, g, 0:(qi + 1) * P - k0], qkT[rows, c, qi * P:(qi + 1) * P],
                              qkT[rows, 8 + c, k0:(qi + 1) * P], start=True, stop=True).then_inc(s_ready, 1)

            def prob_blocks(qi):
                out = []
                for g in range(4):
                    k0 = max(0, qi - 1) if g == 1 else 0
                    out += [(score_at(qi, g) + (kt - k0) * P, kt, g) for kt in range(k0, qi + 1)]
                return out

            def values(n):
                qi, h = divmod(n, 4)
                blocks = prob_blocks(qi)
                pe.wait_ge(probs, 2 * n + 2)
                for b0 in range(0, len(blocks), 4):
                    turn([(j * P, s_buf[:, n % 2, col:col + P]) for j, (col, _, _) in enumerate(blocks[b0:b0 + 4])])
                if n >= 2:
                    pe.wait_ge(o_ready, 2 * (n - 1))
                pe.wait_ge(turned_out, batch.n)
                bank = (4, 7)[n % 2]
                for merged in range(2):
                    mine = [i for i, b in enumerate(blocks) if (b[2] > 0) == bool(merged)]
                    for i in mine:
                        _, kt, g = blocks[i]
                        mm = pe.matmul(ps[:, bank, merged * P:merged * P + P], pT[:, i, :],
                                       v_tok[:, kt, (2 * g + h // 2) * P:(2 * g + h // 2 + 1) * P],
                                       start=i == mine[0], stop=i == mine[-1])
                mm.then_inc(pv_done, 1)

            def turn_o(qi):
                pe.wait_ge(o_ready, 8 * (qi + 1))
                turn([(j * P, o_tok[:, j * P:(j + 1) * P]) for j in range(4)])

            scores(0)
            for n in range(16):
                if n + 1 < 16:
                    scores(n + 1)
                values(n)
                if n % 4 == 3:
                    turn_o(n // 4)

            pe.wait_ge(qz_ready, 1)
            for tile in range(2):
                for s4 in range(4):
                    s = 4 * tile + s4
                    pe.wait_ge(k_cached, 80 * (s + 1))
                    for b0 in range(0, 14, 4):
                        turn([(j * P, k_stage[:, (b0 + j) % NBLK, (b0 + j) // NBLK * P:(b0 + j) // NBLK * P + P])
                              for j in range(min(4, 14 - b0))])
                    pe.wait_ge(turned_out, batch.n)
                    if s4 == 0:
                        pe.wait_ge(s_read, 64 + 4 * tile)
                    for g in range(4):
                        rows = slice(32 * s4, 32 * s4 + 32)
                        past = GROUP_PAST[g]
                        for pair in range(2):
                            b = pair * NBLK + CACHE_BLOCK[g]
                            pe.matmul(ps[rows, g, 0:past], qz[:, 2 * g + pair, s].rearrange("p h q -> p (h q)"),
                                      kcT[:, b:b + past // P, :].rearrange("p b c -> p (b c)"),
                                      start=pair == 0, stop=pair == 1, tile_position=(0, 32 * s4))
                        for pair in range(2):
                            mm = pe.matmul(ps[rows, g, past:past + NS], qz[:, 2 * g + pair, s].rearrange("p h q -> p (h q)"),
                                           qkT[:, 8 + 2 * g + pair, NP:NT],
                                           start=pair == 0, stop=pair == 1, tile_position=(0, 32 * s4))
                    mm.then_inc(sc_done, 1)
                pe.wait_ge(s_norm, 2 * tile + 2)
                pe.wait_ge(v_cached, 320 * (tile + 1))
                for b0 in range(0, len(KEY_BLOCKS), 4):
                    turn([(j * P, s_buf[:, 0, col:col + kn]) for j, (col, kn, _, _) in enumerate(KEY_BLOCKS[b0:b0 + 4])])
                pe.wait_ge(turned_out, batch.n)
                if tile == 0:
                    pe.wait_ge(o_ready, 32)
                else:
                    pe.wait_ge(soT_ready, 1)
                for merged in range(2):
                    mine = [i for i, b in enumerate(KEY_BLOCKS) if (b[2] > 0) == bool(merged)]
                    mine = [i for i in mine if KEY_BLOCKS[i][3] is None] + [i for i in mine if KEY_BLOCKS[i][3] is not None]
                    for pair in range(2):
                        at = (2 * merged + pair) * P
                        for i in mine:
                            _, kn, g, cb = KEY_BLOCKS[i]
                            if cb is None:
                                mm = pe.matmul(ps[:, 4, at:at + P], v_tok[0:NS, PQ, g * 256 + pair * P:g * 256 + pair * P + P],
                                               pT[0:NS, i, :], start=i == mine[0], stop=False, skip_group_check=True)
                                continue
                            for s4 in range(4):
                                mm = pe.matmul(ps[:, 4, at + 32 * s4:at + 32 * s4 + 32], v_cache[:, s4, cb, pair * P:pair * P + P],
                                               pT[:, i, 32 * s4:32 * s4 + 32], start=False, stop=i == mine[-1],
                                               skip_group_check=True)
                mm.then_inc(spv_done, 1)

            pe.wait_ge(soT_ready, 2)
            lo_here(BATCH_O[PQ - 1], 1)
            for half in range(2):
                unit_here(12 + half)
                for t in range(NTILE):
                    if half == 1:
                        pe.wait_ge(z_read, t + 1)
                    project(12 + half, t, 0, 4, True, True)

            def after_ln(stage):
                for t in range(NTILE):
                    pe.wait_ge(ln_done, stage * NTILE + t + 1)
                    turn_x(t)
                pe.wait_ge(turned_out, batch.n)
                lo_here(batch.n - TURNS_X, TURNS_X)

            def ffn(l):
                pe.wait_ge(side_loaded, 48 * (l + 1))
                for v in range(2):
                    turn([(j * SIDE, side[0:SIDE, (v * NJ + j) * P:(v * NJ + j + 1) * P]) for j in range(NJ)])
                pe.wait_ge(turned_out, batch.n)

                base = UNIT_NO[(f"up{l}", 0)]
                parts = xTh, xTl

                def up(j, u, first):
                    slot = (base + u) % 2
                    w = [part[:, slot, :].rearrange("p (v k c) -> p v k c", v=2, k=KD) for part in (w_hi, w_lo)]
                    pe.wait_ge(lo_done, j + (base + 1))
                    for m, (v, run) in enumerate(UP_RUNS):
                        if not first:
                            pe.wait_ge(ext_ready, j * 4 + (l * NJ * 4 - 3 + m))
                        three_products(ps[:, m, 0:SPLIT], lambda k, a: w[a][:, v, k, :],
                                       lambda k, b: parts[b][:, k, run * SPLIT:(run + 1) * SPLIT], KD, True, True).then_inc(steps, 1)

                def turn_tail(j, u, first):
                    pe.wait_ge(tail_ready, j + (l * NJ + 1))
                    if not first:
                        pe.wait_ge(tail_out, j + (l * NJ - 1))
                    for v in range(2):
                        mm = pe.transpose(ps[0:TAIL, TURN[u], v * P:v * P + P], tl[:, u, v, :], ident[:, :])
                    mm.then_inc(tail_turned, 1)

                up(0, 0, True)
                up(1, 1, False)
                turn_tail(0, 0, True)
                with pe.Fori(1, NJ // 2) as i:
                    up(i * 2, 0, False)
                    turn_tail(i * 2 - 1, 1, False)
                    up(i * 2 + 1, 1, False)
                    turn_tail(i * 2, 0, False)
                turn_tail(NJ - 1, 1, False)

                first_unit = UNIT_NO[(f"down{l}", 0)]
                groups = len(DOWN_GROUPS)
                zr = (2 + 4 * l) * NTILE
                pe.wait_ge(ext_ready, (l + 1) * NJ * 4)
                pe.wait_ge(pad_zero, 4 + 2 * l)
                for c in range(2 * groups):
                    n = first_unit + c
                    half, (_, kn) = c // groups, DOWN_GROUPS[c % groups]
                    unit_here(n)
                    pe.wait_ge(h_lo, 2 * l * groups + c + 1)
                    for t in range(NTILE):
                        if c == groups:
                            pe.wait_ge(z_read, zr + t + 1)
                        project(n, t, 4 * (c % 2), kn, c % groups == 0, c % groups == groups - 1)

            after_ln(0)
            ffn(0)
            pe.wait_ge(tail_out, NJ)
            after_ln(1)

            fm = Count(fm_read)

            def fm_banks(i):
                return i % 2, 2 + i % 2

            def feature_major(i, kn, lhs, rhs, done, bias_free=True):
                a, b = fm_banks(i)
                for k in range(kn):
                    pe.matmul(ps[:, a, 0:SPLIT], lhs(k), rhs(k, 0, SPLIT), start=k == 0, stop=k == kn - 1)
                for k in range(kn):
                    mm = pe.matmul(ps[:, b, 0:SPLIT], lhs(k), rhs(k, SPLIT, NT), start=k == 0, stop=k == kn - 1)
                mm.then_inc(done, 1)

            parts = xTh, xTl
            for i in range(2 * GH):
                n = UNIT_NO[("gla_qk", i // 2)]
                if i % 2 == 0:
                    unit_here(n)
                w = of_unit(w_hi, n, KD), of_unit(w_lo, n, KD)
                if i >= 2:
                    pe.wait_ge(fm_read, i - 1)
                for run in range(2):
                    three_products(ps[:, 2 * run + i % 2, 0:SPLIT], lambda k, a: w[a][:, k, i % 2 * P:(i % 2 + 1) * P],
                                   lambda k, b: parts[b][:, k, run * SPLIT:(run + 1) * SPLIT], KD, True, True).then_inc(steps, 1)
            n = UNIT_NO[("gla_a1", 0)]
            unit_here(n)
            w = of_unit(w_hi, n, KD), of_unit(w_lo, n, KD)
            for run in range(2):
                three_products(ps[:, (4, 7)[run], 0:SPLIT], lambda k, a: w[a][:, k, :],
                               lambda k, b: parts[b][:, k, run * SPLIT:(run + 1) * SPLIT], KD, True, True).then_inc(steps, 1)
            pe.wait_ge(gla_loaded, 96)
            pe.wait_ge(fm_read, 2 * GH + 1)
            for h in range(GH):
                if h >= 2:
                    pe.wait_ge(fm_read, 2 * GH + h)
                feature_major(h, 1, lambda k: g_a2[0:16, h * P:(h + 1) * P], lambda k, a, b: g_t1[0:16, a:b], low_filled)
            pe.wait_ge(fm_read, 3 * GH + 1)
            for i in range(8):
                c, late = divmod(i, 2)
                n = UNIT_NO[("gla_vr", i)]
                unit_here(n)
                for t in range(NTILE):
                    if c >= 1 and not late:
                        pe.wait_ge(tok_read, (c - 1) * NTILE + t + 1)
                    project(n, t, 4 * late, 4, not late, bool(late))
            pe.wait_ge(tok_read, 4 * NTILE)

            def level_products(h, l):
                a = l % 2
                done = h * LEV_ALL + LEV_BEFORE[l]
                kk, qq = (lev_k[:, a], lev_q[:, a]) if l < NLEV else (g_k[:, h], g_q[:, h])
                if done:
                    pe.wait_ge(lev_read, done)
                if l < NLEV:
                    pe.wait_ge(lev_ready, h * NLEV + l + 1)
                for c in range(PQ):
                    mm = pe.matmul(ps[:, a, c * P:(c + 1) * P], kk[:, c * P:(c + 1) * P], qq[:, c * P:(c + 1) * P],
                                   start=True, stop=True)
                mm.then_inc(lev_prod, 1)
                if LEV_WITH_SAMPLE[l]:
                    pe.matmul(ps[0:NS, 2, 0:NS], kk[:, NP:NT], qq[:, NP:NT], start=True, stop=True).then_inc(lev_prod, 1)

            for h in range(GH):
                for l in range(NLEV + 1):
                    level_products(h, l)
                pe.wait_ge(kz_ready, 3 * h + 1)
                turn([(c * P, g_kb[:, c * P:(c + 1) * P]) for c in range(PQ)])
                turn([(0, g_kb[:, NP:NT])])
                pe.wait_ge(turned_out, batch.n)
                pe.wait_ge(lev_read, (h + 1) * LEV_ALL)
                for c in range(PQ):
                    n = h * NTILE + c
                    if n >= 2:
                        pe.wait_ge(go_read, n - 1)
                    bank = (4, 7)[n % 2]
                    vv = g_v[:, c, h * GV:(h + 1) * GV]
                    mm = pe.matmul(ps[:, bank, 0:GV], att[:, h % 2, c * P:(c + 1) * P], vv, start=True, stop=c == 0)
                    if c >= 1:
                        pe.wait_ge(gs_read, h * (PQ + SEQS) + c)
                        mm = pe.matmul(ps[:, bank, 0:GV], g_qb[:, c * P:(c + 1) * P], g_state, start=False, stop=True)
                    mm.then_inc(go_done, 1)
                    if h >= 1 or c >= 1:
                        pe.wait_ge(gs_read, h * (PQ + SEQS) + c)
                    pe.matmul(ps[:, 3, 0:GV], g_kt[:, c, :], vv, start=True, stop=True).then_inc(gs_done, 1)
                n = h * NTILE + PQ
                pe.wait_ge(go_read, n - 1)
                bank = (4, 7)[n % 2]
                vv = g_v[0:NS, PQ, h * GV:(h + 1) * GV]
                pe.wait_ge(kz_ready, 3 * h + 3)
                pe.wait_ge(gla_state_in, 16 * (h + 1))
                pe.matmul(ps[0:NS, bank, 0:GV], att[0:NS, h % 2, NP:NT], vv, start=True, stop=False)
                for s in range(SEQS):
                    mm = pe.matmul(ps[0:NS, bank, 0:GV], g_qz[:, s, :], g_sst[:, s, :], start=False, stop=s == SEQS - 1)
                mm.then_inc(go_done, 1)
                for s in range(SEQS):
                    pe.wait_ge(gs_read, h * (PQ + SEQS) + PQ + s)
                    pe.matmul(ps[:, 3, 0:GV], g_kz[0:NS, s, :], vv, start=True, stop=True).then_inc(gs_done, 1)

            for t in range(NTILE):
                r0, n = TILES[t]
                pe.wait_ge(y_ready, t + 1)
                for half in range(2):
                    turn([(j * P, g_r[0:n, t, (half * 4 + j) * P:(half * 4 + j + 1) * P]) for j in range(4)])
            pe.wait_ge(turned_out, batch.n)
            pe.wait_ge(lev_read, GH * LEV_ALL)
            pe.wait_ge(gs_read, GH * (PQ + SEQS))
            pe.wait_ge(go_read, GH * NTILE)
            lo_here(BATCH_Y, TURNS_X)
            pe.wait_ge(pad_zero, 6)
            for i in range(4):
                c, late = divmod(i, 2)
                n = UNIT_NO[("gla_out", i)]
                unit_here(n)
                for t in range(NTILE):
                    if c == 1 and not late:
                        pe.wait_ge(z_read, 4 * NTILE + t + 1)
                    project(n, t, 4 * late, 4, not late, bool(late))
            after_ln(2)
            ffn(1)

        @block.scalar
        def _(act):
            batch = Count(turned_out)

            def take(dst, src_view, wait_more=None):
                act.wait_ge(turned, batch.n + 1)
                act.activation(dst, src_view(ps[:, TURN[batch.n % 2], :]), ACT.Copy).then_inc(turned_out, batch.one())

            def take_x(t):
                r0, n = TILES[t]
                for half in range(2):
                    take(xTh[:, half * 4:half * 4 + 4, r0:r0 + n],
                         lambda b: b.rearrange("p (j c) -> p j c", j=4)[:, :, 0:n])

            def split_hi(n):
                act.wait_ge(raw_loaded[n % 2], 16 * LOADS * (n // 2 + 1))
                if n >= 2:
                    act.wait_ge(steps, STEPS_BEFORE[n - 1])
                a = unit_width(n)
                act.activation(w_hi[:, n % 2, 0:a], raw[:, n % 2, 0:a], ACT.Copy).then_inc(hi_done, 1)

            split_hi(0)
            for t in range(NTILE):
                take_x(t)

            for n in range(12):
                c, late = divmod(n, 2)
                if n < 11:
                    split_hi(n + 1)
                for t in range(NTILE):
                    if c >= 4 and late:
                        rows = TILES[t][1]
                        act.wait_ge(steps, steps_at("attn_in", n, t))
                        act.activation(v_tok[0:rows, t, (c - 4) * HALF:(c - 3) * HALF], ps[0:rows, t, :], ACT.Copy).then_inc(v_read, 1)
                    r = c * NTILE + t - 2
                    if late == (t >= 2) and 0 <= r < 4 * NTILE:
                        rc, rt = divmod(r, NTILE)
                        r0, rn = TILES[rt]
                        take(qkT[:, 4 * rc:4 * rc + 4, r0:r0 + rn],
                             lambda b: b.rearrange("p (j c) -> p j c", j=4)[:, :, 0:rn])

            def exps(n):
                qi = n // 4
                width = (qi + 1) * P
                sbuf = s_buf[:, n % 2]
                act.wait_ge(nm_ready, n + 1)
                act.activation(sbuf[:, 0:width], sbuf[:, 0:width], ACT.Exp, bias=nm[:, n, 0:1], scale=ATT_SCALE,
                               accum_out=den[:, n, 0:1]).then_inc(probs, 1)
                end = score_at(qi, 3) + width
                act.activation(sbuf[:, 512:end], sbuf[:, 512:end], ACT.Exp, bias=nm[:, n, 1:2], scale=ATT_SCALE,
                               accum_out=den[:, n, 1:2]).then_inc(probs, 1)

            def take_probs(n):
                nblk = P_BLOCKS[n // 4]
                if n >= 1:
                    act.wait_ge(pv_done, n)
                for b0 in range(0, nblk, 4):
                    k = min(4, nblk - b0)
                    take(pT[:, b0:b0 + k, :], lambda b: b.rearrange("p (j c) -> p j c", j=4)[:, 0:k, :])

            exps(0)
            for n in range(16):
                if n + 1 < 16:
                    exps(n + 1)
                take_probs(n)
                if n % 4 == 3:
                    qi = n // 4
                    take(xTh[:, 0:4, qi * P:(qi + 1) * P], lambda b: b.rearrange("p (j c) -> p j c", j=4))

            for tile in range(2):
                for s4 in range(4):
                    s = 4 * tile + s4
                    if s >= 1:
                        act.wait_ge(sc_done, s)
                    for b0 in range(0, 14, 4):
                        k = min(4, 14 - b0)
                        take(kcT[:, b0:b0 + k, :], lambda b: b.rearrange("p (j c) -> p j c", j=4)[:, 0:k, :])
                act.wait_ge(nm_ready, 17 + tile)
                for merged, (a, b) in enumerate(((0, 320), (320, S_COLS))):
                    act.activation(s_buf[:, 0, a:b], s_buf[:, 0, a:b], ACT.Exp, bias=snm[:, tile, merged:merged + 1],
                                   scale=ATT_SCALE, accum_out=sden[:, tile, merged:merged + 1]).then_inc(probs, 1)
                act.wait_ge(pv_done, 16)
                if tile:
                    act.wait_ge(spv_done, tile)
                for b0 in range(0, len(KEY_BLOCKS), 4):
                    blocks = KEY_BLOCKS[b0:b0 + 4]
                    full = [b[1] for b in blocks]
                    act.wait_ge(turned, batch.n + 1)
                    bank = TURN[batch.n % 2]
                    for j, kn in enumerate(full):
                        ins = act.activation(pT[0:kn, b0 + j, :], ps[0:kn, bank, j * P:(j + 1) * P], ACT.Copy)
                    ins.then_inc(turned_out, batch.one())

            act.wait_ge(spv_done, 2)
            split_hi(12)
            split_hi(13)
            split_hi(14)

            def ln_roots(stage):
                for t in range(NTILE):
                    n = TILES[t][1]
                    act.wait_ge(ln_var, stage * NTILE + t + 1)
                    act.activation(ln_sd[0:n, t, 0:1], ln_mv[0:n, t, 1:2], ACT.Sqrt, bias=eps_ln[0:n, 0:1]).then_inc(ln_root, 1)
                    if stage < 3 and t >= 1:
                        take_x(t - 1)
                if stage < 3:
                    take_x(NTILE - 1)

            def ffn(l):
                for v in range(2):
                    take(feat[:, v, :, :].rearrange("p j r -> p (j r)"), lambda b: b[:, 0:NJ * SIDE])
                act.wait_ge(turned_out, batch.n)

                act.wait_ge(pads_zero, l + 1)

                base = UNIT_NO[(f"up{l}", 0)]

                def copy_up(j, u, first):
                    slot = (base + u + 1) % 2
                    act.wait_ge(raw_loaded[slot], (j - u) * 16 + 32 * ((base + u + 1) // 2 + 1))
                    act.wait_ge(steps, j * 4 + STEPS_BEFORE[base])
                    act.activation(w_hi[:, slot, :], raw[:, slot, :], ACT.Copy).then_inc(hi_done, 1)
                    if not first:
                        act.wait_ge(conv_step, j * 13 + (l * NJ * 13 - 13))
                        act.wait_ge(tail_ready, j + (l * NJ - 1))
                    act.activation(fj[:, u, :, :], feat[:, :, bass.ds(j, 1), :].rearrange("p v o r -> p v (o r)"), ACT.Copy)
                    for v in range(2):
                        act.activation(ext_s[:, u, v, :, 0:2], feat[:, v, bass.ds(j, 1), 0:2 * SEQS].rearrange("p o (s r) -> p s (o r)", r=2), ACT.Copy)
                    for m, (v, run) in enumerate(UP_RUNS):
                        act.wait_ge(steps, j * 4 + (STEPS_BEFORE[base] + 1 + m))
                        if run == 0:
                            act.activation(ext[:, u, v, 2:2 + SPLIT], ps[:, m, 0:SPLIT], ACT.Copy).then_inc(ext_ready, 1)
                        else:
                            act.activation(ext[:, u, v, 2 + SPLIT:2 + NP], ps[:, m, 0:PRE], ACT.Copy)
                            act.activation(ext_s[:, u, v, :, 2:10], ps[:, m, PRE:SPLIT].rearrange("p (s t) -> p s t", s=SEQS),
                                           ACT.Copy).then_inc(ext_ready, 1)

                def silu(j, u):
                    act.wait_ge(conv_step, j * 13 + (l * NJ * 13 + 6))
                    act.activation(conv_y[:, u, 1, :], conv_y[:, u, 1, :], ACT.Silu).then_inc(silu_done, 1)

                def take_tail(j, u):
                    act.wait_ge(tail_turned, j + (l * NJ + 1))
                    dst = side[0:TAIL, :].rearrange("r (v c) -> r v c", v=2)[:, :, bass.ds(j * P, P)]
                    act.activation(dst, ps[0:TAIL, TURN[u], 0:2 * P].rearrange("r (v c) -> r v c", v=2), ACT.Copy).then_inc(tail_out, 1)

                copy_up(0, 0, True)
                silu(0, 0)
                copy_up(1, 1, True)
                silu(1, 1)
                take_tail(0, 0)
                with act.Fori(1, NJ // 2) as i:
                    copy_up(i * 2, 0, False)
                    silu(i * 2, 0)
                    take_tail(i * 2 - 1, 1)
                    copy_up(i * 2 + 1, 1, False)
                    silu(i * 2 + 1, 1)
                    take_tail(i * 2, 0)
                take_tail(NJ - 1, 1)

                first_unit = UNIT_NO[(f"down{l}", 0)]
                groups = len(DOWN_GROUPS)

                def h_split(c):
                    k0, kn = DOWN_GROUPS[c % groups]
                    act.wait_ge(conv_step, (l * NJ + k0 + kn) * 13)
                    act.wait_ge(steps, STEPS_BEFORE[max(first_unit, first_unit + c - 1)])
                    act.activation(xTh[:, 4 * (c % 2):4 * (c % 2) + kn, 0:NT], hT[:, k0:k0 + kn, :], ACT.Copy).then_inc(h_hi, 1)

                h_split(0)
                for c in range(2 * groups):
                    if first_unit + c + 1 < len(UNITS):
                        split_hi(first_unit + c + 1)
                    if c + 1 < 2 * groups:
                        h_split(c + 1)

            ln_roots(0)
            ffn(0)
            ln_roots(1)

            def copy_fm(i, dst, scale=1.0, func=ACT.Copy, bias=None):
                for bank, a, b in ((i % 2, 0, SPLIT), (2 + i % 2, SPLIT, NT)):
                    if bias is None:
                        ins = act.activation(dst[:, a:b], ps[:, bank, 0:b - a], func, scale=scale)
                    else:
                        ins = act.activation(dst[:, a:b], ps[:, bank, 0:b - a], ACT.Identity, bias=bias)
                ins.then_inc(fm_read, 1)

            for i in range(2 * GH):
                n = UNIT_NO[("gla_qk", i // 2)]
                if i % 2 == 0:
                    split_hi(n + 1)
                act.wait_ge(steps, STEPS_BEFORE[n] + 2 * (i % 2) + 2)
                copy_fm(i, (g_q if i < GH else g_k)[:, i % GH], GK ** -0.5 if i < GH else 1.0)
            n = UNIT_NO[("gla_a1", 0)]
            split_hi(n + 1)
            act.wait_ge(steps, STEPS_BEFORE[n + 1])
            for run in range(2):
                ins = act.activation(g_t1[0:16, run * SPLIT:(run + 1) * SPLIT], ps[0:16, (4, 7)[run], 0:SPLIT], ACT.Copy)
            ins.then_inc(fm_read, 1)
            for h in range(GH):
                act.wait_ge(low_filled, 1 + h)
                copy_fm(h, g_b[:, h], bias=g_ba[:, h:h + 1])
            zz = g_b.rearrange("p h n -> p (h n)")
            act.wait_ge(fm_read, 3 * GH + 1)
            act.activation(g_tmp, zz, ACT.Abs).then_inc(gates, 1)
            act.wait_ge(gates, 1)
            act.activation(g_tmp, g_tmp, ACT.Exp, scale=-1.0).then_inc(gates, 1)
            act.wait_ge(gates, 2)
            act.activation(g_tmp, g_tmp, ACT.Ln, bias=1.0).then_inc(gates, 1)
            for i in range(8):
                c, late = divmod(i, 2)
                split_hi(UNIT_NO[("gla_vr", i)] + 1)
                for t in range(NTILE):
                    if not late:
                        continue
                    n = TILES[t][1]
                    act.wait_ge(steps, steps_at("gla_vr", i, t))
                    dst = (g_v if c < 2 else g_r)[0:n, t, (c % 2) * HALF:(c % 2 + 1) * HALF]
                    act.activation(dst, ps[0:n, t, :], ACT.Copy if c < 2 else ACT.Silu).then_inc(tok_read, 1)
            split_hi(UNIT_NO[("gla_out", 1)])
            sq = Count(sq_done)
            for h in range(GH):
                for l in range(NLEV):
                    ncol = NT if l < 3 else NP
                    act.wait_ge(lev_diff, h * (NLEV + 1) + l + 1)
                    e = lev_e[:, l % 2, 0:ncol]
                    act.activation(e, e, ACT.Exp, scale=1.0 / TAU).then_inc(lev_exp, 1)
                act.wait_ge(lev_ready, h * NLEV + NLEV - 1)
                act.activation(lev_e[:, 1, :], g_b[:, h], ACT.Exp, scale=1.0 / TAU).then_inc(lev_exp, 1)
                act.wait_ge(lev_diff, (h + 1) * (NLEV + 1))
                act.activation(lev_e[:, 0, :], lev_e[:, 0, :], ACT.Exp, scale=1.0 / TAU).then_inc(lev_exp, 1)
                if h >= 1:
                    act.wait_ge(gs_done, h * (PQ + SEQS))
                take(g_kt[:, 0:PQ, :], lambda b: b.rearrange("p (j c) -> p j c", j=4))
                take(g_kt[0:NS, PQ, :], lambda b: b[0:NS, 0:P])
                for t in range(NTILE):
                    n = TILES[t][1]
                    act.wait_ge(go_done, sq.n + 1)
                    if sq.n >= 1:
                        act.wait_ge(sq_done, sq.n)
                    act.activation(squares[0:n, :], ps[0:n, (4, 7)[sq.n % 2], 0:GV], ACT.Square,
                                   accum_out=g_ss[0:n, t, h:h + 1]).then_inc(sq_done, sq.one())
            act.wait_ge(sq_done, GH * NTILE)
            act.activation(g_rs.rearrange("p t h -> p (t h)"), g_ss.rearrange("p t h -> p (t h)"), ACT.Sqrt,
                           bias=eps_ln[:, 1:2], scale=1.0 / GV).then_inc(gates, 1)
            act.wait_ge(gla_state_out, 32 * GH)
            for t in range(NTILE):
                take_x(t)
            for c in range(1, 4):
                split_hi(UNIT_NO[("gla_out", c)] + 1)
            ln_roots(2)
            ffn(1)
            ln_roots(3)

        @block.vector
        def _(dve):
            vs = Count(vec)

            def settle():
                dve.wait_ge(vec, vs.n)

            dve.memset(eps_ln[:, 0:1], LN_EPS)
            dve.memset(eps_ln[:, 1:2], RMS_EPS).then_inc(vec, vs.one())
            def split_lo(n):
                dve.wait_ge(hi_done, n + 1)
                a = unit_width(n)
                dve.tensor_tensor(w_lo[:, n % 2, 0:a], raw[:, n % 2, 0:a], w_hi[:, n % 2, 0:a].bitcast(F32),
                                  ALU.subtract).then_inc(lo_done, 1)

            def batch_lo(b, k0, r0, n):
                dve.wait_ge(turned_out, b + 1)
                dve.tensor_tensor(xTl[:, k0:k0 + 4, r0:r0 + n],
                                  ps[:, TURN[b % 2], :].rearrange("p (j c) -> p j c", j=4)[:, :, 0:n],
                                  xTh[:, k0:k0 + 4, r0:r0 + n].bitcast(F32), ALU.subtract).then_inc(x_lo, 1)

            def x_los(first_batch, t):
                for half in range(2):
                    batch_lo(first_batch + 2 * t + half, 4 * half, *TILES[t])

            split_lo(0)
            for t in range(NTILE):
                x_los(0, t)
            dve.wait_ge(consts_loaded, 64)
            for r in range(4 * NTILE):
                c, t = divmod(r, NTILE)
                n = TILES[t][1]
                if t == 0:
                    split_lo(2 * c + 1)
                    split_lo(2 * c + 2)
                dve.wait_ge(steps, steps_at("attn_in", 2 * c + 1, t))
                if r >= 1:
                    dve.wait_ge(roped, r)
                src = ps[0:n, t, :].rearrange("p (h a d) -> p h a d", h=8, a=2)
                a4 = rope_a[0:n, :].rearrange("p (h d) -> p h d", h=8)
                b4 = rope_b[0:n, :].rearrange("p (h a d) -> p h a d", h=8, a=2)
                dve.tensor_tensor(a4, ps[0:n, t, :].rearrange("p (h d) -> p h d", h=8),
                                  cos_t[0:n, t:t + 1, :].to_broadcast([n, 8, HD]), ALU.mult)
                for a in range(2):
                    ins = dve.tensor_tensor(b4[:, :, a, :], src[:, :, 1 - a, :],
                                            sin_t[0:n, t:t + 1, 32 * a:32 * a + 32].to_broadcast([n, 8, 32]), ALU.mult)
                ins.then_inc(qk_read, 1)
                dve.wait_ge(qk_read, r + 1)
                if r >= 3:
                    dve.wait_ge(turned, TURNS_X + r - 2)
                if r - 3 >= 2 * NTILE:
                    dve.wait_ge(k_stored[r % ROPED], K_STORES[r - 3])
                dve.tensor_tensor(roped_buf[0:n, r % 3, :], rope_a[0:n, :], rope_b[0:n, :], ALU.add).then_inc(roped, 1)

            for n in range(9, 12):
                split_lo(n)

            def soft_scores(n):
                qi, h = divmod(n, 4)
                if n >= 2:
                    dve.wait_ge(pv_done, n - 1)
                else:
                    dve.wait_ge(turned, UP0)
                    for i in range(ROPED):
                        dve.wait_ge(k_stored[i], stores_[i])
                for g in range(4):
                    full = 256 if g == 1 else 512
                    width = min((qi + 1) * P, full)
                    dve.wait_ge(s_ready, 4 * n + g + 1)
                    acc = mb[:, n, 0:1] if g == 0 else mx[:, n, g:g + 1]
                    dve.tensor_tensor_reduce(s_buf[:, n % 2, score_at(qi, g):score_at(qi, g) + width], ps[:, g, 0:width],
                                             masks[:, MASK_AT[g] + full - width:MASK_AT[g] + full],
                                             1.0, LOWEST, ALU.add, ALU.max, acc).then_inc(s_read, 1)
                dve.wait_ge(s_read, 4 * n + 4)
                dve.tensor_reduce(mb[:, n, 1:2], mx[:, n, 1:4], AXX, ALU.max).then_inc(vec, vs.one())
                settle()
                dve.tensor_scalar(nm[:, n, :], mb[:, n, :], -ATT_SCALE, None, ALU.mult).then_inc(nm_ready, 1)

            def outputs(n):
                qi, h = divmod(n, 4)
                dve.wait_ge(probs, 2 * n + 2)
                dve.reciprocal(rden[:, n, :], den[:, n, :]).then_inc(vec, vs.one())
                settle()
                dve.wait_ge(pv_done, n + 1)
                if h == 0 and qi >= 1:
                    dve.wait_ge(turned, UP0 + 4 * sum(P_BATCH[:qi]) + qi)
                for merged in range(2):
                    at = merged * 256 + h * HD
                    own = merged * P + h % 2 * HD
                    dve.tensor_scalar(o_tok[:, at:at + HD], ps[:, (4, 7)[n % 2], own:own + HD],
                                      rden[:, n, merged:merged + 1], None, ALU.mult).then_inc(o_ready, 1)

            soft_scores(0)
            for n in range(16):
                if n + 1 < 16:
                    soft_scores(n + 1)
                if n % 4 == 0 and n:
                    batch_lo(BATCH_O[n // 4 - 1], 0, (n // 4 - 1) * P, P)
                outputs(n)
            batch_lo(BATCH_O[PQ - 1], 0, (PQ - 1) * P, P)

            for tile in range(2):
                dve.wait_ge(sc_done, 4 * tile + 4)
                dve.wait_ge(smask_loaded, 16 * (tile + 1))
                if tile == 0:
                    dve.wait_ge(pv_done, 16)
                else:
                    dve.wait_ge(turned, BATCH_BEFORE_SAMPLE + 4 * K_BATCH + SP_BATCH)
                for g in range(4):
                    a, width = GROUP_AT[g], GROUP_PAST[g] + NS
                    acc = smb[:, tile, 0:1] if g == 0 else smx[:, tile, g:g + 1]
                    dve.tensor_tensor_reduce(s_buf[:, 0, a:a + width], ps[:, g, 0:width], s_mask[:, a:a + width],
                                             1.0, LOWEST, ALU.add, ALU.max, acc).then_inc(s_read, 1)
                dve.wait_ge(s_read, 64 + 4 * (tile + 1))
                dve.tensor_reduce(smb[:, tile, 1:2], smx[:, tile, 1:4], AXX, ALU.max).then_inc(vec, vs.one())
                settle()
                dve.tensor_scalar(snm[:, tile, :], smb[:, tile, :], -ATT_SCALE, None, ALU.mult).then_inc(nm_ready, 1)
                dve.wait_ge(probs, 32 + 2 * (tile + 1))
                dve.reciprocal(srd[:, tile, :], sden[:, tile, :]).then_inc(vec, vs.one())
                settle()
                for merged, (a, b) in enumerate(((0, 320), (320, S_COLS))):
                    dve.tensor_scalar(s_buf[:, 0, a:b], s_buf[:, 0, a:b], srd[:, tile, merged:merged + 1], None,
                                      ALU.mult).then_inc(s_norm, 1)
                dve.wait_ge(spv_done, tile + 1)
                for part in range(2):
                    for merged in range(2):
                        for pair in range(2):
                            for b in range(2):
                                src = (ps[HD * b:HD * b + HD, 4, (2 * merged + pair) * P:(2 * merged + pair + 1) * P]
                                       .rearrange("p (s h q) -> p s h q", s=4, h=4)[:, :, 2 * pair + b, :])
                                t0 = NP + 32 * tile
                                hi, lo = [x[HD * b:HD * b + HD, 2 * merged + pair, t0:t0 + 32].rearrange("p (s q) -> p s q", s=4)
                                          for x in (xTh, xTl)]
                                ins = (dve.tensor_tensor(lo, src, hi.bitcast(F32), ALU.subtract) if part
                                       else dve.tensor_copy(hi, src))
                    if part == 0:
                        ins.then_inc(vec, vs.one())
                        settle()
                ins.then_inc(soT_ready, 1)
            split_lo(12)

            def residual(stage, half, t, step):
                n = TILES[t][1]
                dve.wait_ge(steps, step)
                z = x_tok[0:n, t, half * HALF:(half + 1) * HALF]
                dve.scalar_tensor_tensor(z, z, ALPHA, ps[0:n, t, :], ALU.mult, ALU.add).then_inc(z_read, 1)
                dve.wait_ge(z_read, (2 * stage + half) * NTILE + t + 1)
                dve.bn_stats(ln_stats[0:n, t, half, :], z).then_inc(vec, vs.one())

            def normalise(stage, t):
                n = TILES[t][1]
                settle()
                dve.bn_aggr(ln_mv[0:n, t, :], ln_stats[0:n, t, :, :]).then_inc(ln_var, 1)
                dve.wait_ge(ln_root, stage * NTILE + t + 1)
                dve.reciprocal(ln_sd[0:n, t, 1:2], ln_sd[0:n, t, 0:1]).then_inc(vec, vs.one())
                settle()
                x = x_tok[0:n, t, :]
                dve.tensor_scalar(x, x, ln_mv[0:n, t, 0:1], ln_sd[0:n, t, 1:2], ALU.subtract, ALU.mult).then_inc(vec, vs.one())
                settle()
                dve.tensor_tensor(x, x, gb[0:n, 0, :], ALU.mult).then_inc(vec, vs.one())
                settle()
                dve.tensor_tensor(x, x, gb[0:n, 1, :], ALU.add).then_inc(ln_done, 1)

            def residual_ln(stage, units, duty, first_batch):
                dve.wait_ge(gb_loaded, 32 * (stage + 1))
                per_half = len(units) // 2
                for c, n in enumerate(units):
                    duty(c)
                    half, late = divmod(c, per_half)
                    if late < per_half - 1:
                        continue
                    for t in range(NTILE):
                        residual(stage, half, t, STEPS_BEFORE[n] + t + 1)
                        if half == 1:
                            normalise(stage, t)
                            if t >= 1 and first_batch is not None:
                                x_los(first_batch, t - 1)
                if first_batch is not None:
                    x_los(first_batch, NTILE - 1)

            def units_of(kind, n):
                return [UNIT_NO[(kind, c)] for c in range(n)]

            def down_norm(l, first_batch):
                groups = len(DOWN_GROUPS)
                units = units_of(f"down{l}", 2 * groups)

                def h_split(c):
                    kn = DOWN_GROUPS[c % groups][1]
                    k0 = DOWN_GROUPS[c % groups][0]
                    at = 4 * (c % 2)
                    dve.wait_ge(h_hi, 2 * l * groups + c + 1)
                    dve.tensor_tensor(xTl[:, at:at + kn, 0:NT], hT[:, k0:k0 + kn, :],
                                      xTh[:, at:at + kn, 0:NT].bitcast(F32), ALU.subtract).then_inc(h_lo, 1)

                def duty(c):
                    if units[c] + 1 < len(UNITS):
                        split_lo(units[c] + 1)
                    if c + 1 < 2 * groups:
                        h_split(c + 1)

                h_split(0)
                residual_ln(2 * l + 1, units, duty, first_batch)

            def conv(j, u, l, first):
                n, slot = UNIT_NO[(f"up{l}", 0)] + 1, (UNIT_NO[(f"up{l}", 0)] + u + 1) % 2
                dve.wait_ge(hi_done, j + (n + 1))
                dve.tensor_tensor(w_lo[:, slot, :], raw[:, slot, :], w_hi[:, slot, :].bitcast(F32),
                                  ALU.subtract).then_inc(lo_done, 1)
                base = j * 13 + l * NJ * 13
                for v in (1, 0):
                    at = 0 if v else 6
                    dve.wait_ge(ext_ready, j * 4 + (l * NJ * 4 + (2 if v else 4)))
                    for tap in range(3):
                        if tap:
                            dve.wait_ge(conv_step, base + (at + 2 * tap))
                        w = fj[:, u, v, 2 * SEQS + tap:2 * SEQS + tap + 1]
                        yp, ys = conv_y[:, u, v, 0:NP], conv_y[:, u, v, NP:NT].rearrange("p (s t) -> p s t", s=SEQS)
                        ep, es = ext[:, u, v, tap:tap + NP], ext_s[:, u, v, :, tap:tap + T_NEW]
                        for y, e in ((yp, ep), (ys, es)):
                            if tap == 0:
                                ins = dve.tensor_scalar(y, e, w, fj[:, u, v, SIDE - 1:SIDE], ALU.mult, ALU.add)
                            else:
                                ins = dve.scalar_tensor_tensor(y, e, w, y, ALU.mult, ALU.add)
                            ins.then_inc(conv_step, 1)
                if not first:
                    dve.wait_ge(tail_turned, j + (l * NJ - 1))
                for v in range(2):
                    dve.tensor_copy(tl[:, u, v, 0:2], ext[:, u, v, 512:514])
                    ins = dve.tensor_copy(tl[:, u, v, 2:TAIL].rearrange("p (s r) -> p s r", r=2), ext_s[:, u, v, :, 8:10])
                ins.then_inc(tail_ready, 1)
                dve.wait_ge(conv_step, base + 12)
                dve.wait_ge(silu_done, j + (l * NJ + 1))
                dve.tensor_tensor(hT[:, bass.ds(j, 1), :].rearrange("p o n -> p (o n)"), conv_y[:, u, 0, :],
                                  conv_y[:, u, 1, :], ALU.mult).then_inc(conv_step, 1)

            def ffn(l):
                conv(0, 0, l, True)
                conv(1, 1, l, True)
                with dve.Fori(1, NJ // 2) as i:
                    conv(i * 2, 0, l, False)
                    conv(i * 2 + 1, 1, l, False)

            dve.wait_ge(x_again, 32)
            residual_ln(0, [12, 13], lambda c: split_lo(13 + c), BATCH_LN0)
            dve.wait_ge(v_stored, V_STORES)
            ffn(0)
            down_norm(0, BATCH_LN1)

            for n in units_of("gla_qk", 4) + [UNIT_NO[("gla_a1", 0)]]:
                split_lo(n + 1)
            dve.wait_ge(gates, 3)
            zz = g_b.rearrange("p h n -> p (h n)")
            dve.scalar_tensor_tensor(zz, zz, 0.0, g_tmp, ALU.min, ALU.subtract).then_inc(vec, vs.one())
            split_lo(UNIT_NO[("gla_vr", 1)])
            settle()
            dve.wait_ge(gla_loaded, 96)
            for h in range(GH):
                dve.tensor_tensor_scan(g_b[:, h], g_reset, g_b[:, h], 0.0, ALU.mult, ALU.add).then_inc(vec, vs.one())
            settle()
            dve.tensor_copy(g_mask, mask_words).then_inc(vec, vs.one())
            settle()
            for n in range(UNIT_NO[("gla_vr", 2)], UNIT_NO[("gla_out", 2)]):
                split_lo(n)
            dve.wait_ge(steps, STEPS_BEFORE[UNIT_NO[("gla_out", 0)]])
            for z in (lev_q, lev_k, att, g_qz, g_ss):
                dve.memset(z, 0.0).then_inc(vec, vs.one())
            settle()

            def blocks(x, ncol, half):
                return x[:, 0:ncol].rearrange("p (n a c) -> p n a c", a=2, c=half)

            def differences(h, l):
                half = 1 << l
                ncol = NT if l < 3 else NP
                if l >= 2:
                    dve.wait_ge(lev_ready, h * NLEV + l - 1)
                elif h:
                    dve.wait_ge(kz_ready, 3 * h)
                    dve.wait_ge(gs_read, h * (PQ + SEQS))
                b, d = blocks(g_b[:, h], ncol, half), blocks(lev_e[:, l % 2], ncol, half)
                ref = b[:, :, 0, half - 1:half].to_broadcast([P, ncol // (2 * half), half])
                dve.tensor_tensor(d[:, :, 1, :], b[:, :, 1, :], ref, ALU.subtract)
                dve.tensor_tensor(d[:, :, 0, :], ref, b[:, :, 0, :], ALU.subtract).then_inc(lev_diff, 1)

            def decayed(h, l):
                half = 1 << l
                ncol = NT if l < 3 else NP
                dve.wait_ge(lev_exp, h * (NLEV + 2) + l + 1)
                if l >= 2:
                    dve.wait_ge(lev_prod, h * LEV_ALL + LEV_BEFORE[l - 1])
                elif h:
                    dve.wait_ge(lev_prod, h * LEV_ALL)
                e = blocks(lev_e[:, l % 2], ncol, half)
                q, k = blocks(g_q[:, h], ncol, half), blocks(g_k[:, h], ncol, half)
                dve.tensor_tensor(blocks(lev_q[:, l % 2], ncol, half)[:, :, 1, :], q[:, :, 1, :], e[:, :, 1, :], ALU.mult)
                dve.tensor_tensor(blocks(lev_k[:, l % 2], ncol, half)[:, :, 0, :], k[:, :, 0, :], e[:, :, 0, :],
                                  ALU.mult).then_inc(lev_ready, 1)

            def placed(h, l):
                n = h * LEV_ALL + LEV_BEFORE[l]
                if l == 0 and h >= 2:
                    dve.wait_ge(go_done, (h - 1) * NTILE)
                dve.wait_ge(lev_prod, n + 1)
                if n:
                    dve.wait_ge(lev_read, n)
                a = att[:, h % 2]
                m = g_mask[:, l:l + 1, :].to_broadcast([P, PQ, P])
                dve.copy_predicated(a[:, 0:NP].rearrange("p (c n) -> p c n", c=PQ), m,
                                    ps[:, l % 2, :].rearrange("p (c n) -> p c n", c=PQ)).then_inc(lev_read, 1)
                if LEV_WITH_SAMPLE[l]:
                    dve.wait_ge(lev_prod, n + 2)
                    dve.copy_predicated(a[0:NS, NP:NT], g_mask[0:NS, l, 0:NS], ps[0:NS, 2, 0:NS]).then_inc(lev_read, 1)

            for h in range(GH):
                differences(h, 0)
                differences(h, 1)
                for l in range(NLEV):
                    decayed(h, l)
                    if l >= 1:
                        placed(h, l - 1)
                    if l + 2 < NLEV:
                        dve.wait_ge(lev_ready, h * NLEV + l + 1)
                        differences(h, l + 2)
                placed(h, NLEV - 1)
                placed(h, NLEV)
                dve.wait_ge(lev_ready, (h + 1) * NLEV)
                dve.wait_ge(lev_exp, h * (NLEV + 2) + NLEV + 1)
                if h:
                    dve.wait_ge(go_done, h * NTILE)
                    dve.wait_ge(turned, BATCH_GLA + 2 * h)
                e0 = lev_e[:, 1]
                dve.tensor_tensor(g_qb, g_q[:, h], e0, ALU.mult).then_inc(vec, vs.one())
                e1 = lev_e[:, 0]
                for a, b, n, c in ((0, NP, PQ, P), (NP, NT, SEQS, T_NEW)):
                    bb = g_b[:, h, a:b].rearrange("p (n c) -> p n c", n=n)
                    ins = dve.tensor_tensor(e1[:, a:b].rearrange("p (n c) -> p n c", n=n),
                                            bb[:, :, c - 1:c].to_broadcast([P, n, c]), bb, ALU.subtract)
                ins.then_inc(lev_diff, 1)
                dve.wait_ge(lev_exp, (h + 1) * (NLEV + 2))
                dve.tensor_tensor(g_kb, g_k[:, h], e1, ALU.mult).then_inc(kz_ready, 1)
                settle()
                if h:
                    dve.wait_ge(gs_done, h * (PQ + SEQS))
                dve.tensor_copy(g_qz_own, g_qb[:, NP:NT].rearrange("p (s t) -> p s t", s=SEQS)).then_inc(kz_ready, 1)
                dve.wait_ge(turned_out, BATCH_GLA + 2 * h + 2)
                dve.tensor_tensor(g_kz[0:NS, :, :], g_kt[0:NS, PQ:PQ + 1, :].to_broadcast([NS, SEQS, P]),
                                  seq_of_row.rearrange("p (s o) -> p s o", o=1).to_broadcast([NS, SEQS, P]), ALU.mult).then_inc(kz_ready, 1)
                if h == 0:
                    dve.wait_ge(r_scaled, NTILE)

                def gate_out(t):
                    n = h * NTILE + t
                    rows = TILES[t][1]
                    dve.wait_ge(sq_done, n + 1)
                    r = g_r[0:rows, t, h * GV:(h + 1) * GV]
                    dve.tensor_tensor(r, ps[0:rows, (4, 7)[n % 2], 0:GV], r, ALU.mult).then_inc(go_read, 1)

                for c in range(PQ):
                    n = h * (PQ + SEQS) + c
                    dve.wait_ge(gs_done, n + 1)
                    if c == 0:
                        if h:
                            dve.wait_ge(gla_state_out, 32 * h)
                        dve.tensor_copy(g_state, ps[:, 3, 0:GV]).then_inc(gs_read, 1)
                    else:
                        dve.wait_ge(go_done, h * NTILE + c + 1)
                        dve.wait_ge(gs_read, n)
                        dve.scalar_tensor_tensor(g_state, g_state, e0[:, c * P + P - 1:c * P + P], ps[:, 3, 0:GV],
                                                 ALU.mult, ALU.add).then_inc(gs_read, 1)
                    gate_out(c)
                dve.wait_ge(go_done, (h + 1) * NTILE)
                gate_out(PQ)
                for s in range(SEQS):
                    n = h * (PQ + SEQS) + PQ + s
                    dve.wait_ge(gs_done, n + 1)
                    col = NP + s * T_NEW + T_NEW - 1
                    dve.scalar_tensor_tensor(g_sst[:, s, :], g_sst[:, s, :], e0[:, col:col + 1], ps[:, 3, 0:GV],
                                             ALU.mult, ALU.add).then_inc(gs_read, 1)
            dve.wait_ge(gates, 4)
            dve.reciprocal(g_rs, g_rs).then_inc(vec, vs.one())
            settle()
            dve.wait_ge(go_read, GH * NTILE)
            for t in range(NTILE):
                n = TILES[t][1]
                r = g_r[0:n, t, :].rearrange("p (h c) -> p h c", h=GH)
                dve.tensor_tensor(r, r, g_rs[0:n, t, :].rearrange("p (h o) -> p h o", o=1).to_broadcast([n, GH, GV]),
                                  ALU.mult).then_inc(y_ready, 1)
            dve.wait_ge(gla_state_out, 32 * GH)
            for t in range(NTILE):
                x_los(BATCH_Y, t)
            residual_ln(2, units_of("gla_out", 4), lambda c: split_lo(UNIT_NO[("gla_out", c)] + 1) if c else None, BATCH_LN2)
            ffn(1)
            down_norm(1, None)

        @block.gpsimd
        def _(pool):
            pool.dma_start(ident[:, :], io["ident"]).then_inc(consts_loaded, 16)

            def zero_pads():
                for x in (xTh, xTl):
                    pool.memset(x[:, :, NT:SLOT].bitcast(F32), 0.0).then_inc(pad_zero, 1)
            zero_pads()
            pool.wait_ge(consts_loaded, 16)
            pool.dma_start(cos_t, io["rope_cos"]).then_inc(consts_loaded, 16)
            pool.dma_start(sin_t, io["rope_sin"]).then_inc(consts_loaded, 16)
            pool.dma_start(masks, io["prompt_masks"]).then_inc(consts_loaded, 16)
            pool.memset(qz_reg, 0.0).then_inc(qz_zero, 1)

            new_rows = {0: ("moba", None), 1: ("swa0", 120), 2: ("swa1", 248), 3: ("swa2", 248)}

            def store_piece(src, t, g, a, done):
                if not pieces_of(t, g):
                    return
                name, at = new_rows[g]
                if t < PQ:
                    r0 = 0 if g == 1 else t * P
                    dst = io[f"{name}_p"][0, 0, r0:r0 + P, a].rearrange("r h d -> r (h d)")
                elif g == 0:
                    dst = io["moba_s"][0, :, :, a].rearrange("s r h d -> s r (h d)")
                else:
                    dst = io[f"{name}_s"][0, :, at:at + T_NEW, a].rearrange("s r h d -> s r (h d)")
                pool.dma_start(dst, src).then_inc(done, 16)

            for r in range(2 * NTILE, 4 * NTILE):
                c, t = divmod(r, NTILE)
                n = TILES[t][1]
                pool.wait_ge(roped, r + 1)
                for half in range(2):
                    store_piece(roped_buf[0:n, r % 3, half * 256:half * 256 + 256], t, 2 * (c - 2) + half, 0, k_stored[r % ROPED])
            pool.wait_ge(qz_zero, 1)
            pool.wait_ge(turned_out, UP0)
            for c in range(8):
                for b in range(2):
                    src = qkT[HD * b:HD * b + HD, c, NP:NT].rearrange("p (s q) -> p s q", s=SEQS)
                    ins = pool.tensor_copy(qz[HD * b:HD * b + HD, c, :, 2 * (c % 2) + b, :], src)
            ins.then_inc(qz_ready, 1)
            pool.wait_ge(v_read, 2 * NTILE)
            for t in range(NTILE):
                n = TILES[t][1]
                for g in range(4):
                    store_piece(v_tok[0:n, t, g * 256:(g + 1) * 256], t, g, 1, v_stored)

            def ffn(l):
                pool.memset(ext[:, :, :, 0:2], 0.0).then_inc(pads_zero, 1)

                pool.wait_ge(tail_out, (l + 1) * NJ)
                pool.dma_start(io["ffn_p"][l, 0], side[0:2, :]).then_inc(tail_stored, 16)
                pool.dma_start(io["ffn_s"][l].rearrange("s r c -> (s r) c"), side[2:TAIL, :]).then_inc(tail_stored, 16)

            pool.wait_ge(soT_ready, 2)
            pool.wait_ge(steps, STEPS_BEFORE[14])
            zero_pads()
            ffn(0)
            pool.wait_ge(gla_loaded, 96)
            for t in range(NTILE):
                n = TILES[t][1]
                pool.wait_ge(tok_read, 3 * NTILE + t + 1)
                r = g_r[0:n, t, :].rearrange("p (h c) -> p h c", h=GH)
                pool.tensor_tensor(r, r, g_norm[0:n, :].rearrange("p (o c) -> p o c", o=1).to_broadcast([n, GH, GV]),
                                   ALU.mult).then_inc(r_scaled, 1)
            for h in range(GH):
                pool.wait_ge(gs_read, h * (PQ + SEQS) + PQ)
                pool.dma_start(io["gla_p"][0, 0, h], g_state).then_inc(gla_state_out, 16)
                pool.wait_ge(gs_read, (h + 1) * (PQ + SEQS))
                pool.dma_start(io["gla_s"][0, :, h].rearrange("s d v -> d s v"), g_sst).then_inc(gla_state_out, 16)
            pool.wait_ge(go_read, GH * NTILE)
            pool.wait_ge(gla_state_out, 32 * GH)
            zero_pads()
            ffn(1)
            for t in range(NTILE):
                n = TILES[t][1]
                pool.wait_ge(ln_done, 3 * NTILE + t + 1)
                dst = (io["y_prompt"][0, t * P:(t + 1) * P, :] if t < PQ
                       else io["y_sample"].rearrange("s t c -> (s t) c"))
                pool.dma_start(dst, x_tok[0:n, t, :]).then_inc(y_stored, 16)
            pool.wait_ge(y_stored, 16 * NTILE)
            pool.wait_ge(tail_stored, 64)
            pool.wait_ge(gla_state_out, 32 * GH)
            for i in range(ROPED):
                pool.wait_ge(k_stored[i], stores_[i])
            pool.wait_ge(v_stored, V_STORES)
            pool.wait_ge(kv_stored, 48)


_INS = ["x_prompt", "x_sample", "cache_moba_kv", "state_swa0_kv", "state_swa1_kv", "state_swa2_kv", "state_gla",
        "state_ffn_conv", "page_table", "attn_w_in", "attn_w_out", "gla_w_in", "gla_w_a1", "gla_w_a2", "gla_b_a",
        "gla_norm_g", "gla_w_out", "ln_mix_g", "ln_mix_b", "ffn_w_up", "ffn_conv_w", "ffn_conv_b", "ffn_w_down",
        "ln_ffn_g", "ln_ffn_b"]
_OUTS = [("y_prompt", (1, 512, 1024)), ("y_sample", (8, 8, 1024)),
         ("moba_p", (1, 1, 512, 2, 4, 64)), ("moba_s", (1, 8, 8, 2, 4, 64)),
         ("swa0_p", (1, 1, 128, 2, 4, 64)), ("swa0_s", (1, 8, 128, 2, 4, 64)),
         ("swa1_p", (1, 1, 512, 2, 4, 64)), ("swa1_s", (1, 8, 256, 2, 4, 64)),
         ("swa2_p", (1, 1, 512, 2, 4, 64)), ("swa2_s", (1, 8, 256, 2, 4, 64)),
         ("gla_p", (1, 1, 4, 128, 256)), ("gla_s", (1, 8, 4, 128, 256)),
         ("ffn_p", (2, 1, 2, 5632)), ("ffn_s", (2, 8, 2, 5632))]


def shape_constants():
    import numpy as np

    past_len, theta, off = 256, 10000.0, -1.0e30
    half = HD // 2
    inv = np.float32(theta) ** (-np.arange(half, dtype=np.float32) / np.float32(half))
    cos, sin = np.zeros((P, NTILE, HD), np.float32), np.zeros((P, NTILE, HD), np.float32)
    for t, (first, n) in enumerate(TILES):
        pos = (first + np.arange(n)) if t < PQ else past_len + np.arange(n) % T_NEW
        ang = pos.astype(np.float32)[:, None] * inv[None, :]
        cos[:n, t] = np.concatenate([np.cos(ang), np.cos(ang)], 1)
        sin[:n, t] = np.concatenate([-np.sin(ang), np.sin(ang)], 1)

    i, past = np.arange(P)[:, None], np.arange(-3 * P, P)[None, :]
    causal = past <= i
    window = (past <= i) & (i - past <= 128)
    groups = [causal, window[:, 2 * P:], causal & ((i - past) % 4 == 0), causal & ((i - past) % 16 == 0)]
    prompt = np.where(np.concatenate(groups, 1), 0.0, off).astype(np.float32)

    sample = np.zeros((P, 2, S_COLS), np.float32)
    row = np.arange(P)
    s4, q = row // 32, row % T_NEW
    tok = np.arange(NS)
    for g in range(4):
        n = GROUP_PAST[g]
        dil = (1, 1, 4, 16)[g]
        back = n + q[:, None] - np.arange(n)[None, :]
        seen = (back % dil == 0) & ((back <= 128 * dil) | (g == 0))
        for tile in range(2):
            same = (tok // T_NEW)[None, :] == (4 * tile + s4)[:, None]
            ago = q[:, None] - (tok % T_NEW)[None, :]
            new = same & (ago >= 0) & (ago % dil == 0)
            sample[:, tile, GROUP_AT[g]:GROUP_AT[g] + n + NS] = np.where(np.concatenate([seen, new], 1), 0.0, off)

    level = np.zeros((P, NLEV + 1, P), np.int32)
    s, t = np.arange(P)[:, None], np.arange(P)[None, :]
    for l in range(NLEV):
        h = 1 << l
        level[:, l] = (s // (2 * h) == t // (2 * h)) & (s // h % 2 == 0) & (t // h % 2 == 1)
    level[:, NLEV] = s == t
    reset = np.ones((P, NT), np.float32)
    reset[:, 0:NP:P] = 0.0
    reset[:, NP:NT:T_NEW] = 0.0
    seq_of_row = (np.arange(NS)[:, None] // T_NEW == np.arange(SEQS)[None, :]).astype(np.float32)
    return {"ident": np.eye(P, dtype=np.float32), "rope_cos": cos, "rope_sin": sin, "prompt_masks": prompt,
            "sample_masks": sample, "level_masks": level, "scan_reset": reset, "seq_of_row": seq_of_row}


def kernel(**inputs):
    import numpy as np
    import concourse.bacc as bacc
    from concourse.bass_utils import run_bass_kernel_spmd

    nc = bacc.Bacc("TRN2", target_bir_lowering=False, num_devices=1)
    arrays, io = {}, {}
    given = {name: np.ascontiguousarray(inputs[name]) for name in _INS}
    for name, a in list(given.items()) + list(shape_constants().items()):
        arrays[f"in_{name}"] = a
        io[name] = nc.dram_tensor(f"in_{name}", a.shape, mybir.dt.from_np(a.dtype), kind="ExternalInput").ap()
    for name, shape in _OUTS:
        io[name] = nc.dram_tensor(f"out_{name}", shape, F32, kind="ExternalOutput").ap()
    build_program(nc, io)
    r = run_bass_kernel_spmd(nc, [arrays], core_ids=[0])
    return tuple(r.results[0][f"out_{name}"] for name, _ in _OUTS)
```

```python
from contextlib import ExitStack

import concourse.bass as bass
from concourse import mybir

F32 = mybir.dt.float32
F32R = mybir.dt.float32r
I32 = mybir.dt.int32
U8 = mybir.dt.uint8
ALU = mybir.AluOpType
ACT = mybir.ActivationFunctionType
AXX = mybir.AxisListType.X

P = 128
D = 1024
KD = D // P
NP = 512
SEQS, T_NEW = 8, 8
NS = SEQS * T_NEW
NT = NP + NS
TILES = [(0, P), (P, P), (2 * P, P), (3 * P, P), (NP, NS)]
NTILE = len(TILES)
PQ = NP // P
HALF = 512
SPLIT = NT // 2
PRE = NP - SPLIT
HD = 64
PAGE = 128
DFF = 2816
NJ = DFF // P
DOWN_GROUPS = [(k0, min(4, NJ - k0)) for k0 in range(0, NJ, 4)]
SIDE = 2 * SEQS + 4
UP_RUNS = [(1, 0), (0, 0), (1, 1), (0, 1)]
TAIL = 2 + 2 * SEQS
ALPHA = (2.0 * 2) ** 0.25
LN_EPS = 1e-5
RMS_EPS = 1e-6
ATT_SCALE = HD ** -0.5
GH, GK, GV = 4, 128, 256
NLEV = 7
TAU = 16.0
LOWEST = -3.0e38

GROUP_PAST = [256, 128, 256, 256]
GROUP_AT = [0, 320, 512, 832]
S_COLS = 1152
CACHE_BLOCK = [0, 2, 3, 5]
NBLK = 7
KEY_BLOCKS = []
for g_ in range(4):
    for b_ in range(GROUP_PAST[g_] // P):
        KEY_BLOCKS.append((GROUP_AT[g_] + b_ * P, P, g_, CACHE_BLOCK[g_] + b_))
    KEY_BLOCKS.append((GROUP_AT[g_] + GROUP_PAST[g_], NS, g_, None))

UNIT = 2048
UNITS = ([("attn_in", c, NTILE) for c in range(12)] + [("attn_out", c, NTILE) for c in range(2)]
         + [("up0", j, 4) for j in range(NJ)] + [("down0", c, NTILE) for c in range(2 * len(DOWN_GROUPS))]
         + [("gla_qk", c, 4) for c in range(4)] + [("gla_a1", 0, 2)] + [("gla_vr", c, NTILE) for c in range(8)]
         + [("gla_out", c, NTILE) for c in range(4)]
         + [("up1", j, 4) for j in range(NJ)] + [("down1", c, NTILE) for c in range(2 * len(DOWN_GROUPS))])
UNIT_NO = {(k, c): n for n, (k, c, _) in enumerate(UNITS)}
STEPS_BEFORE = [sum(s for _, _, s in UNITS[:n]) for n in range(len(UNITS) + 1)]
LOADS = 2


def steps_at(kind, c, t):
    return STEPS_BEFORE[UNIT_NO[(kind, c)]] + t + 1


PAIR = [(0, 0), (0, 1), (1, 0), (0, 2), (1, 1), (0, 3), (1, 2), (0, 4), (1, 3), (1, 4)]
NORM_UNITS = []
for k_, n_ in (("attn_out", 2), ("down0", 2 * len(DOWN_GROUPS)), ("gla_out", 4), ("down1", 2 * len(DOWN_GROUPS))):
    NORM_UNITS.append([UNIT_NO[(k_, c_)] for c_ in range(n_)])
PAIRED = {units_[-2] for units_ in NORM_UNITS}


def freed(n):
    return STEPS_BEFORE[n] + PAIR.index((0, NTILE - 1)) + 1 if n in PAIRED else STEPS_BEFORE[n + 1]


def norm_steps(stage):
    m = len(NORM_UNITS[stage])
    return [(c, t) for c in range(m - 2) for t in range(NTILE)] + [(m - 2 + a, t) for a, t in PAIR]


def norm_sums(stage):
    per_half = len(NORM_UNITS[stage]) // 2
    return [(c // per_half, t) for c, t in norm_steps(stage) if c % per_half == per_half - 1]


def unit_width(n):
    kind, c, _ = UNITS[n]
    if kind in ("down0", "down1"):
        return DOWN_GROUPS[c % len(DOWN_GROUPS)][1] * HALF
    return KD * P if kind == "gla_a1" else UNIT


LEV_WITH_SAMPLE = [l < 3 or l == NLEV for l in range(NLEV + 1)]
LEV_BEFORE = [sum(1 + w for w in LEV_WITH_SAMPLE[:l]) for l in range(NLEV + 2)]
LEV_ALL = LEV_BEFORE[-1]
LEV_FIRST = 6
HEAD_STEPS = PQ + SEQS


def levels_done(m):
    h, l = divmod(m, NLEV + 1)
    return h * LEV_ALL + LEV_BEFORE[l + 1]


def decayed_of(m):
    h, l = divmod(m, NLEV + 1)
    return None if l == NLEV else h * NLEV + l


LEVEL_STEPS = GH * (NLEV + 1)


def pieces_of(t, g):
    return g != 1 or t >= PQ - 1


ROPED = 3
K_STORES, stores_ = [], [0] * ROPED
for r_ in range(4 * NTILE):
    c_, t_ = divmod(r_, NTILE)
    stores_[r_ % ROPED] += 16 * sum(pieces_of(t_, 2 * (c_ - 2) + half_) for half_ in range(2)) if c_ >= 2 else 0
    K_STORES.append(stores_[r_ % ROPED])
V_STORES = 16 * sum(pieces_of(t_, g_) for t_ in range(NTILE) for g_ in range(4))


class Count:

    def __init__(self, sem):
        self.sem, self.n = sem, 0

    def one(self):
        self.n += 1
        return 1


def build_program(nc, io):
    with ExitStack() as ctx:
        def sb(name, shape, dt=F32):
            return ctx.enter_context(nc.sbuf_tensor(name, shape, dt))

        def sem(name):
            return ctx.enter_context(nc.semaphore(name))

        SBUF_FIRST = 16512

        def at_place(name, shape, first, dt=F32):
            return nc.alloc_sbuf_tensor_at(name, shape, dt, offset=SBUF_FIRST + 4 * first)

        SLOT = NT + NS
        x_reg = at_place("x_reg", [P, NTILE * D], 0)
        xh_reg = at_place("xh_reg", [P, KD * SLOT], 5120, F32R)
        xl_reg = at_place("xl_reg", [P, KD * SLOT], 10240, F32R)
        raw = at_place("raw", [P, 2, UNIT], 15360)
        w_hi = at_place("w_hi", [P, 2, UNIT], 19456, F32R)
        w_lo = at_place("w_lo", [P, 2, UNIT], 23552, F32R)
        ident = at_place("ident", [P, P], 27648)
        ln_stats = at_place("ln_stats", [P, NTILE, 2, 6], 27776)
        ln_mv = at_place("ln_mv", [P, NTILE, 2], 27840)
        ln_sd = at_place("ln_sd", [P, NTILE, 2], 27856)
        eps_ln = at_place("eps_ln", [P, 2], 27872)
        page_ids = at_place("page_ids", [1, 16], 27880, I32)
        arena = at_place("arena", [P, 24592], 27904)
        attn_side = at_place("attn_side", [P, 4 * SLOT], 5120 + 4 * SLOT)
        attn_side2 = at_place("attn_side2", [P, 4 * SLOT], 10240 + 4 * SLOT)
        gla_side = at_place("gla_side", [P, 2 * KD * SLOT], 5120)
        v_cache_reg = at_place("v_cache_reg", [P, 4 * NBLK * 256], 19456)
        ps = ctx.enter_context(nc.psum_tensor("ps", [P, 8, HALF], F32))
        TURN = (5, 6)

        x_tok = x_reg[:, :].rearrange("p (t c) -> p t c", t=NTILE)
        xTh = xh_reg[:, :].rearrange("p (k n) -> p k n", k=KD)
        xTl = xl_reg[:, :].rearrange("p (k n) -> p k n", k=KD)

        def cut(region, at, n):
            return region[:, at:at + n]

        gb = cut(arena, 21560, 2 * D).rearrange("p (a c) -> p a c", a=2)

        v_tok = cut(arena, 0, 5120).rearrange("p (t c) -> p t c", t=NTILE)
        qkT = cut(arena, 5120, 16 * NT).rearrange("p (c n) -> p c n", c=16)
        v_cache = v_cache_reg[:, :].rearrange("p (s b c) -> p s b c", s=4, b=NBLK)
        masks = cut(arena, 14336, 1792)
        MASK_AT = [0, 512, 768, 1280]
        s_buf = cut(arena, 16128, 3584).rearrange("p (b c) -> p b c", b=2)

        def score_at(qi, g):
            width = (qi + 1) * P
            return [0, 512, 512 + min(width, 256), 512 + min(width, 256) + width][g]

        small = cut(arena, 19712, 216)
        mx = small[:, 0:64].rearrange("p (n g) -> p n g", g=4)
        mb = small[:, 64:96].rearrange("p (n g) -> p n g", g=2)
        nm = small[:, 96:128].rearrange("p (n g) -> p n g", g=2)
        den = small[:, 128:160].rearrange("p (n g) -> p n g", g=2)
        rden = small[:, 160:192].rearrange("p (n g) -> p n g", g=2)
        smx = small[:, 192:200].rearrange("p (n g) -> p n g", g=4)
        smb = small[:, 200:204].rearrange("p (n g) -> p n g", g=2)
        snm = small[:, 204:208].rearrange("p (n g) -> p n g", g=2)
        sden = small[:, 208:212].rearrange("p (n g) -> p n g", g=2)
        srd = small[:, 212:216].rearrange("p (n g) -> p n g", g=2)
        rope_a = cut(arena, 16128, 512)
        rope_b = cut(arena, 16640, 512)
        roped_buf = cut(arena, 17152, 1536).rearrange("p (b c) -> p b c", b=3)
        cos_t = cut(arena, 18688, 320).rearrange("p (t c) -> p t c", t=NTILE)
        sin_t = cut(arena, 19008, 320).rearrange("p (t c) -> p t c", t=NTILE)
        k_stage = [region.rearrange("p (b c) -> p b c", b=NBLK)
                   for region in (cut(x_reg, 0, NBLK * 256), cut(arena, 22016, NBLK * 256))]
        pT = cut(x_reg, 1792, 14 * P).rearrange("p (b c) -> p b c", b=14)
        s_mask = cut(x_reg, 3584, S_COLS)
        kcT = [cut(region, 0, 14 * P).rearrange("p (a c) -> p a c", a=14) for region in (attn_side, attn_side2)]
        o_tok = cut(attn_side, 14 * P, 512)
        qz_reg = cut(arena, 19968, 2048)
        qz = qz_reg.rearrange("p (c s h q) -> p c s h q", c=8, s=SEQS, h=4)

        hT = cut(arena, 0, NJ * NT).rearrange("p (j n) -> p j n", j=NJ)
        side = cut(arena, 12672, 2 * DFF)
        feat = cut(arena, 18304, 2 * NJ * SIDE).rearrange("p (v j r) -> p v j r", v=2, j=NJ)
        ext = cut(arena, 19184, 4 * 514).rearrange("p (u v n) -> p u v n", u=2, v=2)
        ext_s = cut(arena, 21240, 320).rearrange("p (u v s n) -> p u v s n", u=2, v=2, s=SEQS)
        conv_y = cut(arena, 21560, 4 * NT).rearrange("p (u v n) -> p u v n", u=2, v=2)
        fj = cut(arena, 23864, 2 * 2 * SIDE).rearrange("p (u v r) -> p u v r", u=2, v=2)
        tl = cut(arena, 23944, 4 * TAIL).rearrange("p (u v r) -> p u v r", u=2, v=2)

        g_v = cut(arena, 0, 5120).rearrange("p (t c) -> p t c", t=NTILE)
        g_r = cut(arena, 5120, 5120).rearrange("p (t c) -> p t c", t=NTILE)
        g_q = cut(arena, 10240, GH * NT).rearrange("p (h n) -> p h n", h=GH)
        g_k = cut(arena, 12544, GH * NT).rearrange("p (h n) -> p h n", h=GH)
        g_b = cut(arena, 14848, GH * NT).rearrange("p (h n) -> p h n", h=GH)
        g_tmp = cut(arena, 21560, GH * NT)
        lev_e = cut(arena, 17152, 2 * NT).rearrange("p (b n) -> p b n", b=2)
        att = [cut(arena, at, NT) for at in (18304, 18880, 20064, 20640)]
        from_start = [lev_e[:, i] for i in range(2)]
        to_end = cut(arena, 24016, NT)
        lev_q = cut(arena, 21560, 2 * NT).rearrange("p (b n) -> p b n", b=2)
        lev_k = cut(arena, 22712, 2 * NT).rearrange("p (b n) -> p b n", b=2)
        g_mask = cut(arena, 19456, (NLEV + 1) * P // 4).bitcast(U8).rearrange("p (l c) -> p l c", l=NLEV + 1)
        mask_words = cut(arena, 17152, (NLEV + 1) * P).bitcast(I32).rearrange("p (l c) -> p l c", l=NLEV + 1)
        g_small = cut(arena, 19712, 64)
        g_ss = g_small[:, 0:20].rearrange("p (t h) -> p t h", t=NTILE)
        g_rs = g_small[:, 20:40].rearrange("p (t h) -> p t h", t=NTILE)
        g_ba = g_small[:, 40:44]
        g_norm = cut(arena, 19776, GV)
        seq_of_row = cut(arena, 20032, SEQS)[0:NS, :]
        g_reset = cut(arena, 20064, NT)
        g_a2 = cut(arena, 20640, 512)
        g_t1 = cut(arena, 18304, NT)
        def pair_of(at, n):
            return [cut(gla_side, at + i * n, n) for i in range(2)]

        g_qb = pair_of(0, NT)
        g_kb = pair_of(1152, NT)
        g_kt = [x.rearrange("p (t c) -> p t c", t=NTILE) for x in pair_of(2304, NTILE * P)]
        qz_places = pair_of(3584, SEQS * (NS + T_NEW))
        g_qz = [x[:, 0:SEQS * NS].rearrange("p (s n) -> p s n", s=SEQS) for x in qz_places]
        g_qz_own = [x.rearrange("p (s n) -> p s n", s=SEQS)[:, :, 0:T_NEW] for x in qz_places]
        g_kz = [x.rearrange("p (s n) -> p s n", s=SEQS) for x in pair_of(4736, SEQS * P)]
        g_state = pair_of(6784, GV)
        g_sst = [x.rearrange("p (s n) -> p s n", s=SEQS)
                 for x in (cut(gla_side, 7296, SEQS * GV), cut(arena, 21560, SEQS * GV))]
        squares = cut(gla_side, 9344, GV)
        gb_of = [gb, gb, cut(arena, 10240, 2 * D).rearrange("p (a c) -> p a c", a=2), gb]

        x_loaded = [sem(f"x_loaded{t}") for t in range(NTILE)]
        masks_loaded = sem("masks_loaded")
        consts_loaded = sem("consts_loaded")
        pages_loaded = sem("pages_loaded")
        raw_loaded = [sem(f"raw_loaded{i}") for i in range(2)]
        hi_done = sem("hi_done")
        lo_done = sem("lo_done")
        h_hi = sem("h_hi")
        h_lo = sem("h_lo")
        x_lo = sem("x_lo")
        pad_zero = sem("pad_zero")
        steps = sem("steps")
        turned = sem("turned")
        turned_out = sem("turned_out")
        vec = sem("vec")
        qk_read = sem("qk_read")
        roped = sem("roped")
        v_stored = sem("v_stored")
        qz_zero = sem("qz_zero")
        v_read = sem("v_read")
        k_stored = [sem(f"k_stored{i}") for i in range(ROPED)]
        kv_stored = sem("kv_stored")
        s_ready = sem("s_ready")
        s_read = sem("s_read")
        nm_ready = sem("nm_ready")
        probs = sem("probs")
        pv_done = sem("pv_done")
        o_ready = sem("o_ready")
        qz_ready = sem("qz_ready")
        k_cached = [sem(f"k_cached{i}") for i in range(2)]
        v_cached = sem("v_cached")
        smask_loaded = sem("smask_loaded")
        sc_done = sem("sc_done")
        so_scaled = sem("so_scaled")
        spv_done = sem("spv_done")
        so_turned = sem("so_turned")
        soT_ready = sem("soT_ready")
        x_again = sem("x_again")
        gb_loaded = sem("gb_loaded")
        z_read = sem("z_read")
        ln_var = sem("ln_var")
        ln_root = sem("ln_root")
        ln_done = sem("ln_done")
        side_loaded = sem("side_loaded")
        pads_zero = sem("pads_zero")
        ext_ready = sem("ext_ready")
        conv_step = sem("conv_step")
        silu_done = sem("silu_done")
        tail_ready = sem("tail_ready")
        tail_turned = sem("tail_turned")
        tail_out = sem("tail_out")
        tail_stored = sem("tail_stored")
        gla_loaded = sem("gla_loaded")
        gla_state_in = [sem(f"gla_state_in{i}") for i in range(2)]
        p_state_out = sem("p_state_out")
        s_state_out = [sem(f"s_state_out{i}") for i in range(2)]
        decays = sem("decays")
        end_diff = sem("end_diff")
        fm_read = sem("fm_read")
        low_filled = sem("low_filled")
        gates = sem("gates")
        tok_read = sem("tok_read")
        r_scaled = sem("r_scaled")
        lev_diff = sem("lev_diff")
        lev_exp = sem("lev_exp")
        lev_ready = sem("lev_ready")
        lev_prod = sem("lev_prod")
        lev_read = sem("lev_read")
        kz_ready = sem("kz_ready")
        go_done = sem("go_done")
        gs_done = sem("gs_done")
        sq_done = sem("sq_done")
        go_read = sem("go_read")
        gs_read = sem("gs_read")
        y_ready = sem("y_ready")
        y_stored = sem("y_stored")

        TURNS_X = 2 * NTILE
        TURNS_QK = 4 * NTILE
        P_BLOCKS = [(qi + 1) + min(qi + 1, 2) + 2 * (qi + 1) for qi in range(PQ)]
        P_BATCH = [-(-b // 4) for b in P_BLOCKS]
        UP0 = TURNS_X + TURNS_QK
        K_BATCH = 4
        SP_BATCH = -(-len(KEY_BLOCKS) // 4)
        BATCH_BEFORE_SAMPLE = UP0 + 4 * sum(P_BATCH) + PQ
        BATCH_LN0 = BATCH_BEFORE_SAMPLE + 2 * (4 * K_BATCH + SP_BATCH) + 2
        BATCH_LN1 = BATCH_LN0 + TURNS_X
        BATCH_GLA = BATCH_LN1 + TURNS_X
        BATCH_Y = BATCH_GLA + 2 * GH
        BATCH_LN2 = BATCH_Y + TURNS_X + 2
        BATCH_O = [UP0 + 4 * sum(P_BATCH[:qi + 1]) + qi for qi in range(PQ)]
        LO_BATCHES = ([b for b in range(TURNS_X)] + BATCH_O
                      + [b0 + b for b0 in (BATCH_LN0, BATCH_LN1, BATCH_Y, BATCH_LN2) for b in range(TURNS_X)])

        def keys_turned(s):
            return BATCH_BEFORE_SAMPLE + (s + 1) * K_BATCH + (SP_BATCH if s > 5 else 0)

        def h_count(l, c, t):
            before = l * (2 * len(DOWN_GROUPS) + NTILE - 1)
            return before + (t + 1 if c == 0 else c + NTILE)

        block = ctx.enter_context(nc.Block())

        def unit_source(n):
            kind, c, _ = UNITS[n]
            if kind in ("attn_in", "gla_vr", "gla_out"):
                w = {"attn_in": io["attn_w_in"], "gla_vr": io["gla_w_in"], "gla_out": io["gla_w_out"]}[kind][0]
                k0, kn, c0, cn = c % 2 * 4, 4, (c // 2 + (2 if kind == "gla_vr" else 0)) * HALF, HALF
            elif kind == "attn_out":
                w, k0, kn, c0, cn = io["attn_w_out"][0], 0, 4, c * HALF, HALF
            elif kind in ("down0", "down1"):
                w = io["ffn_w_down"][int(kind[-1])]
                (k0, kn), c0, cn = DOWN_GROUPS[c % len(DOWN_GROUPS)], c // len(DOWN_GROUPS) * HALF, HALF
            elif kind == "gla_qk":
                w, k0, kn, c0, cn = io["gla_w_in"][0], 0, KD, c * 2 * P, 2 * P
            else:
                w, k0, kn, c0, cn = io["gla_w_a1"][0], 0, KD, 0, 16
            src = w[k0 * P:(k0 + kn) * P, c0:c0 + cn].rearrange("(k p) c -> p k c", p=P)
            dst = raw[:, n % 2, 0:unit_width(n)].rearrange("p (k c) -> p k c", k=kn)[:, :, 0:cn]
            return [(dst[:, a:a + kn // 2, :], src[:, a:a + kn // 2, :]) for a in (0, kn // 2)]

        def of_unit(w, n, kn):
            return w[:, n % 2, 0:unit_width(n)].rearrange("p (k c) -> p k c", k=kn)

        @block.sync
        def _(sp):
            def load_unit(n):
                if n >= 2:
                    sp.wait_ge(lo_done, n - 1)
                for dst, src in unit_source(n):
                    sp.dma_start(dst, src).then_inc(raw_loaded[n % 2], 16)

            for t in range(NTILE):
                n = TILES[t][1]
                src = io["x_prompt"][0, t * P:(t + 1) * P, :] if t < PQ else io["x_sample"].rearrange("s t c -> (s t) c")
                sp.dma_start(x_tok[0:n, t, :], src).then_inc(x_loaded[t], 16)
                if t == 1:
                    load_unit(0)
            load_unit(1)
            sp.dma_start(page_ids[:, :], io["page_table"].rearrange("s (g o) -> o (s g)", o=1)).then_inc(pages_loaded, 16)
            for n in range(2, 14):
                load_unit(n)
            sp.wait_ge(turned, TURNS_X)
            sp.dma_start(s_mask, io["sample_masks"][:, 0, :]).then_inc(smask_loaded, 16)
            sp.wait_ge(pages_loaded, 16)

            def cache_rows(s, what):
                def to(b, n):
                    return k_stage[s % 2][:, b:b + n, :] if what == 0 else v_cache[:, s % 4, b:b + n, :]
                done = k_cached[s % 2] if what == 0 else v_cached
                if what == 0 and s >= 2:
                    sp.wait_ge(turned, keys_turned(s - 2))
                for pg in range(2):
                    page = sp.value_load(page_ids[0:1, 2 * s + pg:2 * s + pg + 1], min_val=0,
                                         max_val=io["cache_moba_kv"].shape[1] - 1)
                    src = io["cache_moba_kv"][0, bass.ds(page, 1), :, what].rearrange("o r h d -> r o (h d)")
                    sp.dma_start(to(pg, 1), src).then_inc(done, 16)
                for g in range(3):
                    src = io[f"state_swa{g}_kv"][0, s, :, what].rearrange("(b r) h d -> r b (h d)", r=P)
                    sp.dma_start(to(CACHE_BLOCK[g + 1], GROUP_PAST[g + 1] // P), src).then_inc(done, 16)

            for s in range(2):
                cache_rows(s, 0)
            sp.wait_ge(steps, STEPS_BEFORE[12])
            for s in range(4):
                cache_rows(s, 1)
            for g in range(3):
                rows = io[f"state_swa{g}_kv"].shape[2]
                sp.dma_start(io[f"swa{g}_s"][0, :, 0:rows - T_NEW].rearrange("s r a h d -> s (r a h d)"),
                             io[f"state_swa{g}_kv"][0, :, T_NEW:rows].rearrange("s r a h d -> s (r a h d)")).then_inc(kv_stored, 16)
            for s in range(2, SEQS):
                cache_rows(s, 0)
            sp.wait_ge(s_read, 16 * 4 + 4)
            sp.dma_start(s_mask, io["sample_masks"][:, 1, :]).then_inc(smask_loaded, 16)
            sp.wait_ge(spv_done, 1)
            for s in range(4, SEQS):
                cache_rows(s, 1)
            sp.wait_ge(spv_done, 2)
            sp.dma_start(x_tok[:, 0:PQ, :], io["x_prompt"][0].rearrange("(t p) c -> p t c", p=P)).then_inc(x_again, 16)
            sp.dma_start(x_tok[0:NS, PQ, :], io["x_sample"].rearrange("s t c -> (s t) c")).then_inc(x_again, 16)

            def load_ln(n, which, l):
                for a, v in enumerate((io[f"ln_{which}_g"], io[f"ln_{which}_b"])):
                    sp.dma_start(gb_of[n][:, a, :], v[l:l + 1, :].partition_broadcast(P)
                                 .rearrange("q o c -> q (o c)")).then_inc(gb_loaded, 16)

            def ffn_up(l):
                for a, (r0, rn, src) in enumerate((
                        (0, 2 * SEQS, io["state_ffn_conv"][l].rearrange("s r c -> (s r) c")),
                        (2 * SEQS, 3, io["ffn_conv_w"][l]),
                        (2 * SEQS + 3, 1, io["ffn_conv_b"][l:l + 1, :]))):
                    sp.dma_start(side[r0:r0 + rn, :], src).then_inc(side_loaded, 16)
                base = UNIT_NO[(f"up{l}", 0)]
                with sp.Fori(0, NJ // 2) as i:
                    for u in range(2):
                        sp.wait_ge(lo_done, i * 2 + (base + u - 1))
                        slot = (base + u) % 2
                        place = raw[:, slot, :].rearrange("p (v k c) -> p v k c", v=2, k=KD)
                        for v in range(2):
                            src = (io["ffn_w_up"][l].rearrange("(k p) c -> p k c", p=P)
                                   [:, :, bass.ds((i * 2 + u) * P + v * DFF, P)])
                            sp.dma_start(place[:, v, :, :], src).then_inc(raw_loaded[slot], 16)

            def ffn_down(l, extra):
                base = UNIT_NO[(f"down{l}", 0)]
                load_unit(base)
                load_unit(base + 1)
                sp.wait_ge(conv_step, (l + 1) * NJ * 13)
                load_ln(2 * l + 1, "ffn", l)
                for n in range(base + 2, base + 12 + extra):
                    load_unit(n)

            sp.wait_ge(soT_ready, 2)
            load_ln(0, "mix", 0)
            ffn_up(0)
            ffn_down(0, 2)
            sp.wait_ge(tail_stored, 32)
            sp.dma_start(mask_words, io["level_masks"]).then_inc(gla_loaded, 16)
            with nc.allow_non_contiguous_dma(reason="512 biases, feature-major"):
                sp.dma_start(g_ba, io["gla_b_a"][0].rearrange("(h d o) -> d h o", h=GH, o=1).rearrange("d h o -> d (h o)")).then_inc(gla_loaded, 16)
            sp.dma_start(g_a2[0:16, :], io["gla_w_a2"][0]).then_inc(gla_loaded, 16)
            sp.dma_start(g_reset, io["scan_reset"]).then_inc(gla_loaded, 16)
            sp.dma_start(g_norm, io["gla_norm_g"][0:1, :].partition_broadcast(P).rearrange("q o c -> q (o c)")).then_inc(gla_loaded, 16)
            sp.dma_start(seq_of_row, io["seq_of_row"]).then_inc(gla_loaded, 16)
            out = UNIT_NO[("gla_out", 0)]
            for n in range(UNIT_NO[("gla_qk", 2)], out + 2):
                load_unit(n)
            for h in range(GH):
                if h == 0:
                    sp.wait_ge(steps, STEPS_BEFORE[out])
                elif h == 1:
                    sp.wait_ge(lev_prod, GH * LEV_ALL)
                else:
                    sp.wait_ge(s_state_out[h % 2], 16)
                sp.dma_start(g_sst[h % 2], io["state_gla"][0, :, h].rearrange("s d v -> d s v")).then_inc(gla_state_in[h % 2], 16)
                if h == 1:
                    load_unit(out + 2)
                    load_unit(out + 3)
            sp.wait_ge(kz_ready, 3 * GH)
            load_ln(2, "mix", 1)
            sp.wait_ge(go_done, GH * NTILE)
            sp.wait_ge(gs_read, GH * HEAD_STEPS)
            sp.wait_ge(go_read, GH * NTILE)
            ffn_up(1)
            ffn_down(1, 0)

        @block.tensor
        def _(pe):
            batch = Count(turned)

            def turn(pieces):
                bank = TURN[batch.n % 2]
                if batch.n >= 2:
                    pe.wait_ge(turned_out, batch.n - 1)
                if batch.n - 2 in LO_BATCHES:
                    pe.wait_ge(x_lo, LO_BATCHES.index(batch.n - 2) + 1)
                for col, src in pieces:
                    rows, cols = src.shape
                    last = pe.transpose(ps[0:cols, bank, col:col + rows], src, ident[0:rows, 0:rows])
                last.then_inc(turned, batch.one())

            def turn_x(t):
                r0, n = TILES[t]
                for half in range(2):
                    turn([(j * P, x_tok[0:n, t, (half * 4 + j) * P:(half * 4 + j + 1) * P]) for j in range(4)])

            def unit_here(n):
                pe.wait_ge(lo_done, n + 1)

            def lo_here(stage_batch, n):
                pe.wait_ge(x_lo, LO_BATCHES.index(stage_batch) + n)

            def three_products(out, lhs, rhs, ks, first, last):
                for i in range(ks):
                    for a, b in ((0, 0), (0, 1), (1, 0)):
                        mm = pe.matmul(out, lhs(i, a), rhs(i, b), start=first and i == 0 and a + b == 0,
                                       stop=last and i == ks - 1 and a == 1)
                return mm

            def project(n, t, k0, kn, first, last):
                parts = xTh, xTl
                w = of_unit(w_hi, n, kn), of_unit(w_lo, n, kn)
                three_products(ps[:, t, :], lambda i, a: parts[a][:, k0 + i, t * P:(t + 1) * P],
                               lambda i, b: w[b][:, i, :], kn, first, last).then_inc(steps, 1)

            pe.wait_ge(consts_loaded, 16)
            for t in range(NTILE):
                pe.wait_ge(x_loaded[t], 16)
                turn_x(t)

            def turn_rope(r):
                c, t = divmod(r, NTILE)
                n = TILES[t][1]
                pe.wait_ge(roped, r + 1)
                turn([(j * P, roped_buf[0:n, r % 3, j * P:(j + 1) * P]) for j in range(4)])

            pe.wait_ge(pad_zero, 2)
            for n in range(12):
                c, late = divmod(n, 2)
                unit_here(n)
                for t in range(NTILE):
                    if n == 0:
                        pe.wait_ge(turned_out, 2 * t + 2)
                        lo_here(0, 2 * t + 2)
                    elif not late and c <= 4:
                        pe.wait_ge(qk_read, (c - 1) * NTILE + t + 1)
                    elif not late:
                        pe.wait_ge(v_read, t + 1)
                    project(n, t, 4 * late, 4, not late, bool(late))
                    r = c * NTILE + t - 2
                    if late == (t >= 2) and 0 <= r < 4 * NTILE:
                        turn_rope(r)

            def head_rows(g, h):
                return slice(HD * (h % 2), HD * (h % 2) + HD), 2 * g + h // 2

            def scores(n, groups=range(4)):
                qi, h = divmod(n, 4)
                for g in groups:
                    rows, c = head_rows(g, h)
                    k0 = max(0, qi - 1) * P if g == 1 else 0
                    if n >= 1:
                        pe.wait_ge(s_read, 4 * (n - 1) + g + 1)
                    elif g == 0:
                        pe.wait_ge(turned_out, UP0)
                        pe.wait_ge(qk_read, 4 * NTILE)
                        pe.wait_ge(v_read, 2 * NTILE)
                    pe.matmul(ps[:, g, 0:(qi + 1) * P - k0], qkT[rows, c, qi * P:(qi + 1) * P],
                              qkT[rows, 8 + c, k0:(qi + 1) * P], start=True, stop=True).then_inc(s_ready, 1)

            def prob_blocks(qi):
                out = []
                for g in range(4):
                    k0 = max(0, qi - 1) if g == 1 else 0
                    out += [(score_at(qi, g) + (kt - k0) * P, kt, g) for kt in range(k0, qi + 1)]
                return out

            def values(n):
                qi, h = divmod(n, 4)
                blocks = prob_blocks(qi)
                pe.wait_ge(probs, 2 * n + 2)
                for g in range(4):
                    if g < P_BATCH[qi]:
                        turn([(j * P, s_buf[:, n % 2, col:col + P]) for j, (col, _, _) in enumerate(blocks[4 * g:4 * g + 4])])
                    if n + 1 < 16:
                        scores(n + 1, [g])
                if n >= 2:
                    pe.wait_ge(o_ready, 2 * (n - 1))
                pe.wait_ge(turned_out, batch.n)
                bank = (4, 7)[n % 2]
                for merged in range(2):
                    mine = [i for i, b in enumerate(blocks) if (b[2] > 0) == bool(merged)]
                    for i in mine:
                        _, kt, g = blocks[i]
                        mm = pe.matmul(ps[:, bank, merged * P:merged * P + P], pT[:, i, :],
                                       v_tok[:, kt, (2 * g + h // 2) * P:(2 * g + h // 2 + 1) * P],
                                       start=i == mine[0], stop=i == mine[-1])
                mm.then_inc(pv_done, 1)

            def turn_o(qi):
                pe.wait_ge(o_ready, 8 * (qi + 1))
                turn([(j * P, o_tok[:, j * P:(j + 1) * P]) for j in range(4)])

            scores(0)
            for n in range(16):
                values(n)
                if n % 4 == 3:
                    turn_o(n // 4)

            def turn_keys(s):
                pe.wait_ge(k_cached[s % 2], 80 * (s // 2 + 1))
                for b0 in range(0, 14, 4):
                    turn([(j * P, k_stage[s % 2][:, (b0 + j) % NBLK, (b0 + j) // NBLK * P:(b0 + j) // NBLK * P + P])
                          for j in range(min(4, 14 - b0))])

            def sample_values(tile):
                pe.wait_ge(probs, 32 + 2 * tile + 2)
                pe.wait_ge(v_cached, 320 * (tile + 1))
                for b0 in range(0, len(KEY_BLOCKS), 4):
                    turn([(j * P, s_buf[:, 0, col:col + kn]) for j, (col, kn, _, _) in enumerate(KEY_BLOCKS[b0:b0 + 4])])
                pe.wait_ge(turned_out, batch.n)
                if tile == 0:
                    pe.wait_ge(o_ready, 32)
                else:
                    pe.wait_ge(so_scaled, 2)
                for merged in range(2):
                    mine = [i for i, b in enumerate(KEY_BLOCKS) if (b[2] > 0) == bool(merged)]
                    mine = [i for i in mine if KEY_BLOCKS[i][3] is None] + [i for i in mine if KEY_BLOCKS[i][3] is not None]
                    cols = slice(256 * merged, 256 * merged + 256)
                    for i in mine:
                        _, kn, g, cb = KEY_BLOCKS[i]
                        if cb is None:
                            mm = pe.matmul(ps[:, 4, cols], pT[0:NS, i, :], v_tok[0:NS, PQ, g * 256:g * 256 + 256],
                                           start=i == mine[0], stop=False, skip_group_check=True)
                            continue
                        for s4 in range(4):
                            rows = slice(32 * s4, 32 * s4 + 32)
                            mm = pe.matmul(ps[rows, 4, cols], pT[:, i, rows], v_cache[:, s4, cb, :], start=False,
                                           stop=i == mine[-1], skip_group_check=True, tile_position=(0, 32 * s4))
                mm.then_inc(spv_done, 1)
                if tile == 1:
                    pe.wait_ge(soT_ready, 1)
                pe.wait_ge(so_scaled, 2 * tile + 2)
                for j in range(4):
                    mm = pe.transpose(ps[:, 7, j * P:(j + 1) * P], o_tok[:, j * P:(j + 1) * P], ident[:, :])
                mm.then_inc(so_turned, 1)

            turn_keys(0)
            pe.wait_ge(qz_ready, 1)
            for s in range(SEQS):
                tile, s4 = divmod(s, 4)
                if s + 1 < SEQS:
                    turn_keys(s + 1)
                pe.wait_ge(turned_out, keys_turned(s))
                if s4 == 0:
                    pe.wait_ge(s_read, 64 + 4 * tile)
                for g in range(4):
                    rows = slice(32 * s4, 32 * s4 + 32)
                    past = GROUP_PAST[g]
                    for pair in range(2):
                        b = pair * NBLK + CACHE_BLOCK[g]
                        pe.matmul(ps[rows, g, 0:past], qz[:, 2 * g + pair, s].rearrange("p h q -> p (h q)"),
                                  kcT[s % 2][:, b:b + past // P, :].rearrange("p b c -> p (b c)"),
                                  start=pair == 0, stop=pair == 1, tile_position=(0, 32 * s4))
                    for pair in range(2):
                        mm = pe.matmul(ps[rows, g, past:past + NS], qz[:, 2 * g + pair, s].rearrange("p h q -> p (h q)"),
                                       qkT[:, 8 + 2 * g + pair, NP:NT],
                                       start=pair == 0, stop=pair == 1, tile_position=(0, 32 * s4))
                mm.then_inc(sc_done, 1)
                if s in (4, 7):
                    sample_values(s // 7)

            pe.wait_ge(soT_ready, 2)
            lo_here(BATCH_O[PQ - 1], 1)

            def turn_sides(l):
                pe.wait_ge(side_loaded, 48 * (l + 1))
                for v in range(2):
                    turn([(j * SIDE, side[0:SIDE, (v * NJ + j) * P:(v * NJ + j + 1) * P]) for j in range(NJ)])

            def products_before_norm(stage, groups, before_tile=None):
                sums = norm_sums(stage)
                for c, t in norm_steps(stage):
                    n = NORM_UNITS[stage][c]
                    half, g = divmod(c, len(groups(0)))
                    k0, kn = groups(c)[g]
                    unit_here(n)
                    if stage % 2 == 0 and (c, t) == norm_steps(stage)[-5]:
                        turn_sides(stage // 2)
                    if before_tile is not None:
                        before_tile(c, t)
                    if half == 1 and g == 0:
                        pe.wait_ge(z_read, 2 * stage * NTILE + sums.index((0, t)) + 1)
                    project(n, t, k0, kn, g == 0, g == len(groups(0)) - 1)

            products_before_norm(0, lambda c: [(0, 4)])

            def after_ln(stage, tiles):
                for t in tiles:
                    pe.wait_ge(ln_done, stage * NTILE + t + 1)
                    turn_x(t)

            def run_here(m, stage, first_batch):
                if m == 0:
                    after_ln(stage, range(3))
                    lo_here(first_batch, 6)
                elif m == 1:
                    after_ln(stage, [3])
                elif m == 2:
                    after_ln(stage, [4])
                    pe.wait_ge(turned_out, first_batch + TURNS_X)
                    lo_here(first_batch, TURNS_X)

            def ffn(l):
                base = UNIT_NO[(f"up{l}", 0)]
                parts = xTh, xTl

                def up(j, u, first):
                    slot = (base + u) % 2
                    w = [part[:, slot, :].rearrange("p (v k c) -> p v k c", v=2, k=KD) for part in (w_hi, w_lo)]
                    pe.wait_ge(lo_done, j + (base + 1))
                    for m, (v, run) in enumerate(UP_RUNS):
                        if not first:
                            pe.wait_ge(ext_ready, j * 4 + (l * NJ * 4 - 3 + m))
                        else:
                            run_here(m, 2 * l, BATCH_LN2 if l else BATCH_LN0)
                        three_products(ps[:, m, 0:SPLIT], lambda k, a: w[a][:, v, k, :],
                                       lambda k, b: parts[b][:, k, run * SPLIT:(run + 1) * SPLIT], KD, True, True).then_inc(steps, 1)

                def turn_tail(j, u, first):
                    pe.wait_ge(tail_ready, j + (l * NJ + 1))
                    if not first:
                        pe.wait_ge(tail_out, j + (l * NJ - 1))
                    for v in range(2):
                        mm = pe.transpose(ps[0:TAIL, TURN[u], v * P:v * P + P], tl[:, u, v, :], ident[:, :])
                    mm.then_inc(tail_turned, 1)

                up(0, 0, True)
                up(1, 1, False)
                turn_tail(0, 0, True)
                with pe.Fori(1, NJ // 2) as i:
                    up(i * 2, 0, False)
                    turn_tail(i * 2 - 1, 1, False)
                    up(i * 2 + 1, 1, False)
                    turn_tail(i * 2, 0, False)

                pe.wait_ge(ext_ready, (l + 1) * NJ * 4)
                pe.wait_ge(pad_zero, 4 + 2 * l)

                def rows_here(c, t):
                    pe.wait_ge(h_lo, h_count(l, c, t))
                    if (c, t) == (1, 0):
                        turn_tail(NJ - 1, 1, False)

                products_before_norm(2 * l + 1, lambda c: [(4 * (c % 2), kn) for _, kn in DOWN_GROUPS], rows_here)
                pe.wait_ge(tail_out, (l + 1) * NJ)

            ffn(0)

            fm = Count(fm_read)

            def fm_banks(i):
                return i % 2, 2 + i % 2

            def feature_major(i, kn, lhs, rhs, done, bias_free=True):
                a, b = fm_banks(i)
                for k in range(kn):
                    pe.matmul(ps[:, a, 0:SPLIT], lhs(k), rhs(k, 0, SPLIT), start=k == 0, stop=k == kn - 1)
                for k in range(kn):
                    mm = pe.matmul(ps[:, b, 0:SPLIT], lhs(k), rhs(k, SPLIT, NT), start=k == 0, stop=k == kn - 1)
                mm.then_inc(done, 1)

            parts = xTh, xTl
            for c in range(GH):
                n = UNIT_NO[("gla_qk", c)]
                unit_here(n)
                w = of_unit(w_hi, n, KD), of_unit(w_lo, n, KD)
                for run in range(2):
                    for a in range(2):
                        i = 2 * c + a
                        if c == 0:
                            run_here(2 * run + a, 1, BATCH_LN1)
                        elif run == 0:
                            pe.wait_ge(fm_read, i - 1)
                        three_products(ps[:, 2 * run + a, 0:SPLIT], lambda k, p: w[p][:, k, a * P:(a + 1) * P],
                                       lambda k, p: parts[p][:, k, run * SPLIT:(run + 1) * SPLIT], KD, True, True).then_inc(steps, 1)
            n = UNIT_NO[("gla_a1", 0)]
            unit_here(n)
            w = of_unit(w_hi, n, KD), of_unit(w_lo, n, KD)
            for run in range(2):
                three_products(ps[:, (4, 7)[run], 0:SPLIT], lambda k, a: w[a][:, k, :],
                               lambda k, b: parts[b][:, k, run * SPLIT:(run + 1) * SPLIT], KD, True, True).then_inc(steps, 1)
            pe.wait_ge(gla_loaded, 96)
            pe.wait_ge(fm_read, 2 * GH + 1)
            for h in range(GH):
                if h >= 2:
                    pe.wait_ge(fm_read, 2 * GH + h)
                feature_major(h, 1, lambda k: g_a2[0:16, h * P:(h + 1) * P], lambda k, a, b: g_t1[0:16, a:b], low_filled)
            pe.wait_ge(fm_read, 3 * GH + 1)
            def level_products(m):
                h, l = divmod(m, NLEV + 1)
                g = decayed_of(m)
                kk, qq = (g_k[:, h], g_q[:, h]) if g is None else (lev_k[:, g % 2], lev_q[:, g % 2])
                if m >= 2:
                    pe.wait_ge(lev_read, levels_done(m - 2))
                if g is not None:
                    pe.wait_ge(lev_ready, g + 1)
                for c in range(PQ):
                    mm = pe.matmul(ps[:, TURN[m % 2], c * P:(c + 1) * P], kk[:, c * P:(c + 1) * P], qq[:, c * P:(c + 1) * P],
                                   start=True, stop=True)
                mm.then_inc(lev_prod, 1)
                if LEV_WITH_SAMPLE[l]:
                    if m:
                        pe.wait_ge(lev_read, levels_done(m - 1))
                    pe.matmul(ps[0:NS, 7, 0:NS], kk[:, NP:NT], qq[:, NP:NT], start=True, stop=True).then_inc(lev_prod, 1)

            for i in range(8):
                c, late = divmod(i, 2)
                n = UNIT_NO[("gla_vr", i)]
                unit_here(n)
                for t in range(NTILE):
                    if c >= 1 and not late:
                        pe.wait_ge(tok_read, (c - 1) * NTILE + t + 1)
                    project(n, t, 4 * late, 4, not late, bool(late))
                    m = i * NTILE + t - LEV_FIRST
                    if 0 <= m < LEVEL_STEPS:
                        level_products(m)
            pe.wait_ge(tok_read, 4 * NTILE)
            pe.wait_ge(lev_read, GH * LEV_ALL)

            def turn_keys_of(h):
                pe.wait_ge(kz_ready, 3 * h + 1)
                turn([(c * P, g_kb[h % 2][:, c * P:(c + 1) * P]) for c in range(PQ)])
                turn([(0, g_kb[h % 2][:, NP:NT])])

            def state_product(h, i, lhs, rhs):
                n = h * HEAD_STEPS + i
                if n >= 4:
                    pe.wait_ge(gs_read, n - 3)
                pe.matmul(ps[:, n % 4, 0:GV], lhs, rhs, start=True, stop=True).then_inc(gs_done, 1)

            turn_keys_of(0)
            for h in range(GH):
                par = h % 2
                pe.wait_ge(turned_out, BATCH_GLA + 2 * h + 2)
                for c in range(PQ):
                    state_product(h, c, g_kt[par][:, c, :], g_v[:, c, h * GV:(h + 1) * GV])
                for c in range(PQ):
                    n = h * NTILE + c
                    if n >= 2:
                        pe.wait_ge(go_read, n - 1)
                    bank = (4, 7)[n % 2]
                    mm = pe.matmul(ps[:, bank, 0:GV], att[h][:, c * P:(c + 1) * P], g_v[:, c, h * GV:(h + 1) * GV],
                                   start=True, stop=c == 0)
                    if c >= 1:
                        pe.wait_ge(gs_read, h * HEAD_STEPS + c)
                        mm = pe.matmul(ps[:, bank, 0:GV], g_qb[par][:, c * P:(c + 1) * P], g_state[(c - 1) % 2],
                                       start=False, stop=True)
                    mm.then_inc(go_done, 1)
                n = h * NTILE + PQ
                pe.wait_ge(go_read, n - 1)
                bank = (4, 7)[n % 2]
                vv = g_v[0:NS, PQ, h * GV:(h + 1) * GV]
                pe.wait_ge(kz_ready, 3 * h + 3)
                pe.wait_ge(gla_state_in[par], 16 * (h // 2 + 1))
                pe.matmul(ps[0:NS, bank, 0:GV], att[h][0:NS, NP:NT], vv, start=True, stop=False)
                for s in range(SEQS):
                    mm = pe.matmul(ps[0:NS, bank, 0:GV], g_qz[par][:, s, :], g_sst[par][:, s, :], start=False, stop=s == SEQS - 1)
                mm.then_inc(go_done, 1)
                for s in range(SEQS):
                    if s == 4 and h + 1 < GH:
                        turn_keys_of(h + 1)
                    state_product(h, PQ + s, g_kz[par][0:NS, s, :], vv)

            def turn_y(t):
                r0, n = TILES[t]
                pe.wait_ge(y_ready, t + 1)
                for half in range(2):
                    turn([(j * P, g_r[0:n, t, (half * 4 + j) * P:(half * 4 + j + 1) * P]) for j in range(4)])

            turn_y(0)
            turn_y(1)
            pe.wait_ge(pad_zero, 6)

            def y_here(c, t):
                if c == 0:
                    if t + 2 < NTILE:
                        turn_y(t + 2)
                    pe.wait_ge(turned_out, BATCH_Y + 2 * t + 2)
                    lo_here(BATCH_Y, 2 * t + 2)

            products_before_norm(2, lambda c: [(0, 4), (4, 4)], y_here)
            ffn(1)

        @block.scalar
        def _(act):
            batch = Count(turned_out)

            def take(dst, src_view, wait_more=None):
                act.wait_ge(turned, batch.n + 1)
                act.activation(dst, src_view(ps[:, TURN[batch.n % 2], :]), ACT.Copy).then_inc(turned_out, batch.one())

            def take_x(t):
                r0, n = TILES[t]
                for half in range(2):
                    take(xTh[:, half * 4:half * 4 + 4, r0:r0 + n],
                         lambda b: b.rearrange("p (j c) -> p j c", j=4)[:, :, 0:n])

            def split_hi(n):
                act.wait_ge(raw_loaded[n % 2], 16 * LOADS * (n // 2 + 1))
                if n >= 2:
                    act.wait_ge(steps, freed(n - 2))
                a = unit_width(n)
                act.activation(w_hi[:, n % 2, 0:a], raw[:, n % 2, 0:a], ACT.Copy).then_inc(hi_done, 1)

            split_hi(0)
            for t in range(NTILE):
                take_x(t)

            for n in range(12):
                c, late = divmod(n, 2)
                if n < 11:
                    split_hi(n + 1)
                for t in range(NTILE):
                    if c >= 4 and late:
                        rows = TILES[t][1]
                        act.wait_ge(steps, steps_at("attn_in", n, t))
                        act.activation(v_tok[0:rows, t, (c - 4) * HALF:(c - 3) * HALF], ps[0:rows, t, :], ACT.Copy).then_inc(v_read, 1)
                    r = c * NTILE + t - 2
                    if late == (t >= 2) and 0 <= r < 4 * NTILE:
                        rc, rt = divmod(r, NTILE)
                        r0, rn = TILES[rt]
                        take(qkT[:, 4 * rc:4 * rc + 4, r0:r0 + rn],
                             lambda b: b.rearrange("p (j c) -> p j c", j=4)[:, :, 0:rn])

            def exps(n):
                qi = n // 4
                width = (qi + 1) * P
                sbuf = s_buf[:, n % 2]
                act.wait_ge(nm_ready, n + 1)
                act.activation(sbuf[:, 0:width], sbuf[:, 0:width], ACT.Exp, bias=nm[:, n, 0:1], scale=ATT_SCALE,
                               accum_out=den[:, n, 0:1]).then_inc(probs, 1)
                end = score_at(qi, 3) + width
                act.activation(sbuf[:, 512:end], sbuf[:, 512:end], ACT.Exp, bias=nm[:, n, 1:2], scale=ATT_SCALE,
                               accum_out=den[:, n, 1:2]).then_inc(probs, 1)

            def take_probs(n):
                nblk = P_BLOCKS[n // 4]
                if n >= 1:
                    act.wait_ge(pv_done, n)
                for b0 in range(0, nblk, 4):
                    k = min(4, nblk - b0)
                    take(pT[:, b0:b0 + k, :], lambda b: b.rearrange("p (j c) -> p j c", j=4)[:, 0:k, :])

            exps(0)
            for n in range(16):
                take_probs(n)
                if n + 1 < 16:
                    exps(n + 1)
                if n % 4 == 3:
                    qi = n // 4
                    take(xTh[:, 0:4, qi * P:(qi + 1) * P], lambda b: b.rearrange("p (j c) -> p j c", j=4))

            def take_keys(s):
                if s >= 2:
                    act.wait_ge(sc_done, s - 1)
                for b0 in range(0, 14, 4):
                    k = min(4, 14 - b0)
                    take(kcT[s % 2][:, b0:b0 + k, :], lambda b: b.rearrange("p (j c) -> p j c", j=4)[:, 0:k, :])

            def sample_probs(tile):
                act.wait_ge(nm_ready, 17 + tile)
                for merged, (a, b) in enumerate(((0, 320), (320, S_COLS))):
                    act.activation(s_buf[:, 0, a:b], s_buf[:, 0, a:b], ACT.Exp, bias=snm[:, tile, merged:merged + 1],
                                   scale=ATT_SCALE, accum_out=sden[:, tile, merged:merged + 1]).then_inc(probs, 1)
                act.wait_ge(pv_done, 16)
                if tile:
                    act.wait_ge(spv_done, tile)
                for b0 in range(0, len(KEY_BLOCKS), 4):
                    blocks = KEY_BLOCKS[b0:b0 + 4]
                    full = [b[1] for b in blocks]
                    act.wait_ge(turned, batch.n + 1)
                    bank = TURN[batch.n % 2]
                    for j, kn in enumerate(full):
                        ins = act.activation(pT[0:kn, b0 + j, :], ps[0:kn, bank, j * P:(j + 1) * P], ACT.Copy)
                    ins.then_inc(turned_out, batch.one())

            take_keys(0)
            for s in range(SEQS):
                if s + 1 < SEQS:
                    take_keys(s + 1)
                if s in (4, 7):
                    sample_probs(s // 7)
            act.wait_ge(spv_done, 2)
            split_hi(12)
            split_hi(13)

            def ln_roots(stage):
                for t in range(NTILE):
                    n = TILES[t][1]
                    act.wait_ge(ln_var, stage * NTILE + t + 1)
                    act.activation(ln_sd[0:n, t, 0:1], ln_mv[0:n, t, 1:2], ACT.Sqrt, bias=eps_ln[0:n, 0:1]).then_inc(ln_root, 1)
                    if stage % 2 == 0 and t == 1:
                        take_sides()
                    if t == 3 and stage < 3:
                        split_hi(NORM_UNITS[stage][-1] + 1)
                        for before in range(3):
                            take_x(before)
                if stage < 3:
                    take_x(3)
                    take_x(4)

            def take_sides():
                for v in range(2):
                    take(feat[:, v, :, :].rearrange("p j r -> p (j r)"), lambda b: b[:, 0:NJ * SIDE])

            def ffn(l):
                act.wait_ge(turned_out, batch.n)

                act.wait_ge(pads_zero, l + 1)

                base = UNIT_NO[(f"up{l}", 0)]

                def copy_up(j, u, first):
                    slot = (base + u + 1) % 2
                    act.wait_ge(raw_loaded[slot], (j - u) * 16 + 32 * ((base + u + 1) // 2 + 1))
                    act.wait_ge(steps, j * 4 + STEPS_BEFORE[base])
                    act.activation(w_hi[:, slot, :], raw[:, slot, :], ACT.Copy).then_inc(hi_done, 1)
                    if not first:
                        act.wait_ge(conv_step, j * 13 + (l * NJ * 13 - 13))
                        act.wait_ge(tail_ready, j + (l * NJ - 1))
                    act.activation(fj[:, u, :, :], feat[:, :, bass.ds(j, 1), :].rearrange("p v o r -> p v (o r)"), ACT.Copy)
                    for v in range(2):
                        act.activation(ext_s[:, u, v, :, 0:2], feat[:, v, bass.ds(j, 1), 0:2 * SEQS].rearrange("p o (s r) -> p s (o r)", r=2), ACT.Copy)
                    for m, (v, run) in enumerate(UP_RUNS):
                        act.wait_ge(steps, j * 4 + (STEPS_BEFORE[base] + 1 + m))
                        if run == 0:
                            act.activation(ext[:, u, v, 2:2 + SPLIT], ps[:, m, 0:SPLIT], ACT.Copy).then_inc(ext_ready, 1)
                        else:
                            act.activation(ext[:, u, v, 2 + SPLIT:2 + NP], ps[:, m, 0:PRE], ACT.Copy)
                            act.activation(ext_s[:, u, v, :, 2:10], ps[:, m, PRE:SPLIT].rearrange("p (s t) -> p s t", s=SEQS),
                                           ACT.Copy).then_inc(ext_ready, 1)

                def silu(j, u):
                    act.wait_ge(conv_step, j * 13 + (l * NJ * 13 + 6))
                    act.activation(conv_y[:, u, 1, :], conv_y[:, u, 1, :], ACT.Silu).then_inc(silu_done, 1)

                def take_tail(j, u):
                    act.wait_ge(tail_turned, j + (l * NJ + 1))
                    dst = side[0:TAIL, :].rearrange("r (v c) -> r v c", v=2)[:, :, bass.ds(j * P, P)]
                    act.activation(dst, ps[0:TAIL, TURN[u], 0:2 * P].rearrange("r (v c) -> r v c", v=2), ACT.Copy).then_inc(tail_out, 1)

                copy_up(0, 0, True)
                silu(0, 0)
                copy_up(1, 1, True)
                silu(1, 1)
                take_tail(0, 0)
                with act.Fori(1, NJ // 2 - 1) as i:
                    copy_up(i * 2, 0, False)
                    silu(i * 2, 0)
                    take_tail(i * 2 - 1, 1)
                    copy_up(i * 2 + 1, 1, False)
                    silu(i * 2 + 1, 1)
                    take_tail(i * 2, 0)
                copy_up(NJ - 2, 0, False)
                silu(NJ - 2, 0)
                take_tail(NJ - 3, 1)
                copy_up(NJ - 1, 1, False)

                first_unit = UNIT_NO[(f"down{l}", 0)]
                groups = len(DOWN_GROUPS)

                def h_split(c):
                    k0, kn = DOWN_GROUPS[c % groups]
                    act.wait_ge(conv_step, (l * NJ + k0 + kn) * 13)
                    if c == 0:
                        act.wait_ge(steps, STEPS_BEFORE[first_unit])
                        for r0, n in TILES:
                            act.activation(xTh[:, 0:kn, r0:r0 + n], hT[:, 0:kn, r0:r0 + n], ACT.Copy).then_inc(h_hi, 1)
                        return
                    act.wait_ge(steps, STEPS_BEFORE[max(first_unit, first_unit + c - 1)])
                    act.activation(xTh[:, 4 * (c % 2):4 * (c % 2) + kn, 0:NT], hT[:, k0:k0 + kn, :], ACT.Copy).then_inc(h_hi, 1)

                h_split(0)
                silu(NJ - 1, 1)
                take_tail(NJ - 2, 0)
                for c in range(2 * groups - 1):
                    split_hi(first_unit + c + 1)
                    h_split(c + 1)
                    if c == 0:
                        take_tail(NJ - 1, 1)

            ln_roots(0)
            ffn(0)
            ln_roots(1)

            def copy_fm(i, dst, scale=1.0, func=ACT.Copy, bias=None):
                for bank, a, b in ((i % 2, 0, SPLIT), (2 + i % 2, SPLIT, NT)):
                    if bias is None:
                        ins = act.activation(dst[:, a:b], ps[:, bank, 0:b - a], func, scale=scale)
                    else:
                        ins = act.activation(dst[:, a:b], ps[:, bank, 0:b - a], ACT.Identity, bias=bias)
                ins.then_inc(fm_read, 1)

            for i in range(2 * GH):
                n = UNIT_NO[("gla_qk", i // 2)]
                if i % 2 == 0:
                    split_hi(n + 1)
                act.wait_ge(steps, STEPS_BEFORE[n] + 3 + i % 2)
                copy_fm(i, (g_q if i < GH else g_k)[:, i % GH], GK ** -0.5 if i < GH else 1.0)
            n = UNIT_NO[("gla_a1", 0)]
            split_hi(n + 1)
            act.wait_ge(steps, STEPS_BEFORE[n + 1])
            for run in range(2):
                ins = act.activation(g_t1[0:16, run * SPLIT:(run + 1) * SPLIT], ps[0:16, (4, 7)[run], 0:SPLIT], ACT.Copy)
            ins.then_inc(fm_read, 1)
            for h in range(GH):
                act.wait_ge(low_filled, 1 + h)
                copy_fm(h, g_b[:, h], bias=g_ba[:, h:h + 1])
            zz = g_b.rearrange("p h n -> p (h n)")
            act.wait_ge(fm_read, 3 * GH + 1)
            act.activation(g_tmp, zz, ACT.Abs).then_inc(gates, 1)
            act.wait_ge(gates, 1)
            act.activation(g_tmp, g_tmp, ACT.Exp, scale=-1.0).then_inc(gates, 1)
            act.wait_ge(gates, 2)
            act.activation(g_tmp, g_tmp, ACT.Ln, bias=1.0).then_inc(gates, 1)
            def decay(m):
                g = decayed_of(m) if m < LEVEL_STEPS else None
                if g is not None:
                    act.wait_ge(lev_diff, g + 1)
                    e = lev_e[:, g % 2, 0:NT if g % NLEV < 3 else NP]
                    act.activation(e, e, ACT.Exp, scale=1.0 / TAU).then_inc(lev_exp, 1)

            for i in range(8):
                c, late = divmod(i, 2)
                for t in range(NTILE):
                    if t == 0:
                        split_hi(UNIT_NO[("gla_vr", i)] + 1)
                    m = i * NTILE + t - LEV_FIRST
                    if m + 1 >= 0:
                        decay(m + 1)
                    if not late:
                        continue
                    n = TILES[t][1]
                    act.wait_ge(steps, steps_at("gla_vr", i, t))
                    dst = (g_v if c < 2 else g_r)[0:n, t, (c % 2) * HALF:(c % 2 + 1) * HALF]
                    act.activation(dst, ps[0:n, t, :], ACT.Copy if c < 2 else ACT.Silu).then_inc(tok_read, 1)
            split_hi(UNIT_NO[("gla_out", 1)])
            sq = Count(sq_done)

            def decays_of(h):
                if h == 0:
                    act.wait_ge(lev_ready, GH * NLEV)
                elif h >= 2:
                    act.wait_ge(gs_read, (h - 1) * HEAD_STEPS)
                act.activation(from_start[h % 2], g_b[:, h], ACT.Exp, scale=1.0 / TAU).then_inc(decays, 1)
                act.wait_ge(end_diff, h + 1)
                act.activation(to_end, to_end, ACT.Exp, scale=1.0 / TAU).then_inc(decays, 1)

            def take_keys_of(h):
                if h >= 2:
                    act.wait_ge(gs_done, (h - 1) * HEAD_STEPS)
                take(g_kt[h % 2][:, 0:PQ, :], lambda b: b.rearrange("p (j c) -> p j c", j=4))
                take(g_kt[h % 2][0:NS, PQ, :], lambda b: b[0:NS, 0:P])

            decays_of(0)
            take_keys_of(0)
            for h in range(GH):
                for t in range(NTILE):
                    if t == 3 and h + 1 < GH:
                        decays_of(h + 1)
                    n = TILES[t][1]
                    act.wait_ge(go_done, sq.n + 1)
                    if sq.n >= 1:
                        act.wait_ge(sq_done, sq.n)
                    act.activation(squares[0:n, :], ps[0:n, (4, 7)[sq.n % 2], 0:GV], ACT.Square,
                                   accum_out=g_ss[0:n, t, h:h + 1]).then_inc(sq_done, sq.one())
                if h + 1 < GH:
                    take_keys_of(h + 1)
            act.wait_ge(sq_done, GH * NTILE)
            act.activation(g_rs.rearrange("p t h -> p (t h)"), g_ss.rearrange("p t h -> p (t h)"), ACT.Sqrt,
                           bias=eps_ln[:, 1:2], scale=1.0 / GV).then_inc(gates, 1)
            act.wait_ge(p_state_out, 16 * GH)
            act.wait_ge(s_state_out[0], 32)
            act.wait_ge(s_state_out[1], 32)
            for t in range(NTILE):
                take_x(t)
            for c in range(1, 3):
                split_hi(UNIT_NO[("gla_out", c)] + 1)
            ln_roots(2)
            ffn(1)
            ln_roots(3)

        @block.vector
        def _(dve):
            vs = Count(vec)

            def settle():
                dve.wait_ge(vec, vs.n)

            dve.memset(eps_ln[:, 0:1], LN_EPS)
            dve.memset(eps_ln[:, 1:2], RMS_EPS).then_inc(vec, vs.one())
            def split_lo(n):
                dve.wait_ge(hi_done, n + 1)
                a = unit_width(n)
                dve.tensor_tensor(w_lo[:, n % 2, 0:a], raw[:, n % 2, 0:a], w_hi[:, n % 2, 0:a].bitcast(F32),
                                  ALU.subtract).then_inc(lo_done, 1)

            def batch_lo(b, k0, r0, n):
                dve.wait_ge(turned_out, b + 1)
                dve.tensor_tensor(xTl[:, k0:k0 + 4, r0:r0 + n],
                                  ps[:, TURN[b % 2], :].rearrange("p (j c) -> p j c", j=4)[:, :, 0:n],
                                  xTh[:, k0:k0 + 4, r0:r0 + n].bitcast(F32), ALU.subtract).then_inc(x_lo, 1)

            def x_los(first_batch, t):
                for half in range(2):
                    batch_lo(first_batch + 2 * t + half, 4 * half, *TILES[t])

            split_lo(0)
            for t in range(NTILE):
                x_los(0, t)
            dve.wait_ge(consts_loaded, 48)
            for r in range(4 * NTILE):
                c, t = divmod(r, NTILE)
                n = TILES[t][1]
                if t == 0:
                    split_lo(2 * c + 1)
                    split_lo(2 * c + 2)
                dve.wait_ge(steps, steps_at("attn_in", 2 * c + 1, t))
                if r >= 1:
                    dve.wait_ge(roped, r)
                src = ps[0:n, t, :].rearrange("p (h a d) -> p h a d", h=8, a=2)
                a4 = rope_a[0:n, :].rearrange("p (h d) -> p h d", h=8)
                b4 = rope_b[0:n, :].rearrange("p (h a d) -> p h a d", h=8, a=2)
                dve.tensor_tensor(a4, ps[0:n, t, :].rearrange("p (h d) -> p h d", h=8),
                                  cos_t[0:n, t:t + 1, :].to_broadcast([n, 8, HD]), ALU.mult)
                for a in range(2):
                    ins = dve.tensor_tensor(b4[:, :, a, :], src[:, :, 1 - a, :],
                                            sin_t[0:n, t:t + 1, 32 * a:32 * a + 32].to_broadcast([n, 8, 32]), ALU.mult)
                ins.then_inc(qk_read, 1)
                dve.wait_ge(qk_read, r + 1)
                if r >= 3:
                    dve.wait_ge(turned, TURNS_X + r - 2)
                if r - 3 >= 2 * NTILE:
                    dve.wait_ge(k_stored[r % ROPED], K_STORES[r - 3])
                dve.tensor_tensor(roped_buf[0:n, r % 3, :], rope_a[0:n, :], rope_b[0:n, :], ALU.add).then_inc(roped, 1)

            for n in range(9, 12):
                split_lo(n)
            dve.wait_ge(masks_loaded, 16)

            def soft_scores(n):
                qi, h = divmod(n, 4)
                if n >= 2:
                    dve.wait_ge(pv_done, n - 1)
                else:
                    dve.wait_ge(turned, UP0)
                    for i in range(ROPED):
                        dve.wait_ge(k_stored[i], stores_[i])
                for g in range(4):
                    full = 256 if g == 1 else 512
                    width = min((qi + 1) * P, full)
                    dve.wait_ge(s_ready, 4 * n + g + 1)
                    acc = mb[:, n, 0:1] if g == 0 else mx[:, n, g:g + 1]
                    dve.tensor_tensor_reduce(s_buf[:, n % 2, score_at(qi, g):score_at(qi, g) + width], ps[:, g, 0:width],
                                             masks[:, MASK_AT[g] + full - width:MASK_AT[g] + full],
                                             1.0, LOWEST, ALU.add, ALU.max, acc).then_inc(s_read, 1)
                dve.wait_ge(s_read, 4 * n + 4)
                dve.tensor_reduce(mb[:, n, 1:2], mx[:, n, 1:4], AXX, ALU.max).then_inc(vec, vs.one())
                settle()
                dve.tensor_scalar(nm[:, n, :], mb[:, n, :], -ATT_SCALE, None, ALU.mult).then_inc(nm_ready, 1)

            def outputs(n):
                qi, h = divmod(n, 4)
                dve.wait_ge(probs, 2 * n + 2)
                dve.reciprocal(rden[:, n, :], den[:, n, :]).then_inc(vec, vs.one())
                settle()
                dve.wait_ge(pv_done, n + 1)
                if h == 0 and qi >= 1:
                    dve.wait_ge(turned, UP0 + 4 * sum(P_BATCH[:qi]) + qi)
                for merged in range(2):
                    at = merged * 256 + h * HD
                    own = merged * P + h % 2 * HD
                    dve.tensor_scalar(o_tok[:, at:at + HD], ps[:, (4, 7)[n % 2], own:own + HD],
                                      rden[:, n, merged:merged + 1], None, ALU.mult).then_inc(o_ready, 1)

            soft_scores(0)
            for n in range(16):
                if n % 4 == 0 and n:
                    batch_lo(BATCH_O[n // 4 - 1], 0, (n // 4 - 1) * P, P)
                if n + 1 < 16:
                    soft_scores(n + 1)
                outputs(n)
            batch_lo(BATCH_O[PQ - 1], 0, (PQ - 1) * P, P)

            for tile in range(2):
                dve.wait_ge(sc_done, 4 * tile + 4)
                dve.wait_ge(smask_loaded, 16 * (tile + 1))
                if tile == 0:
                    dve.wait_ge(pv_done, 16)
                else:
                    dve.wait_ge(turned, BATCH_BEFORE_SAMPLE + 6 * K_BATCH + SP_BATCH)
                for g in range(4):
                    a, width = GROUP_AT[g], GROUP_PAST[g] + NS
                    acc = smb[:, tile, 0:1] if g == 0 else smx[:, tile, g:g + 1]
                    dve.tensor_tensor_reduce(s_buf[:, 0, a:a + width], ps[:, g, 0:width], s_mask[:, a:a + width],
                                             1.0, LOWEST, ALU.add, ALU.max, acc).then_inc(s_read, 1)
                dve.wait_ge(s_read, 64 + 4 * (tile + 1))
                dve.tensor_reduce(smb[:, tile, 1:2], smx[:, tile, 1:4], AXX, ALU.max).then_inc(vec, vs.one())
                settle()
                dve.tensor_scalar(snm[:, tile, :], smb[:, tile, :], -ATT_SCALE, None, ALU.mult).then_inc(nm_ready, 1)
                dve.wait_ge(probs, 32 + 2 * (tile + 1))
                dve.reciprocal(srd[:, tile, :], sden[:, tile, :]).then_inc(vec, vs.one())
                settle()
                dve.wait_ge(spv_done, tile + 1)
                if tile == 0:
                    dve.wait_ge(turned, BATCH_O[PQ - 1] + 1)
                for merged in range(2):
                    cols = slice(256 * merged, 256 * merged + 256)
                    dve.tensor_scalar(o_tok[:, cols], ps[:, 4, cols], srd[:, tile, merged:merged + 1], None,
                                      ALU.mult).then_inc(so_scaled, 1)
                dve.wait_ge(so_turned, tile + 1)
                for part in range(2):
                    for merged in range(2):
                        for pair in range(2):
                            for b in range(2):
                                src = (ps[HD * b:HD * b + HD, 7, (2 * merged + pair) * P:(2 * merged + pair + 1) * P]
                                       .rearrange("p (s h q) -> p s h q", s=4, h=4)[:, :, 2 * pair + b, :])
                                t0 = NP + 32 * tile
                                hi, lo = [x[HD * b:HD * b + HD, 2 * merged + pair, t0:t0 + 32].rearrange("p (s q) -> p s q", s=4)
                                          for x in (xTh, xTl)]
                                ins = (dve.tensor_tensor(lo, src, hi.bitcast(F32), ALU.subtract) if part
                                       else dve.tensor_copy(hi, src))
                    if part == 0:
                        ins.then_inc(vec, vs.one())
                        settle()
                ins.then_inc(soT_ready, 1)
            split_lo(12)

            def residual(stage, half, t, step, count):
                n = TILES[t][1]
                dve.wait_ge(steps, step)
                z = x_tok[0:n, t, half * HALF:(half + 1) * HALF]
                dve.scalar_tensor_tensor(z, z, ALPHA, ps[0:n, t, :], ALU.mult, ALU.add).then_inc(z_read, 1)
                dve.wait_ge(z_read, count)
                dve.bn_stats(ln_stats[0:n, t, half, :], z).then_inc(vec, vs.one())

            def normalise(stage, t):
                n = TILES[t][1]
                settle()
                dve.bn_aggr(ln_mv[0:n, t, :], ln_stats[0:n, t, :, :]).then_inc(ln_var, 1)
                dve.wait_ge(ln_var, stage * NTILE + t + 1)
                x = x_tok[0:n, t, :]
                dve.scalar_tensor_tensor(x, x, ln_mv[0:n, t, 0:1], gb_of[stage][0:n, 0, :], ALU.subtract, ALU.mult).then_inc(vec, vs.one())
                dve.wait_ge(ln_root, stage * NTILE + t + 1)
                dve.reciprocal(ln_sd[0:n, t, 1:2], ln_sd[0:n, t, 0:1]).then_inc(vec, vs.one())
                settle()
                dve.scalar_tensor_tensor(x, x, ln_sd[0:n, t, 1:2], gb_of[stage][0:n, 1, :], ALU.mult, ALU.add).then_inc(ln_done, 1)

            def residual_ln(stage, duty, first_batch):
                dve.wait_ge(gb_loaded, 32 * (stage + 1))
                units = NORM_UNITS[stage]
                per_half = len(units) // 2
                sums = 0
                for i, (c, t) in enumerate(norm_steps(stage)):
                    if t == 0 and c < len(units) - 1:
                        duty(c)
                    half, late = divmod(c, per_half)
                    if late < per_half - 1:
                        continue
                    sums += 1
                    residual(stage, half, t, STEPS_BEFORE[units[0]] + i + 1, 2 * stage * NTILE + sums)
                    if half == 1:
                        normalise(stage, t)
                        if t == 3 and first_batch is not None:
                            split_lo(units[-1] + 1)
                            for before in range(3):
                                x_los(first_batch, before)
                if first_batch is not None:
                    x_los(first_batch, 3)
                    x_los(first_batch, 4)

            def units_of(kind, n):
                return [UNIT_NO[(kind, c)] for c in range(n)]

            def h_split(l, c):
                k0, kn = DOWN_GROUPS[c % len(DOWN_GROUPS)]
                at = 4 * (c % 2)
                for t, (r0, n) in enumerate(TILES if c == 0 else [(0, NT)]):
                    dve.wait_ge(h_hi, h_count(l, c, t))
                    dve.tensor_tensor(xTl[:, at:at + kn, r0:r0 + n], hT[:, k0:k0 + kn, r0:r0 + n],
                                      xTh[:, at:at + kn, r0:r0 + n].bitcast(F32), ALU.subtract).then_inc(h_lo, 1)

            def down_norm(l, first_batch):
                groups = len(DOWN_GROUPS)
                units = units_of(f"down{l}", 2 * groups)

                def duty(c):
                    split_lo(units[c] + 1)
                    h_split(l, c + 1)

                residual_ln(2 * l + 1, duty, first_batch)

            def conv(j, u, l, first, amid=None):
                n, slot = UNIT_NO[(f"up{l}", 0)] + 1, (UNIT_NO[(f"up{l}", 0)] + u + 1) % 2
                dve.wait_ge(hi_done, j + (n + 1))
                dve.tensor_tensor(w_lo[:, slot, :], raw[:, slot, :], w_hi[:, slot, :].bitcast(F32),
                                  ALU.subtract).then_inc(lo_done, 1)
                base = j * 13 + l * NJ * 13
                for v in (1, 0):
                    if v == 0 and amid is not None:
                        amid()
                    at = 0 if v else 6
                    dve.wait_ge(ext_ready, j * 4 + (l * NJ * 4 + (3 if v else 4)))
                    for tap in range(3):
                        if tap:
                            dve.wait_ge(conv_step, base + (at + 2 * tap))
                        w = fj[:, u, v, 2 * SEQS + tap:2 * SEQS + tap + 1]
                        yp, ys = conv_y[:, u, v, 0:NP], conv_y[:, u, v, NP:NT].rearrange("p (s t) -> p s t", s=SEQS)
                        ep, es = ext[:, u, v, tap:tap + NP], ext_s[:, u, v, :, tap:tap + T_NEW]
                        for y, e in ((yp, ep), (ys, es)):
                            if tap == 0:
                                ins = dve.tensor_scalar(y, e, w, fj[:, u, v, SIDE - 1:SIDE], ALU.mult, ALU.add)
                            else:
                                ins = dve.scalar_tensor_tensor(y, e, w, y, ALU.mult, ALU.add)
                            ins.then_inc(conv_step, 1)
                if not first:
                    dve.wait_ge(tail_turned, j + (l * NJ - 1))
                for v in range(2):
                    dve.tensor_copy(tl[:, u, v, 0:2], ext[:, u, v, 512:514])
                    ins = dve.tensor_copy(tl[:, u, v, 2:TAIL].rearrange("p (s r) -> p s r", r=2), ext_s[:, u, v, :, 8:10])
                ins.then_inc(tail_ready, 1)
                dve.wait_ge(conv_step, base + 12)
                dve.wait_ge(silu_done, j + (l * NJ + 1))
                dve.tensor_tensor(hT[:, bass.ds(j, 1), :].rearrange("p o n -> p (o n)"), conv_y[:, u, 0, :],
                                  conv_y[:, u, 1, :], ALU.mult).then_inc(conv_step, 1)

            def ffn(l):
                conv(0, 0, l, True)
                conv(1, 1, l, True)
                with dve.Fori(1, NJ // 2 - 1) as i:
                    conv(i * 2, 0, l, False)
                    conv(i * 2 + 1, 1, l, False)
                conv(NJ - 2, 0, l, False)
                conv(NJ - 1, 1, l, False, lambda: h_split(l, 0))

            dve.wait_ge(x_again, 32)
            residual_ln(0, lambda c: split_lo(13), BATCH_LN0)
            dve.wait_ge(v_stored, V_STORES)
            ffn(0)
            down_norm(0, BATCH_LN1)

            for n in units_of("gla_qk", 4) + [UNIT_NO[("gla_a1", 0)]]:
                split_lo(n + 1)
            dve.wait_ge(gates, 3)
            zz = g_b.rearrange("p h n -> p (h n)")
            dve.scalar_tensor_tensor(zz, zz, 0.0, g_tmp, ALU.min, ALU.subtract).then_inc(vec, vs.one())
            split_lo(UNIT_NO[("gla_vr", 1)])
            settle()
            dve.wait_ge(gla_loaded, 96)
            for h in range(GH):
                dve.tensor_tensor_scan(g_b[:, h], g_reset, g_b[:, h], 0.0, ALU.mult, ALU.add).then_inc(vec, vs.one())
            settle()
            dve.tensor_copy(g_mask, mask_words).then_inc(vec, vs.one())
            settle()
            for z in [lev_q, lev_k, g_ss] + att:
                dve.memset(z, 0.0).then_inc(vec, vs.one())
            settle()

            def blocks(x, ncol, half):
                return x[:, 0:ncol].rearrange("p (n a c) -> p n a c", a=2, c=half)

            def differences(m):
                g = decayed_of(m) if m < LEVEL_STEPS else None
                if g is None:
                    return
                h, l = divmod(g, NLEV)
                half = 1 << l
                ncol = NT if l < 3 else NP
                if g >= 2:
                    dve.wait_ge(lev_ready, g - 1)
                b, d = blocks(g_b[:, h], ncol, half), blocks(lev_e[:, g % 2], ncol, half)
                ref = b[:, :, 0, half - 1:half].to_broadcast([P, ncol // (2 * half), half])
                dve.tensor_tensor(d[:, :, 1, :], b[:, :, 1, :], ref, ALU.subtract)
                dve.tensor_tensor(d[:, :, 0, :], ref, b[:, :, 0, :], ALU.subtract).then_inc(lev_diff, 1)

            def decayed(m):
                g = decayed_of(m)
                if g is None:
                    return
                h, l = divmod(g, NLEV)
                half = 1 << l
                ncol = NT if l < 3 else NP
                dve.wait_ge(lev_exp, g + 1)
                if g >= 2:
                    before = [n for n in range(m) if decayed_of(n) == g - 2][0]
                    dve.wait_ge(lev_prod, levels_done(before))
                e = blocks(lev_e[:, g % 2], ncol, half)
                q, k = blocks(g_q[:, h], ncol, half), blocks(g_k[:, h], ncol, half)
                dve.tensor_tensor(blocks(lev_q[:, g % 2], ncol, half)[:, :, 1, :], q[:, :, 1, :], e[:, :, 1, :], ALU.mult)
                dve.tensor_tensor(blocks(lev_k[:, g % 2], ncol, half)[:, :, 0, :], k[:, :, 0, :], e[:, :, 0, :],
                                  ALU.mult).then_inc(lev_ready, 1)

            def placed(m):
                h, l = divmod(m, NLEV + 1)
                n = levels_done(m) - 1 - LEV_WITH_SAMPLE[l]
                dve.wait_ge(lev_prod, n + 1)
                if n:
                    dve.wait_ge(lev_read, n)
                a = att[h]
                mask = g_mask[:, l:l + 1, :].to_broadcast([P, PQ, P])
                dve.copy_predicated(a[:, 0:NP].rearrange("p (c n) -> p c n", c=PQ), mask,
                                    ps[:, TURN[m % 2], :].rearrange("p (c n) -> p c n", c=PQ)).then_inc(lev_read, 1)
                if LEV_WITH_SAMPLE[l]:
                    dve.wait_ge(lev_prod, n + 2)
                    dve.copy_predicated(a[0:NS, NP:NT], g_mask[0:NS, l, 0:NS], ps[0:NS, 7, 0:NS]).then_inc(lev_read, 1)

            differences(0)
            differences(1)
            for i in range(1, 8):
                for t in range(NTILE):
                    if t == 0:
                        split_lo(UNIT_NO[("gla_vr", i)] + 1)
                    m = i * NTILE + t - LEV_FIRST
                    if not 0 <= m < LEVEL_STEPS:
                        continue
                    decayed(m)
                    if m >= 1:
                        placed(m - 1)
                    g = decayed_of(m)
                    if g is not None:
                        dve.wait_ge(lev_ready, g + 1)
                    differences(m + 2)
            placed(LEVEL_STEPS - 1)
            split_lo(UNIT_NO[("gla_out", 1)])

            def prepare(h):
                par = h % 2
                if h:
                    dve.wait_ge(kz_ready, 3 * h - 2)
                for a, b, n, c in ((0, NP, PQ, P), (NP, NT, SEQS, T_NEW)):
                    bb = g_b[:, h, a:b].rearrange("p (n c) -> p n c", n=n)
                    ins = dve.tensor_tensor(to_end[:, a:b].rearrange("p (n c) -> p n c", n=n),
                                            bb[:, :, c - 1:c].to_broadcast([P, n, c]), bb, ALU.subtract)
                ins.then_inc(end_diff, 1)
                dve.wait_ge(decays, 2 * h + 1)
                if h >= 2:
                    dve.wait_ge(go_done, (h - 1) * NTILE)
                    dve.wait_ge(turned, BATCH_GLA + 2 * (h - 1))
                dve.tensor_tensor(g_qb[par], g_q[:, h], from_start[par], ALU.mult).then_inc(vec, vs.one())
                dve.wait_ge(decays, 2 * h + 2)
                dve.tensor_tensor(g_kb[par], g_k[:, h], to_end, ALU.mult).then_inc(kz_ready, 1)
                settle()
                dve.tensor_copy(g_qz_own[par], g_qb[par][:, NP:NT].rearrange("p (s t) -> p s t", s=SEQS)).then_inc(kz_ready, 1)

            def prepare_samples(h):
                par = h % 2
                if h >= 2:
                    dve.wait_ge(gs_done, (h - 1) * HEAD_STEPS)
                dve.wait_ge(turned_out, BATCH_GLA + 2 * h + 2)
                dve.tensor_tensor(g_kz[par][0:NS, :, :], g_kt[par][0:NS, PQ:PQ + 1, :].to_broadcast([NS, SEQS, P]),
                                  seq_of_row.rearrange("p (s o) -> p s o", o=1).to_broadcast([NS, SEQS, P]), ALU.mult).then_inc(kz_ready, 1)

            def gate_out(h, t):
                n = h * NTILE + t
                rows = TILES[t][1]
                dve.wait_ge(sq_done, n + 1)
                r = g_r[0:rows, t, h * GV:(h + 1) * GV]
                dve.tensor_tensor(r, ps[0:rows, (4, 7)[n % 2], 0:GV], r, ALU.mult).then_inc(go_read, 1)

            def bring_state(h, c):
                n = h * HEAD_STEPS + c
                dve.wait_ge(gs_done, n + 1)
                bank = ps[:, n % 4, 0:GV]
                if c == 0:
                    dve.tensor_copy(g_state[0], bank).then_inc(gs_read, 1)
                    return
                if c >= 2:
                    dve.wait_ge(go_done, h * NTILE + c)
                if c == 1 and h:
                    dve.wait_ge(p_state_out, 16 * h)
                dve.wait_ge(gs_read, n)
                dve.scalar_tensor_tensor(g_state[c % 2], g_state[(c - 1) % 2], from_start[h % 2][:, c * P + P - 1:c * P + P], bank,
                                         ALU.mult, ALU.add).then_inc(gs_read, 1)

            dve.wait_ge(steps, STEPS_BEFORE[UNIT_NO[("gla_out", 0)]])
            for z in g_qz:
                dve.memset(z, 0.0).then_inc(vec, vs.one())
            settle()
            prepare(0)
            prepare_samples(0)
            dve.wait_ge(r_scaled, NTILE)
            for h in range(GH):
                for c in range(PQ):
                    bring_state(h, c)
                    if c >= 1:
                        gate_out(h, c - 1)
                if h + 1 < GH:
                    prepare(h + 1)
                gate_out(h, 3)
                gate_out(h, 4)
                for s in range(SEQS):
                    n = h * HEAD_STEPS + PQ + s
                    if s == 0:
                        dve.wait_ge(go_done, (h + 1) * NTILE)
                    dve.wait_ge(gs_done, n + 1)
                    col = NP + s * T_NEW + T_NEW - 1
                    state = g_sst[h % 2][:, s, :]
                    dve.scalar_tensor_tensor(state, state, from_start[h % 2][:, col:col + 1], ps[:, n % 4, 0:GV],
                                             ALU.mult, ALU.add).then_inc(gs_read, 1)
                if h + 1 < GH:
                    prepare_samples(h + 1)
            dve.wait_ge(gates, 4)
            dve.reciprocal(g_rs, g_rs).then_inc(vec, vs.one())
            settle()
            dve.wait_ge(go_read, GH * NTILE)
            for t in range(NTILE):
                n = TILES[t][1]
                r = g_r[0:n, t, :].rearrange("p (h c) -> p h c", h=GH)
                dve.tensor_tensor(r, r, g_rs[0:n, t, :].rearrange("p (h o) -> p h o", o=1).to_broadcast([n, GH, GV]),
                                  ALU.mult).then_inc(y_ready, 1)
            dve.wait_ge(p_state_out, 16 * GH)
            dve.wait_ge(s_state_out[0], 32)
            dve.wait_ge(s_state_out[1], 32)
            for t in range(NTILE):
                x_los(BATCH_Y, t)
            residual_ln(2, lambda c: split_lo(UNIT_NO[("gla_out", c)] + 1) if c else None, BATCH_LN2)
            ffn(1)
            down_norm(1, None)

        @block.gpsimd
        def _(pool):
            pool.dma_start(ident[:, :], io["ident"]).then_inc(consts_loaded, 16)

            def zero_pads():
                for x in (xTh, xTl):
                    pool.memset(x[:, :, NT:SLOT].bitcast(F32), 0.0).then_inc(pad_zero, 1)
            zero_pads()
            pool.wait_ge(consts_loaded, 16)
            pool.dma_start(cos_t, io["rope_cos"]).then_inc(consts_loaded, 16)
            pool.dma_start(sin_t, io["rope_sin"]).then_inc(consts_loaded, 16)
            pool.memset(qz_reg, 0.0).then_inc(qz_zero, 1)

            new_rows = {0: ("moba", None), 1: ("swa0", 120), 2: ("swa1", 248), 3: ("swa2", 248)}

            def store_piece(src, t, g, a, done):
                if not pieces_of(t, g):
                    return
                name, at = new_rows[g]
                if t < PQ:
                    r0 = 0 if g == 1 else t * P
                    dst = io[f"{name}_p"][0, 0, r0:r0 + P, a].rearrange("r h d -> r (h d)")
                elif g == 0:
                    dst = io["moba_s"][0, :, :, a].rearrange("s r h d -> s r (h d)")
                else:
                    dst = io[f"{name}_s"][0, :, at:at + T_NEW, a].rearrange("s r h d -> s r (h d)")
                pool.dma_start(dst, src).then_inc(done, 16)

            pool.wait_ge(roped, 1)
            pool.dma_start(masks, io["prompt_masks"]).then_inc(masks_loaded, 16)
            for r in range(2 * NTILE, 4 * NTILE):
                c, t = divmod(r, NTILE)
                n = TILES[t][1]
                pool.wait_ge(roped, r + 1)
                for half in range(2):
                    store_piece(roped_buf[0:n, r % 3, half * 256:half * 256 + 256], t, 2 * (c - 2) + half, 0, k_stored[r % ROPED])
            pool.wait_ge(qz_zero, 1)
            pool.wait_ge(turned_out, UP0)
            for c in range(8):
                for b in range(2):
                    src = qkT[HD * b:HD * b + HD, c, NP:NT].rearrange("p (s q) -> p s q", s=SEQS)
                    ins = pool.tensor_copy(qz[HD * b:HD * b + HD, c, :, 2 * (c % 2) + b, :], src)
            ins.then_inc(qz_ready, 1)
            pool.wait_ge(v_read, 2 * NTILE)
            for t in range(NTILE):
                n = TILES[t][1]
                for g in range(4):
                    store_piece(v_tok[0:n, t, g * 256:(g + 1) * 256], t, g, 1, v_stored)

            def ffn(l):
                pool.memset(ext[:, :, :, 0:2], 0.0).then_inc(pads_zero, 1)

                pool.wait_ge(tail_out, (l + 1) * NJ)
                pool.dma_start(io["ffn_p"][l, 0], side[0:2, :]).then_inc(tail_stored, 16)
                pool.dma_start(io["ffn_s"][l].rearrange("s r c -> (s r) c"), side[2:TAIL, :]).then_inc(tail_stored, 16)

            pool.wait_ge(soT_ready, 2)
            pool.wait_ge(steps, STEPS_BEFORE[14])
            zero_pads()
            ffn(0)
            pool.wait_ge(gla_loaded, 96)
            for t in range(NTILE):
                n = TILES[t][1]
                pool.wait_ge(tok_read, 3 * NTILE + t + 1)
                r = g_r[0:n, t, :].rearrange("p (h c) -> p h c", h=GH)
                pool.tensor_tensor(r, r, g_norm[0:n, :].rearrange("p (o c) -> p o c", o=1).to_broadcast([n, GH, GV]),
                                   ALU.mult).then_inc(r_scaled, 1)
            for h in range(GH):
                pool.wait_ge(gs_read, h * HEAD_STEPS + PQ)
                pool.dma_start(io["gla_p"][0, 0, h], g_state[1]).then_inc(p_state_out, 16)
                pool.wait_ge(gs_read, (h + 1) * HEAD_STEPS)
                pool.dma_start(io["gla_s"][0, :, h].rearrange("s d v -> d s v"), g_sst[h % 2]).then_inc(s_state_out[h % 2], 16)
            pool.wait_ge(go_read, GH * NTILE)
            pool.wait_ge(p_state_out, 16 * GH)
            for i in range(2):
                pool.wait_ge(s_state_out[i], 32)
            zero_pads()
            ffn(1)
            for t in range(NTILE):
                n = TILES[t][1]
                pool.wait_ge(ln_done, 3 * NTILE + t + 1)
                dst = (io["y_prompt"][0, t * P:(t + 1) * P, :] if t < PQ
                       else io["y_sample"].rearrange("s t c -> (s t) c"))
                pool.dma_start(dst, x_tok[0:n, t, :]).then_inc(y_stored, 16)
            pool.wait_ge(y_stored, 16 * NTILE)
            pool.wait_ge(tail_stored, 64)
            pool.wait_ge(p_state_out, 16 * GH)
            for i in range(2):
                pool.wait_ge(s_state_out[i], 32)
            for i in range(ROPED):
                pool.wait_ge(k_stored[i], stores_[i])
            pool.wait_ge(v_stored, V_STORES)
            pool.wait_ge(kv_stored, 48)


_INS = ["x_prompt", "x_sample", "cache_moba_kv", "state_swa0_kv", "state_swa1_kv", "state_swa2_kv", "state_gla",
        "state_ffn_conv", "page_table", "attn_w_in", "attn_w_out", "gla_w_in", "gla_w_a1", "gla_w_a2", "gla_b_a",
        "gla_norm_g", "gla_w_out", "ln_mix_g", "ln_mix_b", "ffn_w_up", "ffn_conv_w", "ffn_conv_b", "ffn_w_down",
        "ln_ffn_g", "ln_ffn_b"]
_OUTS = [("y_prompt", (1, 512, 1024)), ("y_sample", (8, 8, 1024)),
         ("moba_p", (1, 1, 512, 2, 4, 64)), ("moba_s", (1, 8, 8, 2, 4, 64)),
         ("swa0_p", (1, 1, 128, 2, 4, 64)), ("swa0_s", (1, 8, 128, 2, 4, 64)),
         ("swa1_p", (1, 1, 512, 2, 4, 64)), ("swa1_s", (1, 8, 256, 2, 4, 64)),
         ("swa2_p", (1, 1, 512, 2, 4, 64)), ("swa2_s", (1, 8, 256, 2, 4, 64)),
         ("gla_p", (1, 1, 4, 128, 256)), ("gla_s", (1, 8, 4, 128, 256)),
         ("ffn_p", (2, 1, 2, 5632)), ("ffn_s", (2, 8, 2, 5632))]


def shape_constants():
    import numpy as np

    past_len, theta, off = 256, 10000.0, -1.0e30
    half = HD // 2
    inv = np.float32(theta) ** (-np.arange(half, dtype=np.float32) / np.float32(half))
    cos, sin = np.zeros((P, NTILE, HD), np.float32), np.zeros((P, NTILE, HD), np.float32)
    for t, (first, n) in enumerate(TILES):
        pos = (first + np.arange(n)) if t < PQ else past_len + np.arange(n) % T_NEW
        ang = pos.astype(np.float32)[:, None] * inv[None, :]
        cos[:n, t] = np.concatenate([np.cos(ang), np.cos(ang)], 1)
        sin[:n, t] = np.concatenate([-np.sin(ang), np.sin(ang)], 1)

    i, past = np.arange(P)[:, None], np.arange(-3 * P, P)[None, :]
    causal = past <= i
    window = (past <= i) & (i - past <= 128)
    groups = [causal, window[:, 2 * P:], causal & ((i - past) % 4 == 0), causal & ((i - past) % 16 == 0)]
    prompt = np.where(np.concatenate(groups, 1), 0.0, off).astype(np.float32)

    sample = np.zeros((P, 2, S_COLS), np.float32)
    row = np.arange(P)
    s4, q = row // 32, row % T_NEW
    tok = np.arange(NS)
    for g in range(4):
        n = GROUP_PAST[g]
        dil = (1, 1, 4, 16)[g]
        back = n + q[:, None] - np.arange(n)[None, :]
        seen = (back % dil == 0) & ((back <= 128 * dil) | (g == 0))
        for tile in range(2):
            same = (tok // T_NEW)[None, :] == (4 * tile + s4)[:, None]
            ago = q[:, None] - (tok % T_NEW)[None, :]
            new = same & (ago >= 0) & (ago % dil == 0)
            sample[:, tile, GROUP_AT[g]:GROUP_AT[g] + n + NS] = np.where(np.concatenate([seen, new], 1), 0.0, off)

    level = np.zeros((P, NLEV + 1, P), np.int32)
    s, t = np.arange(P)[:, None], np.arange(P)[None, :]
    for l in range(NLEV):
        h = 1 << l
        level[:, l] = (s // (2 * h) == t // (2 * h)) & (s // h % 2 == 0) & (t // h % 2 == 1)
    level[:, NLEV] = s == t
    reset = np.ones((P, NT), np.float32)
    reset[:, 0:NP:P] = 0.0
    reset[:, NP:NT:T_NEW] = 0.0
    seq_of_row = (np.arange(NS)[:, None] // T_NEW == np.arange(SEQS)[None, :]).astype(np.float32)
    return {"ident": np.eye(P, dtype=np.float32), "rope_cos": cos, "rope_sin": sin, "prompt_masks": prompt,
            "sample_masks": sample, "level_masks": level, "scan_reset": reset, "seq_of_row": seq_of_row}


def kernel(**inputs):
    import numpy as np
    import concourse.bacc as bacc
    from concourse.bass_utils import run_bass_kernel_spmd

    nc = bacc.Bacc("TRN2", target_bir_lowering=False, num_devices=1)
    arrays, io = {}, {}
    given = {name: np.ascontiguousarray(inputs[name]) for name in _INS}
    for name, a in list(given.items()) + list(shape_constants().items()):
        arrays[f"in_{name}"] = a
        io[name] = nc.dram_tensor(f"in_{name}", a.shape, mybir.dt.from_np(a.dtype), kind="ExternalInput").ap()
    for name, shape in _OUTS:
        io[name] = nc.dram_tensor(f"out_{name}", shape, F32, kind="ExternalOutput").ap()
    build_program(nc, io)
    r = run_bass_kernel_spmd(nc, [arrays], core_ids=[0])
    return tuple(r.results[0][f"out_{name}"] for name, _ in _OUTS)
```
